# Optimizing a Trainium2 kernel written in Bass

```python
import math
import jax, jax.numpy as jnp
from jax import lax
import numpy as np

D_MODEL = 1024
BATCH = 1
SEQ = 256
DEPTH = 1

MEM_LEN = 256
EPS = 1e-6
MLA_HEADS = 8
Q_LORA = 384
KV_LORA = 256
D_NOPE = 64
D_ROPE = 32
D_QK = D_NOPE + D_ROPE
D_V = 64
MLA_WIDTH = MLA_HEADS * D_V
ROPE_THETA = 10000.0
Q_BLOCK = 128
SSM_GROUPS = 32
SSM_GROUP_CH = 16
SSM_WIDTH = SSM_GROUPS * SSM_GROUP_CH
SSM_STATE = 64
DT_MIN = 1e-3
DT_MAX = 1e-1
X_HEADS = 4
X_HEAD_DIM = 128
X_WIDTH = X_HEADS * X_HEAD_DIM
N_BRANCH = 3
D_FF = 2816
CONV_WIDTH = 3
IN_WIDTH = Q_LORA + KV_LORA + D_ROPE + SSM_WIDTH + X_WIDTH + N_BRANCH * D_MODEL


def rmsnorm(x, g):
    xf = x.astype(jnp.float32)
    y = xf * lax.rsqrt(jnp.mean(xf * xf, axis=-1, keepdims=True) + EPS)
    return (y * g.astype(jnp.float32)).astype(x.dtype)

def rope_tables(positions):
    inv_freq = ROPE_THETA ** (-jnp.arange(0, D_ROPE, 2, dtype=jnp.float32) / D_ROPE)
    ang = positions.astype(jnp.float32)[..., None] * inv_freq
    return jnp.cos(ang), jnp.sin(ang)

def apply_rope(x, cos, sin):
    xf = x.astype(jnp.float32)
    x1, x2 = jnp.split(xf, 2, axis=-1)
    return jnp.concatenate([x1 * cos - x2 * sin, x1 * sin + x2 * cos], axis=-1).astype(x.dtype)

def split_combined(proj):
    sizes = (Q_LORA, KV_LORA, D_ROPE, SSM_WIDTH, X_WIDTH)
    idx = [int(v) for v in np.cumsum(sizes)]
    return jnp.split(proj, idx, axis=-1)

def causal_block_attention(q, k, v):
    b, l, h, dq = q.shape
    nb = l // Q_BLOCK
    scale = dq ** -0.5
    qb = jnp.moveaxis(q.reshape(b, nb, Q_BLOCK, h, dq), 1, 0)
    kpos = jnp.arange(l)

    def one_block(args):
        i, qi = args
        s = jnp.einsum('bqhd,bkhd->bhqk', qi, k, preferred_element_type=jnp.float32) * scale
        qpos = i * Q_BLOCK + jnp.arange(Q_BLOCK)
        s = jnp.where(kpos[None, :] <= qpos[:, None], s, -jnp.inf)
        p = jax.nn.softmax(s, axis=-1)
        return jnp.einsum('bhqk,bkhd->bqhd', p.astype(v.dtype), v)

    out = lax.map(one_block, (jnp.arange(nb), qb))
    return jnp.moveaxis(out, 0, 1).reshape(b, l, h * v.shape[-1])

def mla_branch(c_q, c_kv, k_r, cos, sin, q_a_norm_g, w_q_b, kv_a_norm_g, w_kv_b, q_norm_g, k_norm_g):
    b, l, _ = c_q.shape
    q = (rmsnorm(c_q, q_a_norm_g) @ w_q_b).reshape(b, l, MLA_HEADS, D_QK)
    kv = (rmsnorm(c_kv, kv_a_norm_g) @ w_kv_b).reshape(b, l, MLA_HEADS, D_NOPE + D_V)
    k_nope, v = kv[..., :D_NOPE], kv[..., D_NOPE:]
    k_rope = jnp.broadcast_to(k_r[:, :, None, :], (b, l, MLA_HEADS, D_ROPE))
    k = jnp.concatenate([k_nope, k_rope], axis=-1)
    q = rmsnorm(q, q_norm_g)
    k = rmsnorm(k, k_norm_g)
    c4, s4 = cos[:, :, None, :], sin[:, :, None, :]
    q = jnp.concatenate([q[..., :D_NOPE], apply_rope(q[..., D_NOPE:], c4, s4)], axis=-1)
    k = jnp.concatenate([k[..., :D_NOPE], apply_rope(k[..., D_NOPE:], c4, s4)], axis=-1)
    return causal_block_attention(q, k, v)

def _ssm_combine(left, right):
    a1r, a1i, b1r, b1i = left
    a2r, a2i, b2r, b2i = right
    return (a2r * a1r - a2i * a1i,
            a2r * a1i + a2i * a1r,
            a2r * b1r - a2i * b1i + b2r,
            a2r * b1i + a2i * b1r + b2i)

def s5_branch(u, lam_re, lam_im, log_dt, b_re, b_im, c_re, c_im, d_skip, w_glu, b_glu):
    f32 = jnp.float32
    bsz, l, _ = u.shape
    uf = u.astype(f32).reshape(bsz, l, SSM_GROUPS, SSM_GROUP_CH)
    dt = jnp.exp(log_dt.astype(f32))[:, None]
    lr, li = lam_re.astype(f32), lam_im.astype(f32)
    mag = jnp.exp(lr * dt)
    a_re, a_im = mag * jnp.cos(li * dt), mag * jnp.sin(li * dt)
    den = lr * lr + li * li
    e_re, e_im = a_re - 1.0, a_im
    f_re = ((e_re * lr + e_im * li) / den)[..., None]
    f_im = ((e_im * lr - e_re * li) / den)[..., None]
    br, bi = b_re.astype(f32), b_im.astype(f32)
    bb_re = f_re * br - f_im * bi
    bb_im = f_re * bi + f_im * br
    bu_re = jnp.einsum('blgc,gnc->blgn', uf, bb_re)
    bu_im = jnp.einsum('blgc,gnc->blgn', uf, bb_im)
    a_re_t = jnp.broadcast_to(a_re, bu_re.shape)
    a_im_t = jnp.broadcast_to(a_im, bu_im.shape)
    _, _, s_re, s_im = lax.associative_scan(_ssm_combine, (a_re_t, a_im_t, bu_re, bu_im), axis=1)
    y = (jnp.einsum('blgn,gcn->blgc', s_re, c_re.astype(f32))
         - jnp.einsum('blgn,gcn->blgc', s_im, c_im.astype(f32))
         + d_skip.astype(f32) * uf)
    y = jax.nn.gelu(y.reshape(bsz, l, SSM_WIDTH)).astype(u.dtype)
    return y * jax.nn.sigmoid(y @ w_glu + b_glu)

def cross_branch(x_q, mem, mem_norm_g, w_mem_kv, xq_norm_g, xk_norm_g):
    b, l, _ = x_q.shape
    kv = rmsnorm(mem, mem_norm_g) @ w_mem_kv
    k = kv[..., :X_WIDTH].reshape(b, MEM_LEN, X_HEADS, X_HEAD_DIM)
    v = kv[..., X_WIDTH:].reshape(b, MEM_LEN, X_HEADS, X_HEAD_DIM)
    q = rmsnorm(x_q.reshape(b, l, X_HEADS, X_HEAD_DIM), xq_norm_g)
    k = rmsnorm(k, xk_norm_g)
    s = jnp.einsum('blhd,bmhd->bhlm', q, k, preferred_element_type=jnp.float32) * (X_HEAD_DIM ** -0.5)
    p = jax.nn.softmax(s, axis=-1)
    return jnp.einsum('bhlm,bmhd->blhd', p.astype(v.dtype), v).reshape(b, l, X_WIDTH)

def causal_dwconv(x, w, bias):
    c = x.shape[-1]
    y = lax.conv_general_dilated(x, w[:, None, :].astype(x.dtype), window_strides=(1,),
                                 padding=((CONV_WIDTH - 1, 0),),
                                 dimension_numbers=('NWC', 'WIO', 'NWC'),
                                 feature_group_count=c)
    return y + bias

def first_inputs(seed: int = 0) -> dict:
    key = jax.random.key(seed)
    ks = iter(jax.random.split(key, 48))
    f32 = jnp.float32
    L = DEPTH

    def nrm(shape, fan_in):
        return jax.random.normal(next(ks), shape, f32) * (fan_in ** -0.5)

    def gain(shape):
        return 1.0 + 0.02 * jax.random.normal(next(ks), shape, f32)

    def small(shape):
        return 0.01 * jax.random.normal(next(ks), shape, f32)

    x = jax.random.normal(next(ks), (BATCH, SEQ, D_MODEL), f32)
    mem = jax.random.normal(next(ks), (BATCH, MEM_LEN, D_MODEL), f32)
    offset = jax.random.randint(next(ks), (BATCH, 1), 0, 1024, dtype=jnp.int32)
    positions = offset + jnp.arange(SEQ, dtype=jnp.int32)[None, :]
    n_idx = jnp.arange(SSM_STATE, dtype=f32)
    lam_re = -0.5 + small((L, SSM_GROUPS, SSM_STATE))
    lam_im = math.pi * n_idx + small((L, SSM_GROUPS, SSM_STATE))
    log_dt = jax.random.uniform(next(ks), (L, SSM_GROUPS), f32, math.log(DT_MIN), math.log(DT_MAX))
    return {
        "x": x,
        "mem": mem,
        "positions": positions,
        "norm_mix_g": gain((L, D_MODEL)),
        "w_in": nrm((L, D_MODEL, IN_WIDTH), D_MODEL),
        "q_a_norm_g": gain((L, Q_LORA)),
        "w_q_b": nrm((L, Q_LORA, MLA_HEADS * D_QK), Q_LORA),
        "kv_a_norm_g": gain((L, KV_LORA)),
        "w_kv_b": nrm((L, KV_LORA, MLA_HEADS * (D_NOPE + D_V)), KV_LORA),
        "q_norm_g": gain((L, D_QK)),
        "k_norm_g": gain((L, D_QK)),
        "w_o_mla": nrm((L, MLA_WIDTH, D_MODEL), MLA_WIDTH),
        "ssm_lambda_re": lam_re,
        "ssm_lambda_im": lam_im,
        "ssm_log_dt": log_dt,
        "ssm_b_re": nrm((L, SSM_GROUPS, SSM_STATE, SSM_GROUP_CH), 2 * SSM_GROUP_CH),
        "ssm_b_im": nrm((L, SSM_GROUPS, SSM_STATE, SSM_GROUP_CH), 2 * SSM_GROUP_CH),
        "ssm_c_re": nrm((L, SSM_GROUPS, SSM_GROUP_CH, SSM_STATE), SSM_STATE),
        "ssm_c_im": nrm((L, SSM_GROUPS, SSM_GROUP_CH, SSM_STATE), SSM_STATE),
        "ssm_d": jax.random.normal(next(ks), (L, SSM_GROUPS, SSM_GROUP_CH), f32),
        "w_glu": nrm((L, SSM_WIDTH, SSM_WIDTH), SSM_WIDTH),
        "b_glu": small((L, SSM_WIDTH)),
        "w_o_ssm": nrm((L, SSM_WIDTH, D_MODEL), SSM_WIDTH),
        "mem_norm_g": gain((L, D_MODEL)),
        "w_mem_kv": nrm((L, D_MODEL, 2 * X_WIDTH), D_MODEL),
        "xq_norm_g": gain((L, X_HEAD_DIM)),
        "xk_norm_g": gain((L, X_HEAD_DIM)),
        "w_o_cross": nrm((L, X_WIDTH, D_MODEL), X_WIDTH),
        "b_gate": small((L, N_BRANCH * D_MODEL)),
        "w_out": nrm((L, D_MODEL, D_MODEL), D_MODEL),
        "norm_ffn_g": gain((L, D_MODEL)),
        "w_up": nrm((L, D_MODEL, 2 * D_FF), D_MODEL),
        "conv_w": nrm((L, CONV_WIDTH, 2 * D_FF), CONV_WIDTH),
        "conv_b": small((L, 2 * D_FF)),
        "w_down": nrm((L, D_FF, D_MODEL), D_FF),
    }

def first_block(x, mem, positions, norm_mix_g, w_in, q_a_norm_g, w_q_b, kv_a_norm_g, w_kv_b,
              q_norm_g, k_norm_g, w_o_mla, ssm_lambda_re, ssm_lambda_im, ssm_log_dt,
              ssm_b_re, ssm_b_im, ssm_c_re, ssm_c_im, ssm_d, w_glu, b_glu, w_o_ssm,
              mem_norm_g, w_mem_kv, xq_norm_g, xk_norm_g, w_o_cross, b_gate, w_out,
              norm_ffn_g, w_up, conv_w, conv_b, w_down):
    bsz, l, _ = x.shape
    cos, sin = rope_tables(positions)
    for i in range(DEPTH):
        h = rmsnorm(x, norm_mix_g[i])
        c_q, c_kv, k_r, u_ssm, x_q, gate_logits = split_combined(h @ w_in[i])
        y_a = mla_branch(c_q, c_kv, k_r, cos, sin, q_a_norm_g[i], w_q_b[i], kv_a_norm_g[i],
                         w_kv_b[i], q_norm_g[i], k_norm_g[i]) @ w_o_mla[i]
        y_b = s5_branch(u_ssm, ssm_lambda_re[i], ssm_lambda_im[i], ssm_log_dt[i], ssm_b_re[i],
                        ssm_b_im[i], ssm_c_re[i], ssm_c_im[i], ssm_d[i], w_glu[i], b_glu[i]) @ w_o_ssm[i]
        y_c = cross_branch(x_q, mem, mem_norm_g[i], w_mem_kv[i], xq_norm_g[i], xk_norm_g[i]) @ w_o_cross[i]
        gates = jax.nn.sigmoid(gate_logits + b_gate[i]).reshape(bsz, l, N_BRANCH, D_MODEL)
        merged = gates[:, :, 0] * y_a + gates[:, :, 1] * y_b + gates[:, :, 2] * y_c
        x = x + merged @ w_out[i]
        h2 = rmsnorm(x, norm_ffn_g[i])
        up = causal_dwconv(h2 @ w_up[i], conv_w[i], conv_b[i])
        g_ff, v_ff = up[..., :D_FF], up[..., D_FF:]
        x = x + (jax.nn.silu(g_ff) * v_ff) @ w_down[i]
    return x


DEPTH_2 = 2

SB_HEADS = 4
SB_HEAD_DIM = 64
RET_HEADS = 4
RET_QK_DIM = 64
RET_V_DIM = 128
RET_CHUNK = 128
ROPE_BASE = 10000.0
POOL_GROUPS = 4
POOL_GROUP_DIM = 64
POOL_WINDOWS = (2, 4, 8, 16)
N_BRANCHES = 3

SB_W = SB_HEADS * SB_HEAD_DIM
RET_QK_W = RET_HEADS * RET_QK_DIM
RET_V_W = RET_HEADS * RET_V_DIM
POOL_W = POOL_GROUPS * POOL_GROUP_DIM
SPLITS = (SB_W, SB_W, SB_W, RET_QK_W, RET_QK_W, RET_V_W, RET_V_W, POOL_W, N_BRANCHES * D_MODEL)
D_IN = SB_W * 3 + RET_QK_W * 2 + RET_V_W * 2 + POOL_W + N_BRANCHES * D_MODEL


def rmsnorm_2(x, g):
    xf = x.astype(jnp.float32)
    y = xf * lax.rsqrt(jnp.mean(xf * xf, axis=-1, keepdims=True) + EPS)
    return (y * g.astype(jnp.float32)).astype(x.dtype)

def swiglu_half(h, w1, w3, w2):
    return 0.5 * ((jax.nn.silu(h @ w1) * (h @ w3)) @ w2)

def stick_breaking_attention(q, k, v):
    B, S, H, dh = q.shape
    qf = (q.astype(jnp.float32) * (dh ** -0.5)).transpose(0, 2, 1, 3)
    kf = k.astype(jnp.float32).transpose(0, 2, 1, 3)
    vf = v.astype(jnp.float32).transpose(0, 2, 1, 3)
    nb = S // Q_BLOCK
    q_blocks = qf.reshape(B, H, nb, Q_BLOCK, dh).transpose(2, 0, 1, 3, 4)
    key_pos = jnp.arange(S)

    def block(args):
        qb, start = args
        z = jnp.einsum('bhqd,bhkd->bhqk', qb, kf)
        q_pos = start + jnp.arange(Q_BLOCK)
        mask = key_pos[None, :] < q_pos[:, None]
        log_beta = jax.nn.log_sigmoid(z)
        log_fail = jnp.where(mask, log_beta - z, 0.0)
        after = lax.cumsum(log_fail, axis=3, reverse=True) - log_fail
        w = jnp.where(mask, jnp.exp(log_beta + after), 0.0)
        return jnp.einsum('bhqk,bhkd->bhqd', w, vf)

    out = lax.map(block, (q_blocks, jnp.arange(nb) * Q_BLOCK))
    return out.transpose(1, 0, 3, 2, 4).reshape(B, S, H * dh)

def rotary(x, cos, sin):
    half = x.shape[-1] // 2
    x1, x2 = x[..., :half], x[..., half:]
    c = cos[None, :, None, :]
    s = sin[None, :, None, :]
    return jnp.concatenate([x1 * c - x2 * s, x2 * c + x1 * s], axis=-1)

def retention(q, k, v, g):
    B, S, H, dk = q.shape
    dv = v.shape[-1]
    half = dk // 2
    pos = jnp.arange(S, dtype=jnp.float32)
    inv_freq = ROPE_BASE ** (-jnp.arange(half, dtype=jnp.float32) / half)
    ang = pos[:, None] * inv_freq[None, :]
    cos, sin = jnp.cos(ang), jnp.sin(ang)
    qf = rotary(q.astype(jnp.float32), cos, sin)
    kf = rotary(k.astype(jnp.float32), cos, sin) * (dk ** -0.5)
    vf = v.astype(jnp.float32)
    log_gamma = jnp.log(1.0 - 2.0 ** (-5.0 - jnp.arange(H, dtype=jnp.float32)))

    C = RET_CHUNK
    N = S // C
    qc = qf.reshape(B, N, C, H, dk)
    kc = kf.reshape(B, N, C, H, dk)
    vc = vf.reshape(B, N, C, H, dv)
    idx = jnp.arange(C, dtype=jnp.float32)
    diff = idx[:, None] - idx[None, :]
    causal = diff >= 0
    decay = jnp.where(causal[None], jnp.exp(jnp.where(causal, diff, 0.0)[None] * log_gamma[:, None, None]), 0.0)
    scores = jnp.einsum('bnihd,bnjhd->bnhij', qc, kc) * decay
    intra = jnp.einsum('bnhij,bnjhe->bnihe', scores, vc)

    k_decay = jnp.exp((C - 1 - idx)[:, None] * log_gamma[None, :])
    kv = jnp.einsum('bnjhd,bnjhe->nbhde', kc * k_decay[:, :, None], vc)
    chunk_decay = jnp.exp(C * log_gamma)[None, :, None, None]

    def step(state, kv_n):
        return chunk_decay * state + kv_n, state

    _, states = lax.scan(step, jnp.zeros((B, H, dk, dv), jnp.float32), kv)
    q_decay = jnp.exp((idx + 1)[:, None] * log_gamma[None, :])
    cross = jnp.einsum('bnihd,nbhde->bnihe', qc * q_decay[:, :, None], states)

    y = (intra + cross).reshape(B, S, H, dv)
    y = y * lax.rsqrt(jnp.mean(y * y, axis=-1, keepdims=True) + EPS)
    return y.reshape(B, S, H * dv) * jax.nn.silu(g.astype(jnp.float32))

def pool_mixer(u, w_pool, pool_scale):
    B, S, _ = u.shape
    uf = u.astype(jnp.float32).reshape(B, S, POOL_GROUPS, POOL_GROUP_DIM)
    cs = jnp.concatenate([jnp.zeros((B, 1, POOL_GROUPS, POOL_GROUP_DIM), jnp.float32),
                          jnp.cumsum(uf, axis=1)], axis=1)
    t = jnp.arange(S)
    win = jnp.array(POOL_WINDOWS)
    lo = jnp.maximum(t[:, None] + 1 - win[None, :], 0)
    count = (t[:, None] + 1 - lo).astype(jnp.float32)
    cs_lo = cs[:, lo, jnp.arange(POOL_GROUPS)[None, :], :]
    mean = (cs[:, 1:] - cs_lo) / count[None, :, :, None]
    y = jnp.einsum('bsgc,gce->bsge', mean - uf, w_pool.astype(jnp.float32))
    return y.reshape(B, S, POOL_W) * pool_scale.astype(jnp.float32)

def second_inputs(seed: int = 0) -> dict:
    key = jax.random.key(seed)
    ks = jax.random.split(key, 20)

    def w(k, shape, fan_in):
        return jax.random.normal(k, shape, jnp.float32) * (fan_in ** -0.5)

    def gain(k, shape):
        return 1.0 + 0.02 * jax.random.normal(k, shape, jnp.float32)

    return {
        "x": jax.random.normal(ks[0], (BATCH, SEQ, D_MODEL), jnp.float32),
        "g_ffn1": gain(ks[1], (DEPTH_2, D_MODEL)),
        "w1_ffn1": w(ks[2], (DEPTH_2, D_MODEL, D_FF), D_MODEL),
        "w3_ffn1": w(ks[3], (DEPTH_2, D_MODEL, D_FF), D_MODEL),
        "w2_ffn1": w(ks[4], (DEPTH_2, D_FF, D_MODEL), D_FF),
        "g_mix": gain(ks[5], (DEPTH_2, D_MODEL)),
        "w_in": w(ks[6], (DEPTH_2, D_MODEL, D_IN), D_MODEL),
        "w_branch_sb": w(ks[7], (DEPTH_2, SB_W, D_MODEL), SB_W),
        "w_branch_ret": w(ks[8], (DEPTH_2, RET_V_W, D_MODEL), RET_V_W),
        "w_branch_pool": w(ks[9], (DEPTH_2, POOL_W, D_MODEL), POOL_W),
        "w_pool": w(ks[10], (DEPTH_2, POOL_GROUPS, POOL_GROUP_DIM, POOL_GROUP_DIM), POOL_GROUP_DIM),
        "pool_scale": gain(ks[11], (DEPTH_2, POOL_W)),
        "w_out": w(ks[12], (DEPTH_2, D_MODEL, D_MODEL), D_MODEL),
        "g_ffn2": gain(ks[13], (DEPTH_2, D_MODEL)),
        "w1_ffn2": w(ks[14], (DEPTH_2, D_MODEL, D_FF), D_MODEL),
        "w3_ffn2": w(ks[15], (DEPTH_2, D_MODEL, D_FF), D_MODEL),
        "w2_ffn2": w(ks[16], (DEPTH_2, D_FF, D_MODEL), D_FF),
        "g_final": gain(ks[17], (D_MODEL,)),
    }

def second_block(x, g_ffn1, w1_ffn1, w3_ffn1, w2_ffn1, g_mix, w_in, w_branch_sb, w_branch_ret,
              w_branch_pool, w_pool, pool_scale, w_out, g_ffn2, w1_ffn2, w3_ffn2, w2_ffn2, g_final):
    B, S, D = x.shape
    split_points = [int(p) for p in np.cumsum(SPLITS)[:-1]]
    for l in range(DEPTH_2):
        x = x + swiglu_half(rmsnorm_2(x, g_ffn1[l]), w1_ffn1[l], w3_ffn1[l], w2_ffn1[l])

        h = rmsnorm_2(x, g_mix[l])
        proj = h @ w_in[l]
        q_sb, k_sb, v_sb, q_r, k_r, v_r, g_r, u_p, gate = jnp.split(proj, split_points, axis=-1)
        y_sb = stick_breaking_attention(q_sb.reshape(B, S, SB_HEADS, SB_HEAD_DIM),
                                        k_sb.reshape(B, S, SB_HEADS, SB_HEAD_DIM),
                                        v_sb.reshape(B, S, SB_HEADS, SB_HEAD_DIM))
        y_ret = retention(q_r.reshape(B, S, RET_HEADS, RET_QK_DIM),
                          k_r.reshape(B, S, RET_HEADS, RET_QK_DIM),
                          v_r.reshape(B, S, RET_HEADS, RET_V_DIM), g_r)
        y_pool = pool_mixer(u_p, w_pool[l], pool_scale[l])

        gates = jax.nn.sigmoid(gate.astype(jnp.float32)).reshape(B, S, N_BRANCHES, D)
        merged = (gates[:, :, 0] * (y_sb @ w_branch_sb[l].astype(jnp.float32))
                  + gates[:, :, 1] * (y_ret @ w_branch_ret[l].astype(jnp.float32))
                  + gates[:, :, 2] * (y_pool @ w_branch_pool[l].astype(jnp.float32)))
        x = x + merged.astype(x.dtype) @ w_out[l]

        x = x + swiglu_half(rmsnorm_2(x, g_ffn2[l]), w1_ffn2[l], w3_ffn2[l], w2_ffn2[l])
    return rmsnorm_2(x, g_final)


def setup_inputs(seed=0):
    out = dict(first_inputs(seed))
    for name, value in second_inputs(seed + 1).items():
        if name != "x":
            out[name + "_2"] = value
    return out


def reference(
    x, mem, positions, norm_mix_g, w_in, q_a_norm_g, w_q_b, kv_a_norm_g, w_kv_b, q_norm_g,
    k_norm_g, w_o_mla, ssm_lambda_re, ssm_lambda_im, ssm_log_dt, ssm_b_re, ssm_b_im, ssm_c_re,
    ssm_c_im, ssm_d, w_glu, b_glu, w_o_ssm, mem_norm_g, w_mem_kv, xq_norm_g, xk_norm_g,
    w_o_cross, b_gate, w_out, norm_ffn_g, w_up, conv_w, conv_b, w_down, g_ffn1_2, w1_ffn1_2,
    w3_ffn1_2, w2_ffn1_2, g_mix_2, w_in_2, w_branch_sb_2, w_branch_ret_2, w_branch_pool_2,
    w_pool_2, pool_scale_2, w_out_2, g_ffn2_2, w1_ffn2_2, w3_ffn2_2, w2_ffn2_2, g_final_2,
):
    x = first_block(
        x, mem, positions, norm_mix_g, w_in, q_a_norm_g, w_q_b, kv_a_norm_g, w_kv_b, q_norm_g,
        k_norm_g, w_o_mla, ssm_lambda_re, ssm_lambda_im, ssm_log_dt, ssm_b_re, ssm_b_im,
        ssm_c_re, ssm_c_im, ssm_d, w_glu, b_glu, w_o_ssm, mem_norm_g, w_mem_kv, xq_norm_g,
        xk_norm_g, w_o_cross, b_gate, w_out, norm_ffn_g, w_up, conv_w, conv_b, w_down,
    )
    return second_block(
        x, g_ffn1_2, w1_ffn1_2, w3_ffn1_2, w2_ffn1_2, g_mix_2, w_in_2, w_branch_sb_2,
        w_branch_ret_2, w_branch_pool_2, w_pool_2, pool_scale_2, w_out_2, g_ffn2_2, w1_ffn2_2,
        w3_ffn2_2, w2_ffn2_2, g_final_2,
    )


_drawn_inputs = setup_inputs


def setup_inputs(seed=0):
    import zlib

    import numpy as np

    out = dict(_drawn_inputs(seed))
    spreads = {}
    factors = {'norm_mix_g': 6.448,
     'q_a_norm_g': 8.0,
     'kv_a_norm_g': 8.0,
     'q_norm_g': 8.0,
     'k_norm_g': 8.0,
     'ssm_lambda_re': 200.0,
     'ssm_b_re': 3.172,
     'ssm_b_im': 3.131,
     'ssm_c_re': 3.191,
     'ssm_c_im': 3.179,
     'b_glu': 49.483,
     'mem_norm_g': 8.0,
     'xq_norm_g': 8.0,
     'xk_norm_g': 8.0,
     'b_gate': 8.0,
     'norm_ffn_g': 2.826,
     'conv_b': 5.977,
     'g_ffn1_2': 5.147,
     'g_mix_2': 2.924,
     'pool_scale_2': 15.953,
     'g_ffn2_2': 19.612,
     'g_final_2': 23.158}
    for name, (base, spread) in spreads.items():
        noise = np.random.default_rng([zlib.crc32(name.encode()), seed]).standard_normal(out[name].shape)
        drawn = base * np.exp(spread * noise) if base else spread * noise
        out[name] = __import__('jax').numpy.asarray(drawn.astype(out[name].dtype))
    for name, factor in factors.items():
        out[name] = (out[name] * factor).astype(out[name].dtype)
    return out
```

```python
from contextlib import ExitStack

import numpy as np

import concourse.bass as bass
from concourse import mybir

F32 = mybir.dt.float32
FR = mybir.dt.float32r
I32 = mybir.dt.int32
ALU = mybir.AluOpType
ACT = mybir.ActivationFunctionType
AX = mybir.AxisListType

P = 128
TOK = 256
T = TOK // P
D = 1024
KD = D // P
EPS = 1e-6
H_MLA, DQK, DNOPE, DROPE, DV = 8, 96, 64, 32, 64
Q_LORA, KV_LORA = 384, 256
XH, XD = 4, 128
SSM_W = 512
GROUPS, GCH, NST = 32, 16, 64
ST = GROUPS * NST // P
DFF = 2816
NF = DFF // P
NI = NF // 2
LAYERS = 2
SBH, RH = 4, 4
POOLS = (2, 4, 8, 16)

Y_SLOTS = (14, 17, 21, 25)
DVE_LAYER_STEPS = 105

UW = 2048
RING = 3
U_MIX1, U_FFN, U_MIX2 = 37, 3 * NI, 30
U_BLOCK1 = U_MIX1 + U_FFN
U_LAYER = U_FFN + U_MIX2 + U_FFN
U_USED = U_BLOCK1 + LAYERS * U_LAYER
U_ALL = U_USED + RING - 1

MAGIC = 1.5 * 2.0 ** 23
TWO_PI = 2.0 * np.pi
PI_LOW = float(np.nextafter(np.float32(np.pi), np.float32(0)))


def _cody_waite():
    def cut(v, bits):
        m, e = np.frexp(v)
        return float(np.ldexp(np.trunc(m * 2.0 ** bits), int(e) - bits))
    a = cut(TWO_PI, 11)
    b = cut(TWO_PI - a, 11)
    return a, b, float(np.float32(TWO_PI - a - b))


CW = _cody_waite()

C1 = {}
_at = 0
for _n, _w in (("ident", P), ("ones", P), ("causal", 3 * P), ("g_mem", KD), ("g_mix", KD), ("g_qa", 3), ("g_kva", 2),
               ("g_xq", 1), ("g_xk", 1), ("b_glu", 4), ("ssm_d", 4), ("g_ffn", KD), ("b_gate", 3 * KD),
               ("gq_nope", 1), ("gk_nope", 1), ("gq_rope", DROPE), ("gk_rope", DROPE), ("inv_freq", DROPE // 2),
               ("lam_re", ST), ("lam_im", ST), ("log_dt", ST), ("conv_b", 2 * NF), ("conv_w", 6 * NF)):
    C1[_n] = (_at, _w)
    _at += _w
NC1 = _at

C2 = {}
_at = 0
for _n, _w in (("decay", RH * 3 * P), ("pool", 4 * 3 * P), ("cos", TOK), ("sin", TOK), ("rot", P), ("after", P),
               ("strict", 3 * P)):
    C2[_n] = (_at, _w)
    _at += _w
NC2 = _at

LC = {}
_at = 0
for _n, _w in (("g_ffn1", KD), ("g_mix", KD), ("g_ffn2", KD), ("pool_scale", 2), ("w_pool", 2 * P)):
    LC[_n] = (_at, _w)
    _at += _w
NLC = _at


class Plan:

    def __init__(self):
        self.jobs = {}
        self.count = {False: 0, True: 0}
        self.uses = {}
        self.unit_end = {}

    def add(self, name, place, layer):
        k = self.count[layer]
        self.count[layer] += 1
        u = None
        if place:
            per = self.uses.setdefault(place, {False: 0, True: 0})
            u = (place, per[layer])
            per[layer] += 1
        assert (name, layer) not in self.jobs, name
        self.jobs[(name, layer)] = (k, u)

    def done(self, name, l=None):
        k, _ = self.jobs[(name, l is not None)]
        if l is None:
            return k + 1
        return l * self.count[True] + (self.count[False] + k + 1)

    def use(self, name, l=None):
        place, k = self.jobs[(name, l is not None)][1]
        if l is None:
            return k
        return l * self.uses[place][True] + (self.uses[place][False] + k)

    def unit_done(self, k, l=None):
        return self.done(self.unit_end[(k, l is not None)], l)

    def place(self, name, l=None):
        return self.jobs[(name, l is not None)][1][0]


UNITS1 = [["mku0", "mku1"], ["mk0", "mk1"], ["mvu0", "mvu1"], ["mv0", "mv1"], ["xq0"], ["xq1"], ["ux0"], ["ux1"],
          ["c0"], ["c1"], ["c2"], ["gc0"], ["kv"], ["qb"], ["qa"], ["gc1"], ["gc2"], ["gc3"], ["bc0", "bc1"],
          ["bc2", "bc3"], ["gs0"], ["gs1"], ["gs2"], ["gs3"], ["gm0"], ["gm1"], ["gm2"], ["gl0", "gl1"], ["gm3"],
          ["bs0", "bs1"], ["bs2", "bs3"], ["bm0", "bm1"], ["bm2", "bm3"], ["wou0"],
          ["wou1"], ["wou2"], ["wo"]]
UNITS2 = [["sbq"], ["sbk"], ["sbv"], ["rq"], ["rk"], ["rvu0", "rvu1"], ["rv0", "rv1"], ["up"], ["rgu0", "rgu1"],
          ["rg0", "rg1"], ["ga0"], ["ga1"], ["ga2"], ["ga3"], ["ba0", "ba1", "ba2", "ba3"], ["gp0"], ["gp1"],
          ["gp2"], ["gp3"], ["bp0", "bp1", "bp2", "bp3"], ["gr0"], ["gr1"], ["gr2"], ["gr3"], ["br0", "br1"],
          ["br2", "br3"], ["wou0"], ["wou1"], ["wou2"], ["wo"]]


def make_plan():
    plan = Plan()
    turn = [0]

    def part(name, layer):
        plan.add(name, f"p{turn[0] % 3}", layer)
        turn[0] += 1

    def small(name, place, layer):
        plan.add(name, place, layer)

    def norm(tag, layer):
        for c in range(KD // 2):
            small(f"{tag}T{c}", None, layer)

    def ffn(tag, layer, u0):
        names = [("A0", "p0"), ("B0", "p1")]
        for i in range(1, NI):
            names += [(f"A{i}", "p0"), (f"B{i}", "p1"), (f"D{i - 1}", None)]
        names.append((f"D{NI - 1}", "big"))
        for n, (name, place) in enumerate(names):
            small(tag + name, place, layer)
            plan.unit_end[(u0 + n, layer)] = tag + name

    small("bT", "big", False)
    norm("mem", False)
    norm("x", False)
    turn[0] = 0
    for u in range(U_MIX1):
        for j in UNITS1[u]:
            if j in ("wo", "kv", "qa"):
                small(j, "big", False)
            elif j[-2:] in ("u0", "u1", "u2"):
                small(j, None, False)
            elif u < 7:
                part(j, False)
            else:
                small(j, f"p{turn[0] % 2}", False)
                turn[0] += 1
            plan.unit_end[(u, False)] = j
        for j, place in {3: [("kT", "big")], 6: [("ssq", "p3"), ("xs", "big")], 9: [("xp", "big")],
                         10: [("xo", "big")], 11: [("cs", "big")], 24: [("tq0", "big")], 25: [("sc0", "big")],
                         26: [("tq1", "big")], 27: [("sc1", "big")], 28: [("pt0", "big")],
                         29: [("pv0", "p3"), ("pt1", "big")], 30: [("pv1", "p3")]}.get(u, []):
            small(j, place, False)
        if u == 6:
            turn[0] = 0
        if 7 <= u < 7 + ST:
            small(f"bu{u - 7}", "p3", False)
        if 9 <= u < 9 + ST:
            small(f"cy{u - 9}", "p2" if (u - 9) % 4 == 3 else None, False)
    norm("f0", False)
    ffn("f0", False, U_MIX1)
    turn[0] = 0
    norm("f1", True)
    ffn("f1", True, 0)
    norm("m", True)
    for u in range(U_MIX2):
        for j in UNITS2[u]:
            if j == "wo":
                small("wo", "big", True)
            elif j[-2:] in ("u0", "u1", "u2"):
                small(j, None, True)
            else:
                part(j, True)
            plan.unit_end[(U_FFN + u, True)] = j
        for j, place in {3: [("z", "big")], 6: [("pq", "p3"), ("sa", "big")], 8: [("pk", "p3")], 9: [("pv", "p3"),
                         ("rs", "big")], 11: [("ry", "big"), ("pl1", "p3")], 12: [("pl2", "p3")],
                         14: [("rt", "big")]}.get(u, []):
            small(j, place, True)
    norm("f2", True)
    ffn("f2", True, U_FFN + U_MIX2)
    return plan


class Steps:

    def __init__(self, eng, sem):
        self.eng, self.sem, self.n, self.loops = eng, sem, 0, []

    def __call__(self, ins):
        ins.then_inc(self.sem, 1)
        self.n += 1
        self.wait()

    def wait(self):
        v = self.n
        for var, per, _ in self.loops:
            v = var * per + v
        self.eng.wait_ge(self.sem, v)

    def enter(self, var, per):
        self.loops.append((var, per, self.n))

    def leave(self, turns):
        _, per, at = self.loops.pop()
        assert self.n - at == per, f"{self.eng}: {self.n - at} steps in a turn, not {per}"
        self.n = at + per * turns


def build_program(nc, ws, c1_d, c2_d, lc_d, bc_d, x_d, mem_d, pos_d, gfin_d, out_d, debug=None):
    plan = make_plan()
    n_layers = LAYERS
    with ExitStack() as ctx:
        def sb(name, shape, dt=F32):
            return ctx.enter_context(nc.sbuf_tensor(name, shape, dt))

        sems = {}

        def S(name):
            if name not in sems:
                sems[name] = ctx.enter_context(nc.semaphore(name))
            return sems[name]

        raw = sb("raw", [P, RING, UW])
        whi = sb("whi", [P, RING, UW], FR)
        wlo = sb("wlo", [P, RING, UW], FR)
        h_hi = sb("h_hi", [P, KD, TOK], FR)
        h_lo = sb("h_lo", [P, KD, TOK], FR)
        b_hi = sb("b_hi", [P, KD, TOK], FR)
        b_lo = sb("b_lo", [P, KD, TOK], FR)
        x = sb("x_rows", [P, T, D])
        c1 = sb("c1", [P, NC1])
        lc = sb("lc", [P, NLC])
        sm = sb("sm", [P, 1700])
        pos = sb("pos", [P, T], I32)
        s5c = sb("s5c", [P, 2048])
        s5x = sb("s5x", [P, 1024])
        ar = sb("ar", [P, 18432])

        pb = {n: ctx.enter_context(nc.psum_tensor(n, [P, 512], F32)) for n in ("p0", "p1", "p2", "p3")}
        big = ctx.enter_context(nc.psum_tensor("big", [P, 4, 512], F32))
        bigf = big[:, :, :].rearrange("p a b -> p (a b)")

        def area(at, n):
            return ar[:, at:at + n]

        XS, MG, GT, R, W = 0, 2048, 4096, 8192, 12288
        xs = area(XS, 2048).rearrange("p (t d) -> p t d", t=T)
        memx = xs
        merged = area(MG, 2048).rearrange("p (m t) -> p m t", m=KD)
        junk_act, junk_dve = area(MG, 1024), area(MG + 1024, 1024)
        gates = area(GT, 4096).rearrange("p (g t) -> p g t", g=16)
        f_s = area(GT, 512).rearrange("p (a t) -> p a t", a=2)
        f_g = area(GT + 512, 512).rearrange("p (a t) -> p a t", a=2)
        f_c = area(GT + 1024, 1024).rearrange("p (a t) -> p a t", a=2)

        def col(name, k=0, n=1):
            a, _ = C1[name]
            return c1[:, a + k:a + k + n]

        ident, ones, causal = (c1[:, C1[n][0]:C1[n][0] + C1[n][1]] for n in ("ident", "ones", "causal"))
        c2 = area(W, NC2)

        def col2(name):
            a, w = C2[name]
            return c2[:, a:a + w]

        def lcol(name, k=0, n=1):
            a, _ = LC[name]
            return lc[:, a + k:a + k + n]

        smt = [0]

        def small(n):
            a = smt[0]
            smt[0] += n
            assert smt[0] <= 1700
            return sm[:, a:a + n]

        ss, msq, rstd = small(2), small(2), small(2)
        neg_half = small(16)

        ang, tri_k, tri_r, tri_w, tri_m = small(48), small(48), small(48), small(48), small(48)
        cos48, sin48 = small(48), small(48)
        theta, rope_c, rope_s = ang[:, 0:ST], cos48[:, ST:], sin48[:, ST:]
        dt_, mag = small(ST), small(ST)
        tA, tB, tC, tD = small(ST), small(ST), small(ST), small(ST)
        f_re, f_im = small(ST), small(ST)
        pA, pB = small(ST), small(ST)
        pw = [(small(ST), small(ST)), (small(ST), small(ST))]
        e128n = small(ST)
        ini = small(2)
        posf = small(T)
        gxx, gqk = small(1), small(1)
        hb = small(3 * KD)
        ssk, rsk, msx, rsq = small(8), small(8), small(8), small(8)
        xmax, xneg, xsum, xrec, xscl = small(8), small(8), small(8), small(8), small(8)
        msc, rc = small(4), small(4)
        mq, mk, rq_, rk_, mkr, qsc = small(16), small(16), small(16), small(16), small(2), small(16)
        qmx, qng, qsm, qrc = small(8), small(8), small(8), small(8)
        kr, krg, kro = small(64), small(64), small(64)
        rtmp = [small(32) for _ in range(4)]
        rms8, rr8 = small(8), small(8)

        E_c = area(W, ST * P).rearrange("p (j t) -> p j t", j=ST)
        E_s = area(W + ST * P, ST * P).rearrange("p (j t) -> p j t", j=ST)
        s5_m1, s5_m2 = area(W + 4096, 512), area(W + 4608, 512)
        s5_z = [area(W + 5120, 512), area(W + 5632, 512)]
        s5_p, s5_q = s5x[:, 0:512], s5x[:, 512:1024]
        Bl = [s5c[:, 512 * a:512 * (a + 1)].rearrange("p (b n) -> p b n", b=4) for a in range(2)]
        Cl = [s5c[:, 1024 + 512 * a:1536 + 512 * a].rearrange("p (j c) -> p j c", j=ST) for a in range(2)]
        bcr = area(R, 4 * ST * GCH).rearrange("p (a j c) -> p a j c", a=4, j=ST)
        bbd = area(R + 1024, 1024).rearrange("p (a j c) -> p a j c", a=2, j=ST)
        btmp = area(R + 2048, 512).rearrange("p (a j c) -> p a j c", a=2, j=ST)
        e_tmp = [area(GT + 1024 * i, 1024).rearrange("p (j t) -> p j t", j=ST) for i in range(4)]
        kt_x = area(R, 1024).rearrange("p (h t) -> p h t", h=XH)
        v_x = area(R + 1024, 1024).rearrange("p (t n) -> p t n", t=T)
        q_x = area(R + 2048, 1024).rearrange("p (h t) -> p h t", h=XH)
        u_fm = area(R + 3072, 1024).rearrange("p (b t) -> p b t", b=4)
        k_x = area(MG, 1024).rearrange("p (t n) -> p t n", t=T)
        sq_x = area(MG + 1024, 1024).rearrange("p (h t) -> p h t", h=XH)
        p_x = area(GT, 2048).rearrange("p (a t) -> p a t", a=8)
        pT_x = area(GT + 2048, 2048)
        x_y = area(GT + 2048, 1024)
        c_sq = area(MG, 5 * TOK).rearrange("p (c t) -> p c t", c=5)
        K_m = area(R, 16 * DQK).rearrange("p (a d) -> p a d", a=16)
        Q_m = area(R + 1536, 16 * DQK)
        Qh = Q_m.rearrange("p (a d) -> p a d", a=16)
        V_m = area(XS + 1024, 1024).rearrange("p (t n) -> p t n", t=T)
        m_sq = area(MG, 1536)
        m_t = [area(MG + 256 * i, 256) for i in range(4)]
        QT, KT = area(W, 1024), area(W + 1024, 1024)
        P_m = [area(W + 2048 + 1536 * g, 1536).rearrange("p (h c) -> p h c", h=4) for g in range(2)]
        PT = area(W, 1536).rearrange("p (h c) -> p h c", h=4)
        y_s = area(XS, 1024).rearrange("p (b t) -> p b t", b=4)
        sg_s = area(W + 5120, 1024).rearrange("p (b t) -> p b t", b=4)
        A_z, C_z, B_z = (area(a, 1536).rearrange("p (h c) -> p h c", h=4) for a in (GT, GT + 1536, W + 4608))
        sbq, sbk, sbv = area(R, 512), area(R + 512, 512), area(R + 1024, 512)
        rq, rk, rt = area(R + 1536, 512), area(R + 2048, 512), area(R + 2560, 512)
        rv = area(R + 3072, 1024).rearrange("p (t n) -> p t n", t=T)
        rg, up = area(XS, 1024), area(XS + 1024, 512)
        y_sq, y_n = area(GT + 2048, 1024), area(R, 1024)

        def slot(u):
            return u % RING

        def wait(eng, name, v):
            if isinstance(v, int) and v <= 0:
                return
            eng.wait_ge(S(name), v)

        def lv(l, per, c):
            return c if l is None else l * per + c

        def job_done(eng, name, l=None):
            eng.wait_ge(S("pe_done"), plan.done(name, l))

        def place_read(eng, name, l=None):
            wait(eng, plan.place(name, l) + "_read", plan.use(name, l) + 1)

        def place_free(eng, name, l=None):
            wait(eng, plan.place(name, l) + "_read", plan.use(name, l))

        def read_sem(name, l=None):
            return S(plan.place(name, l) + "_read")

        def bank(name, l=None):
            return pb[plan.place(name, l)]

        def unit(k, l=None):
            return k if l is None else l * U_LAYER + (U_BLOCK1 + k)

        def ustat(k, l=None):
            return k if l is None else U_BLOCK1 + k

        def last_split(eng, l):
            s = U_BLOCK1 - 1 + RING
            eng.wait_ge(S("pe_done"), l * plan.count[True] + plan.count[False])
            return s % RING, l * (U_LAYER // RING) + (s // RING + 1), l * U_LAYER + (s + 1)

        def norm_no(k, l=None):
            return k if l is None else l * 3 + (3 + k)

        block = ctx.enter_context(nc.Block())

        @block.sync
        def _(sp):
            sp.dma_start(c1[:, :], c1_d).then_inc(S("c1_in"), 16)
            sp.dma_start(xs, mem_d.rearrange("t p d -> p t d")).then_inc(S("mem_in"), 16)
            for r in range(RING):
                sp.dma_start(raw[:, r, :], ws[r]).then_inc(S(f"raw_in{r}"), 16)
            turns = (U_ALL - RING) // RING
            with sp.Fori(0, turns) as i:
                for r in range(RING):
                    sp.wait_ge(S("lo_done"), i * RING + (r + 1))
                    sp.dma_start(raw[:, r, :], ws[i * RING + (RING + r)]).then_inc(S(f"raw_in{r}"), 16)
            for u in range(RING + turns * RING, U_ALL):
                sp.wait_ge(S("lo_done"), u - RING + 1)
                sp.dma_start(raw[:, u % RING, :], ws[u]).then_inc(S(f"raw_in{u % RING}"), 16)
            for t in range(T):
                sp.wait_ge(S("out_ready"), t + 1)
                sp.dma_start(out_d[t], xs[:, t, :]).then_inc(S("out_sent"), 16)
            sp.wait_ge(S("out_sent"), 16 * T)
            for r in range(RING):
                sp.wait_ge(S(f"raw_in{r}"), 16 * len(range(r, U_ALL, RING)))

        def split_act(act, s, l=None, m=None):
            us = ustat(s, l) + RING
            r, q = us % RING, us // RING + 1
            done = plan.unit_done(s, l)
            if l is not None:
                q = l * (U_LAYER // RING) + q
            if m is not None:
                q, done = m * 2 + q, m * 6 + done
            act.wait_ge(S(f"raw_in{r}"), q * 16)
            act.wait_ge(S("pe_done"), done)
            act.activation(whi[:, r, :], raw[:, r, :], ACT.Copy).then_inc(S("hi_done"), 1)

        def split_dve(dve, s, l=None, m=None):
            r = (ustat(s, l) + RING) % RING
            n = unit(s, l) + (RING + 1)
            if m is not None:
                n = m * 6 + n
            dve.wait_ge(S("hi_done"), n)
            dve.tensor_tensor(wlo[:, r, :], raw[:, r, :], whi[:, r, :].bitcast(F32), ALU.subtract)\
               .then_inc(S("lo_done"), 1)

        @block.gpsimd
        def _(pool):
            step = Steps(pool, S("pool_step"))
            nc.gpsimd.dma_start(bcr, bc_d).then_inc(S("bc_in"), 16)
            nc.gpsimd.dma_start(pos[:, :], pos_d).then_inc(S("pos_in"), 16)
            step(nc.gpsimd.memset(neg_half, -0.5))
            step(nc.gpsimd.memset(area(R + 1024, 1024), 0.0))
            nc.gpsimd.memset(s5c[:, 1024:2048], 0.0).then_inc(S("bd_zero"), 1)

            def rsqrt(dst, src, n, ready, v, done):
                pool.wait_ge(S(ready), v)
                nc.gpsimd.tensor_tensor(dst, src, neg_half[:, 0:n], ALU.pow).then_inc(S(done), 1)

            def norm(n):
                rsqrt(rstd, msq, 2, "msq", n + 1, "rstd")

            norm(0)
            norm(1)
            pool.wait_ge(S("trig"), 2)
            step(nc.gpsimd.memset(E_c[:, :, 0:1], 1.0))
            step(nc.gpsimd.memset(E_s[:, :, 0:1], 0.0))
            e, s = (cos48[:, 0:ST], sin48[:, 0:ST]), 1
            while s < P:
                pc, ps = (a.unsqueeze(2).to_broadcast([P, ST, s]) for a in e)
                a = [t[:, :, 0:s] for t in e_tmp]
                step(nc.gpsimd.tensor_tensor(a[0], E_c[:, :, 0:s], pc, ALU.mult))
                step(nc.gpsimd.tensor_tensor(a[1], E_s[:, :, 0:s], ps, ALU.mult))
                step(nc.gpsimd.tensor_tensor(a[2], E_c[:, :, 0:s], ps, ALU.mult))
                step(nc.gpsimd.tensor_tensor(a[3], E_s[:, :, 0:s], pc, ALU.mult))
                step(nc.gpsimd.tensor_tensor(E_c[:, :, s:2 * s], a[0], a[1], ALU.subtract))
                step(nc.gpsimd.tensor_tensor(E_s[:, :, s:2 * s], a[2], a[3], ALU.add))
                to = pw[1] if e[0] is pw[0][0] else pw[0]
                step(nc.gpsimd.tensor_tensor(pA, e[0], e[0], ALU.mult))
                step(nc.gpsimd.tensor_tensor(pB, e[1], e[1], ALU.mult))
                step(nc.gpsimd.tensor_tensor(to[0], pA, pB, ALU.subtract))
                step(nc.gpsimd.tensor_tensor(pA, e[0], e[1], ALU.mult))
                step(nc.gpsimd.tensor_tensor(to[1], pA, pA, ALU.add))
                e, s = to, 2 * s
            assert e is pw[0]
            nc.gpsimd.tensor_scalar(e128n, e[1], -1.0, None, ALU.mult).then_inc(S("E_ready"), 1)
            rsqrt(rsk, ssk, 8, "kx_msq", 1, "kx_rstd")
            rsqrt(rsq, msx, 8, "p3_read", plan.use("ssq") + 1, "xq_rstd")

            def rotate_out(j):
                z4 = s5_z[j % 2].rearrange("p (a t) -> p a t", a=4)
                pool.wait_ge(S("z_ready"), j + 1)
                if j:
                    job_done(pool, f"cy{j - 1}")
                ec, es = (a[:, j, :].unsqueeze(1).to_broadcast([P, 4, P]) for a in (E_c, E_s))
                step(nc.gpsimd.tensor_tensor(s5_p.rearrange("p (a t) -> p a t", a=4), z4, ec, ALU.mult))
                step(nc.gpsimd.tensor_tensor(s5_q.rearrange("p (a t) -> p a t", a=4), z4, es, ALU.mult))
                step(nc.gpsimd.tensor_tensor(s5_p[:, 0:TOK], s5_p[:, 0:TOK], s5_q[:, TOK:], ALU.subtract))
                nc.gpsimd.tensor_tensor(s5_p[:, TOK:], s5_p[:, TOK:], s5_q[:, 0:TOK], ALU.add).then_inc(S("s_ready"), 1)
                pool.wait_ge(S("s_ready"), j + 1)

            for j in range(ST):
                rotate_out(j)
                if j == 3:
                    rsqrt(rc, msc, 4, "big_read", plan.use("cs") + 1, "c_rstd")
                if j == 8:
                    rsqrt(rq_, mq, 16, "mq_msq", 1, "mq_rstd")
                    rsqrt(rk_, mk, 16, "mk_msq", 1, "mk_rstd")
            norm(2)
            pool.wait_ge(S("p3_read"), plan.use("pv1") + 1)
            nc.gpsimd.dma_start(c2, c2_d).then_inc(S("c2_in"), 16)
            with pool.Fori(0, LAYERS) as l:
                pool.wait_ge(S("h_lo"), l * (3 * KD) + 3 * KD)
                nc.gpsimd.dma_start(lc[:, :], lc_d[l]).then_inc(S("lc_in"), 16)
                norm(l * 3 + 3)
                norm(l * 3 + 4)
                rsqrt(rr8, rms8, 8, "y_msq", l + 1, "y_rstd")
                norm(l * 3 + 5)
            nc.gpsimd.dma_start(area(R, D), gfin_d).then_inc(S("gfin_in"), 16)
            norm(3 + 3 * LAYERS)

        @block.tensor
        def _(pe):
            def mm3(out, s, m, start, stop):
                pe.matmul(out, s[0], m[0], start=start, stop=False)
                pe.matmul(out, s[0], m[1], start=False, stop=False)
                return pe.matmul(out, s[1], m[0], start=False, stop=stop)

            def w(k, l, a, n):
                r = slot(ustat(k, l))
                return whi[:, r, a:a + n], wlo[:, r, a:a + n]

            def hk(k, lo=0, n=TOK):
                return h_hi[:, k, lo:lo + n], h_lo[:, k, lo:lo + n]

            def bk(k, lo=0, n=TOK):
                return b_hi[:, k, lo:lo + n], b_lo[:, k, lo:lo + n]

            def bk_from(k0):
                return lambda k, lo=0, n=TOK: bk(k0 + k, lo, n)

            def unit_in(k, l=None, extra=0):
                pe.wait_ge(S("lo_done"), extra + unit(k, l) + 1)

            def fin(ins):
                ins.then_inc(S("pe_done"), 1)

            def norm_T(n):
                pe.wait_ge(S("xs_dve"), n + 1)
                pe.wait_ge(S("xs_act"), n + 1)
                for c in range(KD // 2):
                    for k in (2 * c, 2 * c + 1):
                        for t in range(T):
                            last = pe.transpose(big[:, c, (k % 2) * TOK + t * P:(k % 2) * TOK + (t + 1) * P],
                                                xs[:, t, k * P:(k + 1) * P], ident)
                    fin(last)

            def fm(k, l, out, moving, K, m, n=None):
                for kk in range(K):
                    if n is not None:
                        pe.wait_ge(S("h_lo"), n * KD + (kk + 1))
                    last = mm3(out, w(k, l, (m * K + kk) * P, P), moving(kk), kk == 0, kk == K - 1)
                return last

            def fm_unit(k, l, name, n=None):
                unit_in(k, l)
                place_free(pe, name, l)
                b = bank(name, l)
                fm(k, l, b[:, 0:TOK], hk, KD, 0, n)
                fin(fm(k, l, b[:, TOK:], hk, KD, 1))

            def tm_half(k, l, name, half, moving=hk):
                unit_in(k, l)
                for t in range(T):
                    job = name + str(t)
                    if half == 0:
                        place_free(pe, job, l)
                    for q in range(4):
                        kk = half * 4 + q
                        last = mm3(bank(job, l)[:, :], moving(kk, t * P, P), w(k, l, q * 512, 512),
                                   kk == 0, kk == KD - 1)
                    fin(last)

            def tm_unit(k, l, name):
                unit_in(k, l)
                place_free(pe, name, l)
                for t in range(T):
                    for kk in range(KD):
                        last = mm3(bank(name, l)[:, t * TOK:(t + 1) * TOK], hk(kk, t * P, P), w(k, l, kk * TOK, TOK),
                                   kk == 0, kk == KD - 1)
                fin(last)

            def branch(k, l, names, moving, K):
                unit_in(k, l)
                for j, name in enumerate(names):
                    place_free(pe, name, l)
                    b = bank(name, l)
                    fm(k, l, b[:, 0:TOK], moving, K, 2 * j)
                    fin(fm(k, l, b[:, TOK:], moving, K, 2 * j + 1))

            def w_out(k, l):
                place_free(pe, "wo", l)
                m_base = 0 if l is None else l * 4 + 4
                for q in range(4):
                    kh, nh = q // 2, q % 2
                    pe.wait_ge(S("m_lo"), m_base + (2 + 2 * kh))
                    unit_in(k + q, l)
                    for t in range(T):
                        for a in range(4):
                            kk = kh * 4 + a
                            last = mm3(big[:, 2 * t + nh, :], hk(kk, t * P, P), w(k + q, l, a * 512, 512),
                                       kk == 0, kk == KD - 1)
                    fin(last)

            def ffn(k0, l, tag, n):
                ua, ub = plan.use(tag + "A0", l), plan.use(tag + "B0", l)

                def up(k, place, used, extra=0, n=None):
                    unit_in(k, l, extra)
                    wait(pe, place + "_read", used)
                    b = pb[place]
                    fm(k, l, b[:, 0:TOK], hk, KD, 0, n)
                    fin(fm(k, l, b[:, TOK:], hk, KD, 1))

                def down(k, start, stop, i, par, extra=0):
                    unit_in(k, l, extra)
                    pe.wait_ge(S("p0_read"), i + (ua + 1))
                    pe.wait_ge(S("p1_read"), i + (ub + 1))
                    for t in range(T):
                        for nh in range(2):
                            for a in range(2):
                                last = mm3(big[:, 2 * t + nh, :], bk(2 * par + a, t * P, P),
                                           w(k, l, a * D + nh * 512, 512), start and a == 0, stop and a == 1)
                    fin(last)

                up(k0, "p0", ua, n=n)
                up(k0 + 1, "p1", ub)
                up(k0 + 2, "p0", ua + 1)
                up(k0 + 3, "p1", ub + 1)
                down(k0 + 4, True, False, 0, 0)
                up(k0 + 5, "p0", ua + 2)
                up(k0 + 6, "p1", ub + 2)
                down(k0 + 7, False, False, 1, 1)
                with pe.Fori(0, (NI - 3) // 2) as m:
                    for h in range(2):
                        up(k0 + 8 + 3 * h, "p0", m * 2 + (ua + 3 + h), extra=m * 6)
                        up(k0 + 9 + 3 * h, "p1", m * 2 + (ub + 3 + h), extra=m * 6)
                        down(k0 + 10 + 3 * h, False, False, m * 2 + (2 + h), h, extra=m * 6)
                down(k0 + 32, False, True, NI - 1, (NI - 1) % 2)

            pe.wait_ge(S("c1_in"), 16)
            pe.wait_ge(S("bbd"), 1)
            for a in range(2):
                for b in range(4):
                    last = pe.transpose(big[:, a, b * P:(b + 1) * P],
                                        bbd[:, a, 4 * b:4 * b + 4, :].rearrange("p j c -> p (j c)"), ident)
            fin(last)
            place_read(pe, "bT")
            norm_T(0)
            pe.wait_ge(S("h_lo"), KD)
            norm_T(1)

            def s5_in(j):
                if j % 8 == 0:
                    place_read(pe, "ux0" if j == 0 else "ux1")
                place_free(pe, f"bu{j}")
                b, q = j // 4, 32 * (j % 4)
                for a in range(2):
                    last = pe.matmul(pb["p3"][:, a * TOK:(a + 1) * TOK], Bl[a][q:q + 32, b, :],
                                     u_fm[q:q + 32, b, :], start=True, stop=True, tile_position=(q, 0))
                fin(last)

            def s5_out(j):
                b, q = j // 4, 32 * (j % 4)
                if j % 4 == 0:
                    place_free(pe, f"cy{j + 3}")
                pe.wait_ge(S("s_ready"), j + 1)
                out = pb["p2"][q:q + 32, (b % 2) * TOK:(b % 2 + 1) * TOK]
                pe.matmul(out, Cl[0][:, j, :], s5_p[:, 0:TOK], start=True, stop=False)
                fin(pe.matmul(out, Cl[1][:, j, :], s5_p[:, TOK:], start=False, stop=True))

            def x_kT():
                pe.wait_ge(S("h_lo"), 2 * KD)
                place_read(pe, "mk0")
                place_read(pe, "mk1")
                for h in range(XH):
                    for t in range(T):
                        last = pe.transpose(big[:, h // 2, (h % 2) * TOK + t * P:(h % 2) * TOK + (t + 1) * P],
                                            k_x[:, t, h * XD:(h + 1) * XD], ident)
                fin(last)

            def x_scores():
                place_read(pe, "xq0")
                place_read(pe, "xq1")
                for t in range(T):
                    for h in range(XH):
                        last = pe.matmul(pb["p3"][:, t * XH + h:t * XH + h + 1], sq_x[:, h, t * P:(t + 1) * P],
                                         ones[:, 0:1], start=True, stop=True)
                fin(last)
                place_read(pe, "kT")
                for t in range(T):
                    for h in range(XH):
                        last = pe.matmul(big[:, 2 * t + h // 2, (h % 2) * TOK:(h % 2 + 1) * TOK],
                                         q_x[:, h, t * P:(t + 1) * P], kt_x[:, h, :], start=True, stop=True)
                fin(last)

            def x_probs():
                pe.wait_ge(S("xp_ready"), 1)
                place_free(pe, "xp")
                for h in range(XH):
                    for kt in range(T):
                        for t in range(T):
                            last = pe.transpose(
                                big[:, 2 * kt + h // 2, (h % 2) * TOK + t * P:(h % 2) * TOK + (t + 1) * P],
                                p_x[:, t * XH + h, kt * P:(kt + 1) * P], ident)
                fin(last)

            def x_out():
                place_read(pe, "mv0")
                place_read(pe, "mv1")
                place_read(pe, "xp")
                for h in range(XH):
                    for kt in range(T):
                        last = pe.matmul(big[:, h // 2, (h % 2) * TOK:(h % 2 + 1) * TOK],
                                         v_x[:, kt, h * XD:(h + 1) * XD],
                                         pT_x[:, kt * 1024 + h * TOK:kt * 1024 + (h + 1) * TOK],
                                         start=kt == 0, stop=kt == 1)
                fin(last)

            def c_sums():
                for name in ("c0", "c1", "c2"):
                    place_read(pe, name)
                place_free(pe, "cs")
                for c, ks in enumerate((range(0, 3), range(3, 5))):
                    for t in range(T):
                        for kk in ks:
                            last = pe.matmul(bigf[:, 2 * c + t:2 * c + t + 1], c_sq[:, kk, t * P:(t + 1) * P],
                                             ones[:, 0:1], start=kk == ks[0], stop=kk == ks[-1])
                fin(last)

            def m_turn(g):
                if g == 0:
                    pe.wait_ge(S("qk_ready"), 1)
                place_free(pe, f"tq{g}")
                for which, src in enumerate((Qh, K_m)):
                    for h in range(4):
                        for t in range(T):
                            at = (h % 2) * TOK + t * P
                            last = pe.transpose(big[0:DQK, 2 * which + h // 2, at:at + P],
                                                src[:, t * H_MLA + 4 * g + h, :], ident)
                fin(last)

            def m_scores(g):
                place_read(pe, f"tq{g}")
                for h in range(4):
                    q, k = QT[0:DQK, h * TOK:(h + 1) * TOK], KT[0:DQK, h * TOK:(h + 1) * TOK]
                    pe.matmul(big[:, h, 0:P], q[:, 0:P], k[:, 0:P], start=True, stop=True)
                    last = pe.matmul(big[:, h, P:3 * P], q[:, P:TOK], k[:, :], start=True, stop=True)
                fin(last)

            def m_probs(g):
                pe.wait_ge(S("mp_ready"), g + 1)
                place_free(pe, f"pt{g}")
                for h in range(4):
                    for c in range(3):
                        last = pe.transpose(big[:, h, c * P:(c + 1) * P], P_m[g][:, h, c * P:(c + 1) * P], ident)
                fin(last)

            def pv_product(out, v0, v1, probs):
                pe.matmul(out, v0, probs[:, 0:TOK], start=True, stop=False)
                return pe.matmul(out[:, P:TOK], v1, probs[:, TOK:3 * P], start=False, stop=True)

            def m_out(g):
                place_read(pe, f"pt{g}")
                place_read(pe, "kv")
                place_free(pe, f"pv{g}")
                for h in range(4):
                    a = (4 * g + h) * DV
                    last = pv_product(pb["p3"][64 * (h % 2):64 * (h % 2) + 64, (h // 2) * TOK:(h // 2 + 1) * TOK],
                                      V_m[:, 0, a:a + DV], V_m[:, 1, a:a + DV], PT[:, h, :])
                fin(last)

            for u in range(U_MIX1):
                names = UNITS1[u]
                if u < 4:
                    tm_half(u, None, ("mk", "mv")[u // 2], u % 2, bk)
                elif u == 10:
                    unit_in(u)
                    place_free(pe, "c2")
                    fm(u, None, bank("c2")[:, 0:TOK], hk, KD, 0)
                    for t in range(T):
                        for kk in range(KD):
                            last = mm3(bank("c2")[:, TOK + t * DROPE:TOK + (t + 1) * DROPE], hk(kk, t * P, P),
                                       w(u, None, D + kk * DROPE, DROPE), kk == 0, kk == KD - 1)
                    fin(last)
                elif u == 12:
                    unit_in(u)
                    place_free(pe, "kv")
                    for part in range(2):
                        for t in range(T):
                            for kk in range(2):
                                last = mm3(big[:, 2 * part + t, :], bk(3 + kk, t * P, P),
                                           w(u, None, kk * D + part * 512, 512), kk == 0, kk == 1)
                    fin(last)
                elif u == 14:
                    unit_in(u)
                    place_free(pe, "qa")
                    for t in range(T):
                        for kk in range(3):
                            last = mm3(big[:, t, :], bk(kk, t * P, P), w(u, None, kk * 512, 512), kk == 0, kk == 2)
                    fin(last)
                elif u == 13:
                    unit_in(u)
                    place_free(pe, "qb")
                    for t in range(T):
                        for kk in range(3):
                            last = mm3(bank("qb")[:, t * TOK:(t + 1) * TOK], bk(kk, t * P, P),
                                       w(u, None, kk * TOK, TOK), kk == 0, kk == 2)
                    fin(last)
                elif names[0][0] == "b":
                    if u == 29:
                        pe.wait_ge(S("s_lo"), 1)
                    if u == 18:
                        pe.wait_ge(S("xo_lo"), 1)
                    if u == 31:
                        place_read(pe, "pv1")
                    branch(u, None, names, bk_from({"c": 4, "s": 4, "m": 0}[names[0][1]]), 4)
                elif u == 27:
                    pe.wait_ge(S("y_lo"), 4)
                    branch(u, None, names, bk, 4)
                elif u == 33:
                    w_out(u, None)
                elif u < 33:
                    fm_unit(u, None, names[0])
                if u == 3:
                    x_kT()
                if u == 6:
                    x_scores()
                if u == 9:
                    x_probs()
                if u == 10:
                    x_out()
                if u == 11:
                    c_sums()
                if u in (24, 26):
                    m_turn((u - 24) // 2)
                if u in (25, 27):
                    m_scores((u - 25) // 2)
                if u == 28:
                    m_probs(0)
                if u == 29:
                    m_out(0)
                    m_probs(1)
                if u == 30:
                    m_out(1)
                if 7 <= u < 7 + ST:
                    s5_in(u - 7)
                if 9 <= u < 9 + ST:
                    s5_out(u - 9)
            norm_T(2)
            ffn(U_MIX1, None, "f0", 2)

            pe.wait_ge(S("c2_in"), 16)
            decay = col2("decay").rearrange("p (h c) -> p h c", h=RH)
            pool_m = col2("pool").rearrange("p (g c) -> p g c", g=4)
            with pe.Fori(0, LAYERS) as l:
                norm_T(l * 3 + 3)
                ffn(0, l, "f1", l * 3 + 3)
                norm_T(l * 3 + 4)

                def head(h):
                    return slice(64 * (h % 2), 64 * (h % 2) + 64), (h // 2) * TOK

                def two_tiles(out, s, m):
                    pe.matmul(out[:, 0:TOK], s[:, 0:P], m[:, 0:TOK], start=True, stop=True)
                    return pe.matmul(out[:, TOK:3 * P], s[:, P:TOK], m[:, P:TOK], start=True, stop=True)

                def sb_scores():
                    place_read(pe, "sbq", l)
                    place_read(pe, "sbk", l)
                    place_free(pe, "z", l)
                    for h in range(SBH):
                        p, c = head(h)
                        last = two_tiles(big[:, h, :], sbk[p, c:c + TOK], sbq[p, c:c + TOK])
                    fin(last)

                def rotate(name, src, needs):
                    place_read(pe, needs, l)
                    place_free(pe, name, l)
                    fin(pe.matmul(pb["p3"][:, :], col2("rot"), src, start=True, stop=True))

                def sb_after():
                    pe.wait_ge(S("lf_ready"), l + 1)
                    place_free(pe, "sa", l)
                    for h in range(SBH):
                        pe.matmul(big[:, h, 0:TOK], col2("after"), C_z[:, h, 0:TOK], start=True, stop=False)
                        pe.matmul(big[:, h, P:TOK], ones, C_z[:, h, TOK:3 * P], start=False, stop=True)
                        last = pe.matmul(big[:, h, TOK:3 * P], col2("after"), C_z[:, h, TOK:3 * P], start=True,
                                         stop=True)
                    fin(last)

                def sb_out():
                    pe.wait_ge(S("w_ready"), l + 1)
                    place_read(pe, "sbv", l)
                    place_free(pe, "pv", l)
                    for h in range(SBH):
                        p, c = head(h)
                        last = pv_product(pb["p3"][p, c:c + TOK], sbv[:, h * 64:h * 64 + 64],
                                          sbv[:, TOK + h * 64:TOK + h * 64 + 64], B_z[:, h, :])
                    fin(last)

                def ret_scores():
                    pe.wait_ge(S("rq_rot"), l + 1)
                    pe.wait_ge(S("rk_rot"), l + 1)
                    place_free(pe, "rs", l)
                    for h in range(RH):
                        p, c = head(h)
                        last = two_tiles(big[:, h, :], rk[p, c:c + TOK], rq[p, c:c + TOK])
                    fin(last)

                def pool_means():
                    place_read(pe, "up", l)
                    place_free(pe, "pl1", l)
                    for g in range(4):
                        p, c = head(g)
                        last = pv_product(pb["p3"][p, c:c + TOK], up[:, g * 64:g * 64 + 64],
                                          up[:, TOK + g * 64:TOK + g * 64 + 64], pool_m[:, g, :])
                    fin(last)

                def pool_mix():
                    place_read(pe, "pl1", l)
                    for c in range(2):
                        last = pe.matmul(pb["p3"][:, c * TOK:(c + 1) * TOK], lcol("w_pool", c * P, P),
                                         rt[:, c * TOK:(c + 1) * TOK], start=True, stop=True)
                    fin(last)

                def ret_out():
                    place_read(pe, "rs", l)
                    place_read(pe, "rv0", l)
                    place_read(pe, "rv1", l)
                    for h in range(RH):
                        o = slice(h * P, (h + 1) * P)
                        pe.matmul(big[:, 0, o], B_z[:, h, 0:P], rv[:, 0, o], start=True, stop=True)
                        pe.matmul(big[:, 1, o], B_z[:, h, P:TOK], rv[:, 0, o], start=True, stop=False)
                        last = pe.matmul(big[:, 1, o], B_z[:, h, TOK:3 * P], rv[:, 1, o], start=False, stop=True)
                    fin(last)

                def ret_turn():
                    pe.wait_ge(S("yn_ready"), l + 1)
                    place_free(pe, "rt", l)
                    for h in range(RH):
                        for t in range(T):
                            last = pe.transpose(big[:, h // 2, (h % 2) * TOK + t * P:(h % 2) * TOK + (t + 1) * P],
                                                y_n[:, t * 512 + h * P:t * 512 + (h + 1) * P], ident)
                    fin(last)

                for u in range(U_MIX2):
                    k, names = U_FFN + u, UNITS2[u]
                    if u in (5, 6):
                        tm_half(k, l, "rv", u - 5)
                    elif u in (8, 9):
                        tm_half(k, l, "rg", u - 8)
                    elif u in (2, 7):
                        tm_unit(k, l, names[0])
                    elif names[0][0] == "b":
                        if u in (14, 19, 24):
                            place_read(pe, {14: "pv", 19: "pl2", 24: "rt"}[u], l)
                        branch(k, l, names, bk_from({"a": 0, "p": 2, "r": 4}[names[0][1]]), 4 if u >= 24 else 2)
                    elif u == 26:
                        w_out(k, l)
                    elif u < 26:
                        fm_unit(k, l, names[0], n=l * 3 + 4 if u == 0 else None)
                    if u == 3:
                        sb_scores()
                    if u == 6:
                        rotate("pq", rq, "rq")
                        sb_after()
                    if u == 8:
                        rotate("pk", rk, "rk")
                    if u == 9:
                        sb_out()
                        ret_scores()
                    if u == 11:
                        ret_out()
                        pool_means()
                    if u == 12:
                        pool_mix()
                    if u == 14:
                        ret_turn()
                norm_T(l * 3 + 5)
                ffn(U_FFN + U_MIX2, l, "f2", l * 3 + 5)

        @block.scalar
        def _(act):
            step = Steps(act, S("act_step"))
            act.dma_start(x[:, :, :], x_d.rearrange("t p d -> p t d")).then_inc(S("x_in"), 16)

            def copy(dst, src, scale=1.0):
                return act.activation(dst, src, ACT.Copy, scale=scale)

            def norm_rows(n, src, ready, v):
                act.wait_ge(S(ready), v)
                act.activation(junk_act, src[:, 1, :], ACT.Square, accum_out=ss[:, 1:2]).then_inc(S("sq_act"), 1)
                act.wait_ge(S("rstd"), n + 1)

            def norm_scale(n, src):
                copy(xs[:, 1, :], src[:, 1, :], rstd[:, 1:2]).then_inc(S("xs_act"), 1)

            def norm_split(n, tag, dst, gain, l=None):
                for k in range(KD):
                    if k % 2 == 0:
                        job_done(act, f"{tag}T{k // 2}", l)
                    copy(dst[:, k, :], big[:, k // 2, (k % 2) * TOK:(k % 2 + 1) * TOK], gain(k)).then_inc(S("h_hi"), 1)

            def evac(name, dst, l=None, scale=1.0, src=None):
                job_done(act, name, l)
                copy(dst, bank(name, l)[:, :] if src is None else src, scale).then_inc(read_sem(name, l), 1)

            def gate(name, first, l=None, bias=None):
                job_done(act, name, l)
                b = bank(name, l)
                if bias is None:
                    act.activation(gates[:, first:first + 2, :], b[:, :].rearrange("p (a t) -> p a t", a=2), ACT.Tanh,
                                   scale=0.5).then_inc(read_sem(name, l), 1)
                    return
                act.activation(gates[:, first, :], b[:, 0:TOK], ACT.Tanh, scale=0.5, bias=hb[:, bias:bias + 1])
                act.activation(gates[:, first + 1, :], b[:, TOK:], ACT.Tanh, scale=0.5, bias=hb[:, bias + 1:bias + 2])\
                   .then_inc(read_sem(name, l), 1)

            def merged_high(j, l=None):
                act.wait_ge(S("merged"), (j + 1) if l is None else l * 4 + (4 + j + 1))
                copy(h_hi[:, 2 * j:2 * j + 2, :], merged[:, 2 * j:2 * j + 2, :]).then_inc(S("m_hi"), 1)

            def ffn_evac(par, done, used):
                act.wait_ge(S("pe_done"), done)
                b = pb[("p0", "p1")[par]]
                wait(act, ("p0", "p1")[par] + "_read", used)
                act.activation(f_s[:, par, :], b[:, 0:TOK], ACT.Silu).then_inc(S("silu"), 1)

            def conv_evac(par, f, done, used):
                act.wait_ge(S("pe_done"), done)
                wait(act, ("p0", "p1")[par] + "_read", used)
                for half in range(2):
                    a = C1["conv_w"][0] + 3 * (half * NF) + 2
                    bb = C1["conv_b"][0] + half * NF
                    ins = act.activation(f_c4[:, par, half, :], pb[("p0", "p1")[par]][:, half * TOK:(half + 1) * TOK],
                                         ACT.Identity, scale=c1[:, bass.ds(f * 3 + a, 1)],
                                         bias=c1[:, bass.ds(f + bb, 1)])
                ins.then_inc(S("conv0"), 1)

            def conv_silu(par, n):
                act.wait_ge(S("conv"), n)
                act.activation(f_s[:, par, :], f_c4[:, par, 0, :], ACT.Silu).then_inc(S("silu"), 1)

            f_c4 = area(GT + 1024, 1024).rearrange("p (a b t) -> p a b t", a=2, b=2)

            def ffn(k0, l, tag, conv=False):
                ua, ub = plan.use(tag + "A0", l), plan.use(tag + "B0", l)

                def up(k, i, par, m=None, i_more=0):
                    split_act(act, k, l, m)
                    done = plan.unit_done(k, l)
                    used = (ua if par == 0 else ub) + i
                    f = 2 * i + par
                    if m is not None:
                        done, used, f = m * 6 + done, m * 2 + used, m * 4 + f
                    if conv:
                        conv_evac(par, f, done, used)
                        conv_silu(par, f + 1)
                    else:
                        ffn_evac(par, done, used)

                def down(k, m=None):
                    split_act(act, k, l, m)

                up(k0, 0, 0)
                up(k0 + 1, 0, 1)
                up(k0 + 2, 1, 0)
                up(k0 + 3, 1, 1)
                down(k0 + 4)
                up(k0 + 5, 2, 0)
                up(k0 + 6, 2, 1)
                down(k0 + 7)
                with act.Fori(0, (NI - 3) // 2) as m:
                    for h in range(2):
                        up(k0 + 8 + 3 * h, 3 + h, 0, m)
                        up(k0 + 9 + 3 * h, 3 + h, 1, m)
                        down(k0 + 10 + 3 * h, m)

            act.wait_ge(S("c1_in"), 16)
            act.activation(dt_, col("log_dt", 0, ST), ACT.Exp).then_inc(S("dt"), 1)
            act.wait_ge(S("s5_a"), 1)
            act.activation(mag, s5_m1[:, 0:ST], ACT.Exp).then_inc(S("mag"), 1)
            act.wait_ge(S("reduced"), 1)
            act.activation(sin48, tri_r, ACT.Sin).then_inc(S("trig"), 1)
            act.activation(cos48, tri_w, ACT.Sin).then_inc(S("trig"), 1)
            norm_rows(0, xs, "mem_in", 16)
            norm_scale(0, xs)
            for r in range(2):
                act.wait_ge(S(f"raw_in{r}"), 16)
                copy(whi[:, r, :], raw[:, r, :]).then_inc(S("hi_done"), 1)
            norm_split(0, "mem", b_hi, lambda k: col("g_mem", k))
            norm_rows(1, x, "x_in", 16)
            job_done(act, "memT3")
            norm_scale(1, x)
            act.wait_ge(S("raw_in2"), 16)
            copy(whi[:, 2, :], raw[:, 2, :]).then_inc(S("hi_done"), 1)
            norm_split(1, "x", h_hi, lambda k: col("g_mix", k))

            for u in range(U_MIX1):
                name = UNITS1[u][0]
                if u < U_MIX1 - 1:
                    split_act(act, u)
                if u == 1:
                    for t in range(T):
                        job_done(act, f"mk{t}")
                        ins = act.activation(sq_x[:, 2 * t:2 * t + 2, :].rearrange("p a t -> p (a t)"),
                                             bank(f"mk{t}")[:, :], ACT.Square)
                    ins.then_inc(S("kx_sq"), 1)
                if u == 3:
                    evac("mv0", v_x[:, 0, :])
                    evac("mv1", v_x[:, 1, :])
                if u == 4:
                    job_done(act, "kT")
                    act.wait_ge(S("gxx"), 1)
                    kt2 = kt_x.rearrange("p (a h) t -> p a (h t)", a=2)
                    copy(kt2[:, 0, :], big[:, 0, :], gxx[:, 0:1])
                    copy(kt2[:, 1, :], big[:, 1, :], gxx[:, 0:1]).then_inc(read_sem("kT"), 1)
                if u in (4, 5):
                    h = 2 * (u - 4)
                    job_done(act, name)
                    b2 = bank(name)[:, :].rearrange("p (a t) -> p a t", a=2)
                    copy(q_x[:, h:h + 2, :], b2)
                    act.activation(sq_x[:, h:h + 2, :], b2, ACT.Square).then_inc(read_sem(name), 1)
                if u in (6, 7):
                    evac(name, u_fm[:, 2 * (u - 6):2 * (u - 6) + 2, :].rearrange("p a t -> p (a t)"))
                if u == 7:
                    job_done(act, "xs")
                    act.wait_ge(S("x_neg"), 1)
                    act.wait_ge(S("E_ready"), 1)
                    for a in range(8):
                        ins = act.activation(p_x[:, a, :], bigf[:, a * TOK:(a + 1) * TOK], ACT.Exp,
                                             scale=xscl[:, a:a + 1], bias=xneg[:, a:a + 1],
                                             accum_out=xsum[:, a:a + 1])
                    ins.then_inc(read_sem("xs"), 1)
                if u in (8, 9, 10):
                    job_done(act, name)
                    for c in range(2 if u < 10 else 1):
                        kk = 2 * (u - 8) + c
                        src = bank(name)[:, c * TOK:(c + 1) * TOK]
                        step(act.activation(c_sq[:, kk, :], src, ACT.Square))
                        g = col("g_qa", kk) if kk < 3 else col("g_kva", kk - 3)
                        copy(b_hi[:, kk, :], src, g).then_inc(S("c_hi"), 1)
                    if u == 10:
                        copy(kr, bank(name)[:, TOK:TOK + 2 * DROPE]).then_inc(S("kr"), 1)
                        job_done(act, "xo")
                        copy(x_y, bigf[:, 0:1024]).then_inc(read_sem("xo"), 1)
                if u == 9:
                    job_done(act, "xp")
                    copy(pT_x[:, 0:1024], bigf[:, 0:1024]).then_inc(S("xpT"), 1)
                if u == 12:
                    act.wait_ge(S("c_rstd"), 1)
                    job_done(act, "kv")
                    for t in range(T):
                        step(copy(K_m[:, t * H_MLA:(t + 1) * H_MLA, 0:DNOPE],
                                  big[:, t, :].rearrange("p (h d) -> p h d", h=H_MLA), rc[:, 2 + t:3 + t]))
                    step(copy(V_m[:, 0, :], big[:, 2, :], rc[:, 2:3]))
                    copy(V_m[:, 1, :], big[:, 3, :], rc[:, 3:4]).then_inc(read_sem("kv"), 1)
                if u == 13:
                    job_done(act, "qb")
                    step(copy(Q_m[:, 512:768], bank("qb")[:, 0:TOK], rc[:, 0:1]))
                    copy(Q_m[:, 768 + 512:1536], bank("qb")[:, TOK:], rc[:, 1:2]).then_inc(read_sem("qb"), 1)
                if u == 14:
                    job_done(act, "qa")
                    step(copy(Q_m[:, 0:512], big[:, 0, :], rc[:, 0:1]))
                    copy(Q_m[:, 768:1280], big[:, 1, :], rc[:, 1:2]).then_inc(read_sem("qa"), 1)
                    place_read(act, "qa")
                    place_read(act, "qb")
                    act.activation(m_sq, Q_m, ACT.Square).then_inc(S("q_sq"), 1)
                if u == 15:
                    act.wait_ge(S("mq_msq"), 1)
                    act.activation(m_sq[:, 0:1024].rearrange("p (a d) -> p a d", a=16), K_m[:, :, 0:DNOPE],
                                   ACT.Square).then_inc(S("k_sq"), 1)
                if name[:2] == "gc":
                    gate(name, 2 * int(name[2]), bias=2 * KD + 2 * int(name[2]))
                if name[:2] == "gs":
                    gate(name, 8 + 2 * (u - 20), bias=KD + 2 * (u - 20))
                if name[:2] == "gm":
                    if u == 24:
                        place_read(act, "bc3")
                    gate(name, 2 * int(name[2]), bias=2 * int(name[2]))
                if u == 16:
                    copy(b_hi[:, 4:8, :].rearrange("p a t -> p (a t)"), x_y).then_inc(S("xo_hi"), 1)
                if u in Y_SLOTS:
                    b = Y_SLOTS.index(u)
                    place_read(act, f"cy{4 * b + 3}")
                    act.activation(y_s[:, b, :], y_s[:, b, :], ACT.Gelu_apprx_tanh).then_inc(S("y_gelu"), 1)
                    act.wait_ge(S("y_gelu"), b + 1)
                    copy(b_hi[:, b, :], y_s[:, b, :]).then_inc(S("y_hi"), 1)
                if u in (24, 26):
                    job_done(act, f"tq{(u - 24) // 2}")
                    job_done(act, "cy15")
                    copy(QT[0:DQK, :], bigf[0:DQK, 0:1024]).then_inc(S("mq_T"), 1)
                if u in (25, 27):
                    g = (u - 25) // 2
                    act.wait_ge(S("m_neg"), g + 1)
                    for t in range(T):
                        for h in range(4):
                            seg = P_m[g][:, h, 0:P] if t == 0 else P_m[g][:, h, P:3 * P]
                            a = t * 4 + h
                            s = t * H_MLA + 4 * g + h
                            ins = act.activation(seg, seg, ACT.Exp, scale=qsc[:, s:s + 1], bias=qng[:, a:a + 1],
                                                 accum_out=qsm[:, a:a + 1])
                    ins.then_inc(S("m_exp"), 1)
                if u == 27:
                    for j in range(2):
                        job_done(act, f"gl{j}")
                        for c in range(2):
                            m = 2 * j + c
                            ins = act.activation(sg_s[:, m, :], bank(f"gl{j}")[:, c * TOK:(c + 1) * TOK], ACT.Sigmoid,
                                                 bias=col("b_glu", m))
                        ins.then_inc(read_sem(f"gl{j}"), 1)
                    act.wait_ge(S("glu"), 1)
                    copy(b_hi[:, 4:8, :], sg_s).then_inc(S("s_hi"), 1)
                if u in (28, 29):
                    job_done(act, f"pt{u - 28}")
                    copy(PT[:, 0:2, :], big[:, 0:2, 0:3 * P]).then_inc(S("mp_T"), 1)
                if u in (29, 30):
                    g = u - 29
                    job_done(act, f"pv{g}")
                    copy(b_hi[:, 2 * g:2 * g + 2, :].rearrange("p a t -> p (a t)"), pb["p3"][:, :]).then_inc(S("pv_hi"), 1)
                if u in (31, 32):
                    merged_high(2 * (u - 31))
                    merged_high(2 * (u - 31) + 1)

            def norm(n, tag, gain, l=None):
                norm_rows(n, x, "x_t1", n - 1)
                norm_scale(n, x)
                norm_split(n, tag, h_hi, gain, l)

            norm(2, "f0", lambda k: col("g_ffn", k))
            split_act(act, U_MIX1 - 1)
            ffn(U_MIX1, None, "f0", conv=True)
            with act.Fori(0, LAYERS) as l:
                step.enter(l, 2)

                def layer_gain(name):
                    return lambda k: lcol(name, k)

                act.wait_ge(S("lc_in"), l * 16 + 16)
                norm(l * 3 + 3, "f1", layer_gain("g_ffn1"), l)
                r, loads, _ = last_split(act, l)
                act.wait_ge(S(f"raw_in{r}"), loads * 16)
                copy(whi[:, r, :], raw[:, r, :]).then_inc(S("hi_done"), 1)
                ffn(0, l, "f1")
                norm(l * 3 + 4, "m", layer_gain("g_mix"), l)
                split_act(act, U_FFN - 1, l)
                for u in range(U_MIX2):
                    k, name = U_FFN + u, UNITS2[u][0]
                    if u < U_MIX2 - 1:
                        split_act(act, k, l)
                    if u == 0:
                        evac(name, sbq, l, scale=64.0 ** -0.5)
                    if u in (1, 2, 3, 4):
                        evac(name, {1: sbk, 2: sbv, 3: rq, 4: rk}[u], l)
                    if u == 4:
                        job_done(act, "z", l)
                        z = big[:, :, 0:3 * P]
                        step(act.activation(A_z, z, ACT.Abs))
                        step(act.activation(A_z, A_z, ACT.Exp, scale=-1.0))
                        act.activation(A_z, A_z, ACT.Ln, bias=1.0).then_inc(S("ln"), 1)
                    if u == 6:
                        evac("rv0", rv[:, 0, :], l)
                        evac("rv1", rv[:, 1, :], l)
                    if u == 7:
                        evac("up", up, l)
                        place_read(act, "sa", l)
                        act.activation(B_z, B_z, ACT.Exp).then_inc(S("w_exp"), 1)
                    if u == 9:
                        for t in range(T):
                            job_done(act, f"rg{t}", l)
                            act.activation(rg[:, t * 512:(t + 1) * 512], bank(f"rg{t}", l)[:, :], ACT.Silu)\
                               .then_inc(read_sem(f"rg{t}", l), 1)
                    if u == 10:
                        job_done(act, "pv", l)
                        copy(b_hi[:, 0:2, :].rearrange("p a t -> p (a t)"), pb["p3"][:, :]).then_inc(S("pv_hi"), 1)
                    if u == 11:
                        evac("pl1", rt, l, src=pb["p3"][:, :])
                    if u == 12:
                        job_done(act, "ry", l)
                        act.activation(y_sq, bigf[:, 0:1024], ACT.Square).then_inc(S("y_sq"), 1)
                    if u == 13:
                        job_done(act, "pl2", l)
                        for c in range(2):
                            ins = copy(b_hi[:, 2 + c, :], pb["p3"][:, c * TOK:(c + 1) * TOK], lcol("pool_scale", c))
                        ins.then_inc(S("pl_hi"), 1)
                    if u == 15:
                        job_done(act, "rt", l)
                        copy(b_hi[:, 4:8, :].rearrange("p a t -> p (a t)"), bigf[:, 0:1024]).then_inc(S("rt_hi"), 1)
                    if name[0] == "g":
                        if u == 20:
                            place_read(act, "ba3", l)
                        gate(name, {"a": 0, "p": 8, "r": 0}[name[1]] + 2 * int(name[2]), l)
                    if u in (24, 25):
                        merged_high(2 * (u - 24), l)
                        merged_high(2 * (u - 24) + 1, l)
                norm(l * 3 + 5, "f2", layer_gain("g_ffn2"), l)
                split_act(act, U_FFN + U_MIX2 - 1, l)
                ffn(U_FFN + U_MIX2, l, "f2")
                step.leave(LAYERS)
            norm_rows(3 + 3 * LAYERS, x, "x_t1", 2 + 3 * LAYERS)

        @block.vector
        def _(dve):
            step = Steps(dve, S("dve_step"))
            f_c4 = area(GT + 1024, 1024).rearrange("p (a b t) -> p a b t", a=2, b=2)

            def tt(out, a, b, op):
                return dve.tensor_tensor(out, a, b, op)

            def ts(out, a, s1, op0, s2=None, op1=None):
                if op1 is None:
                    return dve.tensor_scalar(out, a, s1, None, op0)
                return dve.tensor_scalar(out, a, s1, s2, op0, op1)

            def stt(out, a, s, b, op0, op1):
                return dve.scalar_tensor_tensor(out=out, in0=a, scalar=s, in1=b, op0=op0, op1=op1)

            def low(dst, src, high):
                return tt(dst, src, high.bitcast(F32), ALU.subtract)

            def norm_rows(n, src):
                step(dve.tensor_tensor_reduce(out=junk_dve, in0=src[:, 0, :], in1=src[:, 0, :], scale=1.0, scalar=0.0,
                                              op0=ALU.mult, op1=ALU.add, accum_out=ss[:, 0:1]))
                dve.wait_ge(S("sq_act"), n + 1)
                ts(msq, ss, 1.0 / D, ALU.mult, EPS, ALU.add).then_inc(S("msq"), 1)
                dve.wait_ge(S("rstd"), n + 1)

            def norm_scale(n, src):
                ts(xs[:, 0, :], src[:, 0, :], rstd[:, 0:1], ALU.mult).then_inc(S("xs_dve"), 1)

            def norm_split(n, dst, high, gain):
                for k in range(KD):
                    dve.wait_ge(S("h_hi"), n * KD + (k // 2 * 2 + 2))
                    stt(dst[:, k, :], big[:, k // 2, (k % 2) * TOK:(k % 2 + 1) * TOK], gain(k),
                        high[:, k, :].bitcast(F32), ALU.mult, ALU.subtract).then_inc(S("h_lo"), 1)

            def norm(n, gain):
                norm_rows(n, x)
                norm_scale(n, x)
                norm_split(n, h_lo, h_hi, gain)

            def add_x(name, scale, l=None):
                job_done(dve, name, l)
                for t in (1, 0):
                    for nh in range(2):
                        xx = x[:, t, nh * 512:(nh + 1) * 512]
                        ins = stt(xx, big[:, 2 * t + nh, :], scale, xx, ALU.mult, ALU.add)
                        if nh == 0:
                            step(ins)
                    ins.then_inc(S("x_t1") if t == 1 else read_sem(name, l), 1)
                place_read(dve, name, l)

            def gated(name, first, j, tmp, start, last, l=None):
                job_done(dve, name, l)
                g = gates[:, first + 2 * j:first + 2 * j + 2, :].rearrange("p a t -> p (a t)")
                acc = merged[:, 2 * j:2 * j + 2, :].rearrange("p a t -> p (a t)")
                dst = acc if start else tmp
                stt(dst, g, 1.0, bank(name, l)[:, :], ALU.add, ALU.mult).then_inc(read_sem(name, l), 1)
                place_read(dve, name, l)
                if start:
                    return
                ins = tt(acc, acc, tmp, ALU.add)
                if last:
                    ins.then_inc(S("merged"), 1)
                    dve.wait_ge(S("merged"), (j + 1) if l is None else l * 4 + (4 + j + 1))
                else:
                    step(ins)

            def merged_low(j, l=None):
                dve.wait_ge(S("m_hi"), (j + 1) if l is None else l * 4 + (4 + j + 1))
                low(h_lo[:, 2 * j:2 * j + 2, :], merged[:, 2 * j:2 * j + 2, :], h_hi[:, 2 * j:2 * j + 2, :])\
                    .then_inc(S("m_lo"), 1)

            def ffn(k0, l, tag, scale, conv=False):
                ua, ub = plan.use(tag + "A0", l), plan.use(tag + "B0", l)
                s0 = 0 if l is None else (l * (4 * NI) + (2 * NI if tag == "f1" else 4 * NI))

                def up(k, i, par, m=None):
                    split_dve(dve, k, l, m)
                    n = 2 * i + par + 1
                    f = 2 * i + par
                    if m is not None:
                        n, f = m * 4 + n, m * 4 + f
                    b = pb[("p0", "p1")[par]]
                    g, tile = f_g[:, par, :], 2 * (i % 2) + par
                    if conv:
                        dve.wait_ge(S("conv0"), n)
                        for half in range(2):
                            for tap in (1, 0):
                                back = 2 - tap
                                a = C1["conv_w"][0] + 3 * half * NF + tap
                                y = f_c4[:, par, half, back:]
                                ins = stt(y, b[:, half * TOK:(half + 1) * TOK - back], c1[:, bass.ds(f * 3 + a, 1)], y,
                                          ALU.mult, ALU.add)
                                if half == 0 and tap == 0:
                                    ins.then_inc(S("conv"), 1)
                                    dve.wait_ge(S("conv"), n)
                                else:
                                    step(ins)
                        dve.wait_ge(S("silu"), s0 + n)
                        step(tt(g, f_s[:, par, :], f_c4[:, par, 1, :], ALU.mult))
                    else:
                        dve.wait_ge(S("silu"), s0 + n)
                        step(stt(g, f_s[:, par, :], scale, b[:, TOK:], ALU.mult, ALU.mult))
                    step(dve.tensor_copy(b_hi[:, tile, :], g))
                    low(b_lo[:, tile, :], g, b_hi[:, tile, :]).then_inc(S(("p0", "p1")[par] + "_read"), 1)

                def down(k, m=None):
                    split_dve(dve, k, l, m)

                up(k0, 0, 0)
                up(k0 + 1, 0, 1)
                up(k0 + 2, 1, 0)
                up(k0 + 3, 1, 1)
                down(k0 + 4)
                up(k0 + 5, 2, 0)
                up(k0 + 6, 2, 1)
                down(k0 + 7)
                with dve.Fori(0, (NI - 3) // 2) as m:
                    step.enter(m, 4 * 5 if conv else 4 * 2)
                    for h in range(2):
                        up(k0 + 8 + 3 * h, 3 + h, 0, m)
                        up(k0 + 9 + 3 * h, 3 + h, 1, m)
                        down(k0 + 10 + 3 * h, m)
                    step.leave((NI - 3) // 2)

            dve.wait_ge(S("c1_in"), 16)
            step(ts(hb, col("b_gate", 0, 3 * KD), 0.5, ALU.mult))
            step(tt(gqk, col("gq_nope"), col("gk_nope"), ALU.mult))
            tt(gxx, col("g_xq"), col("g_xk"), ALU.mult).then_inc(S("gxx"), 1)
            dve.wait_ge(S("pos_in"), 16)
            step(dve.tensor_copy(posf, pos[:, :]))
            step(tt(ang[:, ST:].rearrange("p (t f) -> p t f", t=T),
                    col("inv_freq", 0, DROPE // 2).unsqueeze(1).to_broadcast([P, T, DROPE // 2]),
                    posf.unsqueeze(2).to_broadcast([P, T, DROPE // 2]), ALU.mult))
            dve.wait_ge(S("dt"), 1)
            step(tt(theta, col("lam_im", 0, ST), dt_, ALU.mult))
            tt(s5_m1[:, 0:ST], col("lam_re", 0, ST), dt_, ALU.mult).then_inc(S("s5_a"), 1)
            step(ts(tri_k, ang, 1.0 / TWO_PI, ALU.mult))
            step(ts(tri_k, tri_k, MAGIC, ALU.add))
            step(ts(tri_k, tri_k, MAGIC, ALU.subtract))
            step(stt(tri_r, tri_k, -CW[0], ang, ALU.mult, ALU.add))
            step(stt(tri_r, tri_k, -CW[1], tri_r, ALU.mult, ALU.add))
            step(stt(tri_r, tri_k, -CW[2], tri_r, ALU.mult, ALU.add))
            step(ts(tri_w, tri_r, float(np.float32(np.pi / 2)), ALU.add))
            step(ts(tri_m, tri_w, float(np.float32(np.pi)), ALU.is_gt, -float(np.float32(TWO_PI)), ALU.mult))
            step(tt(tri_w, tri_w, tri_m, ALU.add))
            step(ts(tri_w, tri_w, PI_LOW, ALU.min, -PI_LOW, ALU.max))
            ts(tri_r, tri_r, PI_LOW, ALU.min, -PI_LOW, ALU.max).then_inc(S("reduced"), 1)
            dve.wait_ge(S("trig"), 2)
            dve.wait_ge(S("mag"), 1)
            lr, li = col("lam_re", 0, ST), col("lam_im", 0, ST)
            step(tt(tA, mag, cos48[:, 0:ST], ALU.mult))
            step(ts(tA, tA, 1.0, ALU.subtract))
            step(tt(tB, mag, sin48[:, 0:ST], ALU.mult))
            step(tt(tC, lr, lr, ALU.mult))
            step(tt(tD, li, li, ALU.mult))
            step(tt(tC, tC, tD, ALU.add))
            step(dve.reciprocal(tC, tC))
            for dst, (a, b), op in ((f_re, (tA, tB), ALU.add), (f_im, (tB, tA), ALU.subtract)):
                step(tt(dst, a, lr, ALU.mult))
                step(tt(tD, b, li, ALU.mult))
                step(tt(dst, dst, tD, op))
                step(tt(dst, dst, tC, ALU.mult))
            dve.wait_ge(S("bc_in"), 16)
            dve.wait_ge(S("bd_zero"), 1)
            br, bi, cr, ci = (bcr[:, a] for a in range(4))
            fr3, fi3 = (f.unsqueeze(2).to_broadcast([P, ST, GCH]) for f in (f_re, f_im))
            for out, (a, b), op in ((0, (fr3, fi3), ALU.subtract), (1, (fi3, fr3), ALU.add)):
                step(tt(btmp[:, 0], br, a, ALU.mult))
                step(tt(btmp[:, 1], bi, b, ALU.mult))
                for g in range(2):
                    s = slice(64 * g, 64 * g + 64)
                    ins = tt(bbd[s, out, :, GCH * g:GCH * (g + 1)], btmp[s, 0], btmp[s, 1], op)
                    if out == 1 and g == 1:
                        ins.then_inc(S("bbd"), 1)
                        dve.wait_ge(S("bbd"), 1)
                    else:
                        step(ins)
            for g in range(2):
                s = slice(64 * g, 64 * g + 64)
                step(dve.tensor_copy(Cl[0][s, :, GCH * g:GCH * (g + 1)], cr[s]))
                step(ts(Cl[1][s, :, GCH * g:GCH * (g + 1)], ci[s], -1.0, ALU.mult))
            job_done(dve, "bT")
            step(dve.tensor_copy(s5c[:, 0:512], big[:, 0, :]))
            dve.tensor_copy(s5c[:, 512:1024], big[:, 1, :]).then_inc(read_sem("bT"), 1)
            place_read(dve, "bT")

            dve.wait_ge(S("mem_in"), 16)
            norm_rows(0, xs)
            norm_scale(0, xs)
            for r in range(2):
                dve.wait_ge(S("hi_done"), r + 1)
                low(wlo[:, r, :], raw[:, r, :], whi[:, r, :]).then_inc(S("lo_done"), 1)
            norm_split(0, b_lo, b_hi, lambda k: col("g_mem", k))
            dve.wait_ge(S("x_in"), 16)
            norm_rows(1, x)
            job_done(dve, "memT3")
            norm_scale(1, x)
            dve.wait_ge(S("hi_done"), 3)
            low(wlo[:, 2, :], raw[:, 2, :], whi[:, 2, :]).then_inc(S("lo_done"), 1)
            norm_split(1, h_lo, h_hi, lambda k: col("g_mix", k))

            def s5_scan(j):
                job_done(dve, f"bu{j}")
                if j == 0:
                    dve.wait_ge(S("E_ready"), 1)
                src = pb["p3"][:, :].rearrange("p (a t) -> p a t", a=4)
                ec, es = (a[:, j, :].unsqueeze(1).to_broadcast([P, 4, P]) for a in (E_c, E_s))
                step(tt(s5_m1.rearrange("p (a t) -> p a t", a=4), src, ec, ALU.mult))
                tt(s5_m2.rearrange("p (a t) -> p a t", a=4), src, es, ALU.mult).then_inc(S("p3_read"), 1)
                place_read(dve, f"bu{j}")
                step(tt(s5_m1[:, 0:TOK], s5_m1[:, 0:TOK], s5_m2[:, TOK:], ALU.add))
                step(tt(s5_m1[:, TOK:], s5_m1[:, TOK:], s5_m2[:, 0:TOK], ALU.subtract))
                if j >= 2:
                    dve.wait_ge(S("s_ready"), j - 1)
                z, d = s5_z[j % 2], mag[:, j:j + 1].to_broadcast([P, P])
                for a in range(2):
                    step(dve.tensor_tensor_scan(z[:, a * TOK:a * TOK + P], d, s5_m1[:, a * TOK:a * TOK + P], 0.0,
                                                ALU.mult, ALU.add))
                zr, zi = z[:, P - 1:P], z[:, TOK + P - 1:TOK + P]
                er, ei, en = pw[0][0][:, j:j + 1], pw[0][1][:, j:j + 1], e128n[:, j:j + 1]
                step(ts(ini[:, 0:1], zr, er, ALU.mult))
                step(ts(ini[:, 1:2], zi, er, ALU.mult))
                step(stt(ini[:, 0:1], zi, en, ini[:, 0:1], ALU.mult, ALU.add))
                step(stt(ini[:, 1:2], zr, ei, ini[:, 1:2], ALU.mult, ALU.add))
                step(dve.tensor_tensor_scan(z[:, P:TOK], d, s5_m1[:, P:TOK], ini[:, 0:1], ALU.mult, ALU.add))
                dve.tensor_tensor_scan(z[:, TOK + P:], d, s5_m1[:, TOK + P:], ini[:, 1:2], ALU.mult, ALU.add)\
                   .then_inc(S("z_ready"), 1)
                dve.wait_ge(S("z_ready"), j + 1)

            heads = "p (t h) d -> p t h d"

            def mla_prepare_q():
                dve.wait_ge(S("q_sq"), 1)
                step(dve.tensor_reduce(mq, m_sq.rearrange("p (a d) -> p a d", a=16), AX.X, ALU.add))
                ts(mq, mq, 1.0 / DQK, ALU.mult, EPS, ALU.add).then_inc(S("mq_msq"), 1)

            def rope(out, src, n):
                c, s = (a.rearrange("p (t f) -> p t f", t=T).unsqueeze(2).to_broadcast([P, T, n, 16])
                        for a in (rope_c, rope_s))
                x1, x2 = src[:, :, :, 0:16], src[:, :, :, 16:32]
                tmp = [(a[:, 0:T * n * 16]).rearrange("p (t h f) -> p t h f", t=T, h=n) for a in m_t]
                step(tt(tmp[0], x1, c, ALU.mult))
                step(tt(tmp[1], x2, s, ALU.mult))
                step(tt(tmp[2], x1, s, ALU.mult))
                step(tt(tmp[3], x2, c, ALU.mult))
                step(tt(out[:, :, :, 0:16], tmp[0], tmp[1], ALU.subtract))
                step(tt(out[:, :, :, 16:32], tmp[2], tmp[3], ALU.add))

            def mla_prepare_k():
                dve.wait_ge(S("k_sq"), 1)
                dve.wait_ge(S("kr"), 1)
                step(dve.tensor_reduce(mk, m_sq[:, 0:1024].rearrange("p (a d) -> p a d", a=16), AX.X, ALU.add))
                step(tt(krg, kr, kr, ALU.mult))
                step(dve.tensor_reduce(mkr, krg.rearrange("p (t d) -> p t d", t=T), AX.X, ALU.add))
                mk2 = mk.rearrange("p (t h) -> p t h", t=T)
                step(tt(mk2, mk2, mkr.unsqueeze(2).to_broadcast([P, T, H_MLA]), ALU.add))
                ts(mk, mk, 1.0 / DQK, ALU.mult, EPS, ALU.add).then_inc(S("mk_msq"), 1)
                gq3 = col("gq_rope", 0, DROPE).unsqueeze(1).to_broadcast([P, 16, DROPE])
                step(tt(Qh[:, :, DNOPE:], Qh[:, :, DNOPE:], gq3, ALU.mult))
                q4 = Qh[:, :, DNOPE:].rearrange(heads, t=T)
                rope(q4, q4, H_MLA)
                gk3 = col("gk_rope", 0, DROPE).unsqueeze(1).to_broadcast([P, T, DROPE])
                step(tt(krg.rearrange("p (t d) -> p t d", t=T), kr.rearrange("p (t d) -> p t d", t=T), gk3, ALU.mult))
                rope(kro.rearrange("p (t h d) -> p t h d", t=T, h=1), krg.rearrange("p (t h d) -> p t h d", t=T, h=1), 1)

            def mla_scale_k():
                dve.wait_ge(S("mk_rstd"), 1)
                dve.wait_ge(S("mq_rstd"), 1)
                rk3 = rk_.rearrange("p (t h) -> p t h", t=T).unsqueeze(3)
                step(tt(K_m[:, :, DNOPE:].rearrange(heads, t=T),
                        kro.rearrange("p (t d) -> p t d", t=T).unsqueeze(2).to_broadcast([P, T, H_MLA, DROPE]),
                        rk3.to_broadcast([P, T, H_MLA, DROPE]), ALU.mult))
                step(tt(K_m[:, :, 0:DNOPE], K_m[:, :, 0:DNOPE], rk_.unsqueeze(2).to_broadcast([P, 16, DNOPE]), ALU.mult))
                ts(qsc, rq_, float(DQK) ** -0.5, ALU.mult).then_inc(S("qk_ready"), 1)
                dve.wait_ge(S("qk_ready"), 1)

            causal4 = causal.unsqueeze(1).to_broadcast([P, 4, 3 * P])

            def mla_mask(g):
                job_done(dve, f"sc{g}")
                tt(P_m[g], big[:, :, 0:3 * P], causal4, ALU.add).then_inc(read_sem(f"sc{g}"), 1)
                place_read(dve, f"sc{g}")
                step(dve.tensor_reduce(qmx[:, 0:4], P_m[g][:, :, 0:P], AX.X, ALU.max))
                step(dve.tensor_reduce(qmx[:, 4:8], P_m[g][:, :, P:], AX.X, ALU.max))
                v = "p (t h) -> p t h"
                stt(qng.rearrange(v, t=T), qmx.rearrange(v, t=T), -1.0,
                    qsc.rearrange(v, t=T)[:, :, 4 * g:4 * g + 4], ALU.mult, ALU.mult).then_inc(S("m_neg"), 1)

            def mla_weights(g):
                dve.wait_ge(S("m_exp"), g + 1)
                step(dve.reciprocal(qrc, qsm))
                step(tt(P_m[g][:, :, 0:P], P_m[g][:, :, 0:P], qrc[:, 0:4].unsqueeze(2).to_broadcast([P, 4, P]), ALU.mult))
                tt(P_m[g][:, :, P:], P_m[g][:, :, P:], qrc[:, 4:8].unsqueeze(2).to_broadcast([P, 4, TOK]), ALU.mult)\
                    .then_inc(S("mp_ready"), 1)
                dve.wait_ge(S("mp_ready"), g + 1)

            def branch_evac(u, i):
                name = UNITS1[u][i]
                kind = name[1]
                gated(name, 8 if kind == "s" else 0, int(name[2]), area(XS, 512), kind == "c", kind == "m")

            for u in range(U_MIX1):
                name = UNITS1[u][0]
                if u in (13, 17, 21, 25):
                    b = (u - 13) // 4
                    job_done(dve, f"cy{4 * b + 3}")
                    stt(y_s[:, b, :], u_fm[:, b, :], col("ssm_d", b), pb["p2"][:, (b % 2) * TOK:(b % 2 + 1) * TOK],
                        ALU.mult, ALU.add).then_inc(read_sem(f"cy{4 * b + 3}"), 1)
                if u == 11:
                    job_done(dve, "cs")
                    step(ts(msc[:, 0:2], bigf[:, 0:2], 1.0 / Q_LORA, ALU.mult, EPS, ALU.add))
                    ts(msc[:, 2:4], bigf[:, 2:4], 1.0 / KV_LORA, ALU.mult, EPS, ALU.add)\
                        .then_inc(read_sem("cs"), 1)
                if name[0] == "b":
                    branch_evac(u, 1)
                if u < U_MIX1 - 1:
                    split_dve(dve, u)
                if u == 1:
                    dve.wait_ge(S("kx_sq"), 1)
                    step(dve.tensor_reduce(ssk, sq_x.rearrange("p a t -> p (a t)").rearrange("p (a d) -> p a d", a=8),
                                           AX.X, ALU.add))
                    ts(ssk, ssk, 1.0 / XD, ALU.mult, EPS, ALU.add).then_inc(S("kx_msq"), 1)
                    dve.wait_ge(S("kx_rstd"), 1)
                    for t in range(T):
                        tt(k_x[:, t, :].rearrange("p (h d) -> p h d", h=XH),
                           bank(f"mk{t}")[:, :].rearrange("p (h d) -> p h d", h=XH),
                           rsk[:, t * XH:(t + 1) * XH].unsqueeze(2).to_broadcast([P, XH, XD]), ALU.mult)\
                            .then_inc(read_sem(f"mk{t}"), 1)
                if u == 6:
                    job_done(dve, "ssq")
                    ts(msx, pb["p3"][:, 0:8], 1.0 / XD, ALU.mult, EPS, ALU.add).then_inc(read_sem("ssq"), 1)
                if u == 7:
                    job_done(dve, "xs")
                    step(dve.tensor_reduce(xmax, bigf.rearrange("p (a t) -> p a t", a=8), AX.X, ALU.max))
                    dve.wait_ge(S("xq_rstd"), 1)
                    step(ts(xscl, rsq, float(XD) ** -0.5, ALU.mult))
                    stt(xneg, xmax, -1.0, xscl, ALU.mult, ALU.mult).then_inc(S("x_neg"), 1)
                if u == 8:
                    place_read(dve, "xs")
                    step(dve.reciprocal(xrec, xsum))
                    tt(p_x, p_x, xrec.unsqueeze(2).to_broadcast([P, 8, TOK]), ALU.mult).then_inc(S("xp_ready"), 1)
                if u in (8, 9, 10):
                    for c in range(2 if u < 10 else 1):
                        kk = 2 * (u - 8) + c
                        dve.wait_ge(S("c_hi"), min(2 * (u - 8) + 2, 5))
                        g = col("g_qa", kk) if kk < 3 else col("g_kva", kk - 3)
                        if u == 10:
                            dve.wait_ge(S("kr"), 1)
                        ins = stt(b_lo[:, kk, :], bank(name)[:, c * TOK:(c + 1) * TOK], g, b_hi[:, kk, :].bitcast(F32),
                                  ALU.mult, ALU.subtract)
                    ins.then_inc(read_sem(name), 1)
                if u == 9:
                    dve.wait_ge(S("xpT"), 1)
                    dve.tensor_copy(pT_x[:, 1024:], bigf[:, 1024:]).then_inc(read_sem("xp"), 1)
                if u == 16:
                    dve.wait_ge(S("xo_hi"), 1)
                    low(b_lo[:, 4:8, :].rearrange("p a t -> p (a t)"), x_y,
                        b_hi[:, 4:8, :].rearrange("p a t -> p (a t)")).then_inc(S("xo_lo"), 1)
                if 7 <= u < 7 + ST:
                    s5_scan(u - 7)
                if u == 14:
                    mla_prepare_q()
                if u == 15:
                    mla_prepare_k()
                if u == 18:
                    mla_scale_k()
                if u in Y_SLOTS:
                    b = Y_SLOTS.index(u)
                    dve.wait_ge(S("y_hi"), b + 1)
                    low(b_lo[:, b, :], y_s[:, b, :], b_hi[:, b, :]).then_inc(S("y_lo"), 1)
                if u in (24, 26):
                    g = (u - 24) // 2
                    dve.wait_ge(S("mq_T"), g + 1)
                    ts(KT[0:DQK, :], bigf[0:DQK, 1024:], gqk[0:DQK, :], ALU.mult).then_inc(read_sem(f"tq{g}"), 1)
                if u in (25, 27):
                    mla_mask((u - 25) // 2)
                if u in (26, 28):
                    mla_weights((u - 26) // 2)
                if u == 27:
                    for j in range(2):
                        place_read(dve, f"gl{j}")
                        a = sg_s[:, 2 * j:2 * j + 2, :]
                        ins = tt(a, a, y_s[:, 2 * j:2 * j + 2, :], ALU.mult)
                        if j == 0:
                            step(ins)
                    ins.then_inc(S("glu"), 1)
                    dve.wait_ge(S("s_hi"), 1)
                    low(b_lo[:, 4:8, :], sg_s, b_hi[:, 4:8, :]).then_inc(S("s_lo"), 1)
                if u in (28, 29):
                    dve.wait_ge(S("mp_T"), u - 27)
                    dve.tensor_copy(PT[:, 2:4, :], big[:, 2:4, 0:3 * P]).then_inc(read_sem(f"pt{u - 28}"), 1)
                if u in (29, 30):
                    g = u - 29
                    dve.wait_ge(S("pv_hi"), g + 1)
                    low(b_lo[:, 2 * g:2 * g + 2, :].rearrange("p a t -> p (a t)"), pb["p3"][:, :],
                        b_hi[:, 2 * g:2 * g + 2, :].rearrange("p a t -> p (a t)")).then_inc(read_sem(f"pv{g}"), 1)
                if u in (31, 32):
                    merged_low(2 * (u - 31))
                    merged_low(2 * (u - 31) + 1)
                if u < U_MIX1 - 1 and UNITS1[u + 1][0][0] == "b":
                    branch_evac(u + 1, 0)
            add_x("wo", 0.5)
            norm(2, lambda k: col("g_ffn", k))
            split_dve(dve, U_MIX1 - 1)
            ffn(U_MIX1, None, "f0", 1.0, conv=True)
            add_x(f"f0D{NI - 1}", 1.0)

            decay = col2("decay").rearrange("p (h c) -> p h c", h=RH)
            strict4 = col2("strict").unsqueeze(1).to_broadcast([P, 4, 3 * P])
            with dve.Fori(0, LAYERS) as l:
                step.enter(l, DVE_LAYER_STEPS)
                norm(l * 3 + 3, lambda k: lcol("g_ffn1", k))
                r, _, units = last_split(dve, l)
                dve.wait_ge(S("hi_done"), units)
                low(wlo[:, r, :], raw[:, r, :], whi[:, r, :]).then_inc(S("lo_done"), 1)
                ffn(0, l, "f1", 0.5)
                add_x(f"f1D{NI - 1}", 1.0, l)
                norm(l * 3 + 4, lambda k: lcol("g_mix", k))
                split_dve(dve, U_FFN - 1, l)

                def rotated(name, src, ready):
                    job_done(dve, name, l)
                    c, s = (col2(n).unsqueeze(1).to_broadcast([P, 2, TOK]) for n in ("cos", "sin"))
                    v = "p (a t) -> p a t"
                    tt(rt.rearrange(v, a=2), pb["p3"][:, :].rearrange(v, a=2), s, ALU.mult)\
                        .then_inc(read_sem(name, l), 1)
                    place_read(dve, name, l)
                    step(tt(src.rearrange(v, a=2), src.rearrange(v, a=2), c, ALU.mult))
                    tt(src, src, rt, ALU.add).then_inc(S(ready), 1)
                    dve.wait_ge(S(ready), l + 1)

                def branch_evac(names):
                    for name in names:
                        kind = name[1]
                        gated(name, 8 if kind == "p" else 0, int(name[2]), area(XS + 1536, 512), kind == "a",
                              kind == "r", l)

                for u in range(U_MIX2):
                    k, name = U_FFN + u, UNITS2[u][0]
                    if name[0] == "b":
                        branch_evac(UNITS2[u][-1:])
                    if u < U_MIX2 - 1:
                        split_dve(dve, k, l)
                    if u == 5:
                        dve.wait_ge(S("ln"), l + 1)
                        z = big[:, :, 0:3 * P]
                        step(stt(B_z, z, 0.0, A_z, ALU.min, ALU.subtract))
                        tt(C_z, B_z, z, ALU.subtract).then_inc(read_sem("z", l), 1)
                        place_read(dve, "z", l)
                        tt(C_z, C_z, strict4, ALU.mult).then_inc(S("lf_ready"), 1)
                    if u == 7:
                        rotated("pq", rq, "rq_rot")
                        job_done(dve, "sa", l)
                        tt(B_z, B_z, big[:, :, 0:3 * P], ALU.add).then_inc(read_sem("sa", l), 1)
                        place_read(dve, "sa", l)
                    if u == 8:
                        dve.wait_ge(S("w_exp"), l + 1)
                        tt(B_z, B_z, strict4, ALU.mult).then_inc(S("w_ready"), 1)
                        rotated("pk", rk, "rk_rot")
                    if u == 10:
                        dve.wait_ge(S("pv_hi"), l + 3)
                        low(b_lo[:, 0:2, :].rearrange("p a t -> p (a t)"), pb["p3"][:, :],
                            b_hi[:, 0:2, :].rearrange("p a t -> p (a t)")).then_inc(read_sem("pv", l), 1)
                        job_done(dve, "rs", l)
                        tt(B_z, big[:, :, 0:3 * P], decay, ALU.mult).then_inc(read_sem("rs", l), 1)
                    if u == 12:
                        dve.wait_ge(S("y_sq"), l + 1)
                        step(dve.tensor_reduce(rms8, y_sq.rearrange("p (a e) -> p a e", a=8), AX.X, ALU.add))
                        ts(rms8, rms8, 1.0 / P, ALU.mult, EPS, ALU.add).then_inc(S("y_msq"), 1)
                    if u == 13:
                        dve.wait_ge(S("y_rstd"), l + 1)
                        v = "p (a e) -> p a e"
                        tt(y_n.rearrange(v, a=8), bigf[:, 0:1024].rearrange(v, a=8),
                           rr8.unsqueeze(2).to_broadcast([P, 8, P]), ALU.mult).then_inc(read_sem("ry", l), 1)
                        place_read(dve, "ry", l)
                        place_read(dve, "rg0", l)
                        place_read(dve, "rg1", l)
                        tt(y_n, y_n, rg, ALU.mult).then_inc(S("yn_ready"), 1)
                        dve.wait_ge(S("pl_hi"), l + 1)
                        for c in range(2):
                            ins = stt(b_lo[:, 2 + c, :], pb["p3"][:, c * TOK:(c + 1) * TOK], lcol("pool_scale", c),
                                      b_hi[:, 2 + c, :].bitcast(F32), ALU.mult, ALU.subtract)
                        ins.then_inc(read_sem("pl2", l), 1)
                    if u == 15:
                        dve.wait_ge(S("rt_hi"), l + 1)
                        low(b_lo[:, 4:8, :].rearrange("p a t -> p (a t)"), bigf[:, 0:1024],
                            b_hi[:, 4:8, :].rearrange("p a t -> p (a t)")).then_inc(read_sem("rt", l), 1)
                    if u in (24, 25):
                        merged_low(2 * (u - 24), l)
                        merged_low(2 * (u - 24) + 1, l)
                    if u < U_MIX2 - 1 and UNITS2[u + 1][0][0] == "b":
                        branch_evac(UNITS2[u + 1][0:-1])
                add_x("wo", 0.5, l)
                norm(l * 3 + 5, lambda k: lcol("g_ffn2", k))
                split_dve(dve, U_FFN + U_MIX2 - 1, l)
                ffn(U_FFN + U_MIX2, l, "f2", 0.5)
                add_x(f"f2D{NI - 1}", 1.0, l)
                step.leave(LAYERS)
            norm_rows(3 + 3 * LAYERS, x)
            dve.wait_ge(S("gfin_in"), 16)
            for t in range(T):
                stt(xs[:, t, :], x[:, t, :], rstd[:, t:t + 1], area(R, D), ALU.mult, ALU.mult).then_inc(S("out_ready"), 1)


def _units(v):
    def fm(wt, ks, ms):
        return [wt[k * P:(k + 1) * P, m * P:(m + 1) * P] for m in ms for k in ks]

    def tm(wt, ks, n0, n):
        return [wt[k * P:(k + 1) * P, n0:n0 + n] for k in ks]

    out = []

    def unit(parts):
        w = sum(p.shape[1] for p in parts)
        if w < UW:
            parts = parts + [np.zeros((P, UW - w), np.float32)]
        out.append(np.concatenate(parts, axis=1))

    K8 = range(KD)

    def fm_units(wt, c0, n):
        ww = wt[:, c0:c0 + n]
        for m in range(0, n // P, 2):
            unit(fm(ww, K8, (m, m + 1)))

    def tm512(wt, c0):
        for half in range(2):
            unit(tm(wt, range(4 * half, 4 * half + 4), c0, 512))

    def wout(wt):
        for kh in range(2):
            for nh in range(2):
                unit(tm(wt, range(4 * kh, 4 * kh + 4), nh * 512, 512))

    def ffn(w1, w3, w2):
        def up(f):
            unit(fm(w1, K8, (f,)) + fm(w3, K8, (f,)))

        def down(i):
            unit([w2[f * P:(f + 1) * P] for f in (2 * i, 2 * i + 1)])

        up(0)
        up(1)
        for i in range(1, NI):
            up(2 * i)
            up(2 * i + 1)
            down(i - 1)
        down(NI - 1)

    kvw = v["w_mem_kv"][0]
    tm512(kvw, 0)
    tm512(kvw, 512)
    wi = v["w_in"][0]
    o_kv, o_kr, o_u = Q_LORA, Q_LORA + KV_LORA, Q_LORA + KV_LORA + DROPE
    o_x, o_g = o_u + SSM_W, o_u + SSM_W + XH * XD
    fm_units(wi, o_x, XH * XD)
    fm_units(wi, o_u, SSM_W)
    unit(fm(wi, K8, (0, 1)))
    unit(fm(wi, K8, (2, 3)))
    unit(fm(wi, K8, (4,)) + tm(wi, K8, o_kr, DROPE))
    kv = v["w_kv_b"][0].reshape(KV_LORA, H_MLA, DNOPE + DV)
    kv = np.concatenate([kv[:, :, :DNOPE].reshape(KV_LORA, -1), kv[:, :, DNOPE:].reshape(KV_LORA, -1)], axis=1)
    qb = v["w_q_b"][0]
    fm_units(wi, o_g + 2 * D, TOK)
    unit([kv[0:P], kv[P:2 * P]])
    unit(tm(qb, range(3), 512, TOK))
    unit(tm(qb, range(3), 0, 512))
    fm_units(wi, o_g + 2 * D + TOK, D - TOK)

    def gates(wt, c0, g):
        fm_units(wt, c0 + g * D, D)

    def branch(wt, K):
        per = UW // (K * P)
        for m in range(0, KD, per):
            unit(fm(wt, range(K), range(m, m + per)))

    branch(v["w_o_cross"][0], 4)
    gates(wi, o_g, 1)
    fm_units(wi, o_g, D - TOK)
    unit(fm(v["w_glu"][0], range(4), range(4)))
    fm_units(wi, o_g + D - TOK, TOK)
    branch(v["w_o_ssm"][0], 4)
    branch(v["w_o_mla"][0], 4)
    wout(v["w_out"][0])
    assert len(out) == U_MIX1
    wu = v["w_up"][0]
    ffn(wu[:, :DFF], wu[:, DFF:], v["w_down"][0])
    for l in range(LAYERS):
        ffn(v["w1_ffn1_2"][l], v["w3_ffn1_2"][l], v["w2_ffn1_2"][l])
        w2 = v["w_in_2"][l]
        o = np.cumsum([0, 256, 256, 256, 256, 256, 512, 512, 256])
        fm_units(w2, o[0], 256)
        fm_units(w2, o[1], 256)
        unit(tm(w2, K8, o[2], 256))
        fm_units(w2, o[3], 256)
        fm_units(w2, o[4], 256)
        tm512(w2, o[5])
        unit(tm(w2, K8, o[7], 256))
        tm512(w2, o[6])
        gates(w2, o[8], 0)
        branch(v["w_branch_sb_2"][l], 2)
        gates(w2, o[8], 2)
        branch(v["w_branch_pool_2"][l], 2)
        gates(w2, o[8], 1)
        branch(v["w_branch_ret_2"][l], 4)
        wout(v["w_out_2"][l])
        ffn(v["w1_ffn2_2"][l], v["w3_ffn2_2"][l], v["w2_ffn2_2"][l])
    assert len(out) == U_USED, len(out)
    while len(out) < U_ALL:
        out.append(np.zeros((P, UW), np.float32))
    return np.stack(out)


def _cols(a):
    return np.ascontiguousarray(a.reshape(-1, P).T)


def _rows(a):
    return np.broadcast_to(a.reshape(1, -1), (P, a.size))


def _state_cols(a):
    return a.reshape(ST, 2 * NST).T


def _tri(fill_true, fill_false, keep):
    q, k = np.arange(P)[:, None], np.arange(P)[None, :]
    return np.where(keep(q, k), fill_true, fill_false).astype(np.float32)


def _consts1(v):
    a = np.zeros((P, NC1), np.float32)

    def put(name, val):
        c, w = C1[name]
        a[:, c:c + w] = val

    put("ident", np.eye(P, dtype=np.float32))
    put("ones", 1.0)
    diag = _tri(0.0, -1e37, lambda q, k: k <= q)
    put("causal", np.concatenate([diag, np.zeros((P, P), np.float32), diag], axis=1))
    for name, src in (("g_mem", "mem_norm_g"), ("g_mix", "norm_mix_g"), ("g_qa", "q_a_norm_g"),
                      ("g_kva", "kv_a_norm_g"), ("g_xq", "xq_norm_g"), ("g_xk", "xk_norm_g"), ("b_glu", "b_glu"),
                      ("g_ffn", "norm_ffn_g"), ("b_gate", "b_gate"), ("conv_b", "conv_b")):
        put(name, _cols(v[src][0]))
    put("ssm_d", _cols(v["ssm_d"][0].reshape(-1)))
    for name, src in (("gq_nope", "q_norm_g"), ("gk_nope", "k_norm_g")):
        c = np.ones((P, 1), np.float32)
        c[:DNOPE, 0] = v[src][0][:DNOPE]
        put(name, c)
    put("gq_rope", _rows(v["q_norm_g"][0][DNOPE:]))
    put("gk_rope", _rows(v["k_norm_g"][0][DNOPE:]))
    freq = np.float32(10000.0) ** (-np.arange(0, DROPE, 2, dtype=np.float32) / np.float32(DROPE))
    put("inv_freq", _rows(freq))
    put("lam_re", _state_cols(v["ssm_lambda_re"][0]))
    put("lam_im", _state_cols(v["ssm_lambda_im"][0]))
    put("log_dt", _state_cols(np.repeat(v["ssm_log_dt"][0][:, None], NST, axis=1)))
    cw = v["conv_w"][0].reshape(3, 2 * NF, P)
    put("conv_w", cw.transpose(2, 1, 0).reshape(P, 6 * NF))
    return a


def _consts2():
    a = np.zeros((P, NC2), np.float32)

    def put(name, val):
        c, w = C2[name]
        a[:, c:c + w] = val

    j = np.arange(TOK)[:, None]
    i = np.arange(TOK)[None, :]

    def two(m):
        return np.concatenate([m[:P], m[P:, P:]], axis=1)

    dec = []
    for h in range(RH):
        lg = np.log(1.0 - 2.0 ** (-5.0 - h))
        dec.append(two(np.where(i >= j, np.exp(np.maximum(i - j, 0) * lg), 0.0) * 64.0 ** -0.5))
    put("decay", np.concatenate(dec, axis=1))
    pl = []
    for win in POOLS:
        cnt = np.minimum(i + 1, win)
        pl.append(two(np.where((j <= i) & (j > i - win), 1.0 / cnt, 0.0) - (i == j)))
    put("pool", np.concatenate(pl, axis=1))
    d = np.arange(P) % 64 % 32
    freq = 10000.0 ** (-d.astype(np.float64) / 32)
    angle = (freq.astype(np.float32)[:, None] * np.arange(TOK, dtype=np.float32)[None, :]).astype(np.float64)
    put("cos", np.cos(angle))
    put("sin", np.sin(angle))
    rot = np.zeros((P, P), np.float32)
    for m in range(P):
        if m % 64 < 32:
            rot[m + 32, m] = -1.0
        else:
            rot[m - 32, m] = 1.0
    put("rot", rot)
    put("after", _tri(1.0, 0.0, lambda q, k: q > k))
    put("strict", two((j < i).astype(np.float64)))
    return a


def _layer_consts(v, l):
    a = np.zeros((P, NLC), np.float32)
    for name, val in (("g_ffn1", _cols(v["g_ffn1_2"][l])), ("g_mix", _cols(v["g_mix_2"][l])),
                      ("g_ffn2", _cols(v["g_ffn2_2"][l])), ("pool_scale", _cols(v["pool_scale_2"][l]))):
        c, w = LC[name]
        a[:, c:c + w] = val
    c, w = LC["w_pool"]
    for g in range(4):
        q, m = 64 * (g % 2), c + P * (g // 2) + 64 * (g % 2)
        a[q:q + 64, m:m + 64] = v["w_pool_2"][l][g]
    return a


def kernel(**inputs):
    import concourse.bacc as bacc
    from concourse.bass_utils import run_bass_kernel_spmd

    v = {k: np.asarray(a) for k, a in inputs.items()}
    b_re, b_im = (v[n][0].reshape(ST, P, GCH).transpose(1, 0, 2) for n in ("ssm_b_re", "ssm_b_im"))
    c_re, c_im = (v[n][0].transpose(0, 2, 1).reshape(ST, P, GCH).transpose(1, 0, 2)
                  for n in ("ssm_c_re", "ssm_c_im"))
    arrays = {
        "weights": _units(v),
        "consts1": _consts1(v),
        "consts2": _consts2(),
        "layer_consts": np.stack([_layer_consts(v, l) for l in range(LAYERS)]),
        "ssm_bc": np.ascontiguousarray(np.stack([b_re, b_im, c_re, c_im], axis=1)),
        "x": np.ascontiguousarray(v["x"].reshape(T, P, D)),
        "mem": np.ascontiguousarray(v["mem"].reshape(T, P, D)),
        "positions": np.ascontiguousarray(v["positions"].reshape(T, P).T),
        "g_final": np.ascontiguousarray(_rows(v["g_final_2"])),
    }
    nc = bacc.Bacc("TRN2", target_bir_lowering=False, num_devices=1)
    args = [nc.dram_tensor(n, a.shape, mybir.dt.from_np(a.dtype), kind="ExternalInput").ap()
            for n, a in arrays.items()]
    out = nc.dram_tensor("out", (T, P, D), F32, kind="ExternalOutput").ap()
    build_program(nc, *args, out)
    r = run_bass_kernel_spmd(nc, [arrays], core_ids=[0])
    return r.results[0]["out"].reshape(1, TOK, D)
```

```python
from contextlib import ExitStack

import numpy as np

import concourse.bass as bass
from concourse import mybir

F32 = mybir.dt.float32
FR = mybir.dt.float32r
I32 = mybir.dt.int32
ALU = mybir.AluOpType
ACT = mybir.ActivationFunctionType
AX = mybir.AxisListType

P = 128
TOK = 256
T = TOK // P
D = 1024
KD = D // P
EPS = 1e-6
H_MLA, DQK, DNOPE, DROPE, DV = 8, 96, 64, 32, 64
Q_LORA, KV_LORA = 384, 256
XH, XD = 4, 128
SSM_W = 512
GROUPS, GCH, NST = 32, 16, 64
ST = GROUPS * NST // P
DFF = 2816
NF = DFF // P
NI = NF // 2
LAYERS = 2
SBH, RH = 4, 4
POOLS = (2, 4, 8, 16)

Y_SLOTS = (14, 17, 21, 24)
DVE_LAYER_STEPS = 99

UW = 2048
RING = 3
U_MIX1, U_FFN, U_MIX2 = 37, 3 * NI, 30
U_BLOCK1 = U_MIX1 + U_FFN
U_LAYER = U_FFN + U_MIX2 + U_FFN
U_USED = U_BLOCK1 + LAYERS * U_LAYER
U_ALL = U_USED + RING - 2

MAGIC = 1.5 * 2.0 ** 23
TWO_PI = 2.0 * np.pi
PI_LOW = float(np.nextafter(np.float32(np.pi), np.float32(0)))


def _cody_waite():
    def cut(v, bits):
        m, e = np.frexp(v)
        return float(np.ldexp(np.trunc(m * 2.0 ** bits), int(e) - bits))
    a = cut(TWO_PI, 11)
    b = cut(TWO_PI - a, 11)
    return a, b, float(np.float32(TWO_PI - a - b))


CW = _cody_waite()

C1 = {}
_at = 0
for _n, _w in (("ident", P), ("ones", P), ("causal", 3 * P), ("g_mem", KD), ("g_mix", KD), ("g_qa", 3), ("g_kva", 2),
               ("g_xq", 1), ("g_xk", 1), ("b_glu", 4), ("ssm_d", 4), ("g_ffn", KD), ("b_gate", 3 * KD),
               ("gq_nope", 1), ("gk_nope", 1), ("gq_rope", DROPE), ("gk_rope", DROPE), ("inv_freq", DROPE // 2),
               ("lam_re", ST), ("lam_im", ST), ("log_dt", ST), ("conv_b", 2 * NF), ("conv_w", 6 * NF)):
    C1[_n] = (_at, _w)
    _at += _w
NC1 = _at

C2 = {}
_at = 0
for _n, _w in (("decay", RH * 3 * P), ("pool", 4 * 3 * P), ("cos", TOK), ("sin", TOK), ("rot", P), ("after", P),
               ("strict", 3 * P)):
    C2[_n] = (_at, _w)
    _at += _w
NC2 = _at

LC = {}
_at = 0
for _n, _w in (("g_ffn1", KD), ("g_mix", KD), ("g_ffn2", KD), ("pool_scale", 2), ("w_pool", 2 * P)):
    LC[_n] = (_at, _w)
    _at += _w
NLC = _at


class Plan:

    def __init__(self):
        self.jobs = {}
        self.count = {False: 0, True: 0}
        self.uses = {}
        self.unit_end = {}

    def add(self, name, place, layer):
        k = self.count[layer]
        self.count[layer] += 1
        u = None
        if place:
            per = self.uses.setdefault(place, {False: 0, True: 0})
            u = (place, per[layer])
            per[layer] += 1
        assert (name, layer) not in self.jobs, name
        self.jobs[(name, layer)] = (k, u)

    def done(self, name, l=None):
        k, _ = self.jobs[(name, l is not None)]
        if l is None:
            return k + 1
        return l * self.count[True] + (self.count[False] + k + 1)

    def use(self, name, l=None):
        place, k = self.jobs[(name, l is not None)][1]
        if l is None:
            return k
        return l * self.uses[place][True] + (self.uses[place][False] + k)

    def unit_done(self, k, l=None):
        return self.done(self.unit_end[(k, l is not None)], l)

    def place(self, name, l=None):
        return self.jobs[(name, l is not None)][1][0]


UNITS1 = [["mku0", "mku1"], ["mk0", "mk1"], ["mvu0", "mvu1"], ["mv0", "mv1"], ["xq0"], ["xq1"], ["ux0"], ["ux1"],
          ["c0"], ["c1"], ["c2"], ["gc0"], ["kv"], ["qb"], ["qa"], ["gc1"], ["gc2"], ["gc3"], ["bc0", "bc1"],
          ["bc2", "bc3"], ["gs0"], ["gs1"], ["gs2"], ["gs3"], ["gm0"], ["gm1"], ["gl0", "gl1"], ["gm2"], ["gm3"],
          ["bs0", "bs1"], ["bs2", "bs3"], ["bm0", "bm1"], ["bm2", "bm3"], ["wou0"],
          ["wou1"], ["wou2"], ["wo"]]
UNITS2 = [["sbq"], ["sbk"], ["sbv"], ["rq"], ["rk"], ["rvu0", "rvu1"], ["rv0", "rv1"], ["up"], ["rgu0", "rgu1"],
          ["rg0", "rg1"], ["ga0"], ["ga1"], ["ga2"], ["ga3"], ["ba0", "ba1", "ba2", "ba3"], ["gp0"], ["gp1"],
          ["gp2"], ["gp3"], ["bp0", "bp1", "bp2", "bp3"], ["gr0"], ["gr1"], ["gr2"], ["gr3"], ["br0", "br1"],
          ["br2", "br3"], ["wou0"], ["wou1"], ["wou2"], ["wo"]]


def make_plan():
    plan = Plan()
    turn = [0]

    def part(name, layer):
        plan.add(name, f"p{turn[0] % 3}", layer)
        turn[0] += 1

    def small(name, place, layer):
        plan.add(name, place, layer)

    def norm(tag, layer):
        for c in range(KD // 2):
            small(f"{tag}T{c}", None, layer)

    def ffn(tag, layer, u0):
        names = [("A0", "p0"), ("B0", "p1")]
        for i in range(1, NI):
            names += [(f"A{i}", "p0"), (f"B{i}", "p1"), (f"D{i - 1}", None)]
        names.append((f"D{NI - 1}", "big"))
        for n, (name, place) in enumerate(names):
            if place == "big":
                small(tag + name + "t1", None, layer)
            small(tag + name, place, layer)
            plan.unit_end[(u0 + n, layer)] = tag + name

    norm("mem", False)
    turn[0] = 0
    for u in range(U_MIX1):
        for j in UNITS1[u]:
            if j == "wo":
                small("wot1", None, False)
            if j in ("wo", "kv", "qa"):
                small(j, "big", False)
            elif j[-2:] in ("u0", "u1", "u2"):
                small(j, None, False)
            elif u < 7:
                part(j, False)
            else:
                small(j, f"p{turn[0] % 2}", False)
                turn[0] += 1
            plan.unit_end[(u, False)] = j
        for j, place in {0: [(f"xT{c}", None) for c in range(KD // 2)], 3: [("kT", "big")], 5: [("bT", "big")], 6: [("ssq", "p3"), ("xs", "big")], 9: [("xp", "big")],
                         10: [("xo", "big")], 11: [("cs", "big")], 24: [("tq0", "big")], 25: [("sc0", "big")],
                         26: [("tq1", "big")], 27: [("sc1", "big")], 28: [("pt0", "big")],
                         29: [("pv0", "p3"), ("pt1", "big")], 30: [("pv1", "p3")]}.get(u, []):
            small(j, place, False)
        if u == 6:
            turn[0] = 0
        if 7 <= u < 7 + ST:
            small(f"bu{u - 7}", "p3", False)
        if 9 <= u < 9 + ST:
            small(f"cy{u - 9}", "p2" if (u - 9) % 4 == 3 else None, False)
    norm("f0", False)
    ffn("f0", False, U_MIX1)
    turn[0] = 0
    norm("f1", True)
    ffn("f1", True, 0)
    norm("m", True)
    for u in range(U_MIX2):
        for j in UNITS2[u]:
            if j == "wo":
                small("wot1", None, True)
                small("wo", "big", True)
            elif j[-2:] in ("u0", "u1", "u2"):
                small(j, None, True)
            else:
                part(j, True)
            plan.unit_end[(U_FFN + u, True)] = j
        for j, place in {3: [("z", "big")], 5: [("pq", "p3")], 6: [("pk", "p3")], 8: [("pl1", "p3")],
                         9: [("pl2", "p3"), ("sa", "big")], 11: [("rs", "big")], 12: [("pv", "p3")],
                         13: [("ry", "big")], 19: [("rt", "big")]}.get(u, []):
            small(j, place, True)
    norm("f2", True)
    ffn("f2", True, U_FFN + U_MIX2)
    return plan


class Steps:

    def __init__(self, eng, sem):
        self.eng, self.sem, self.n, self.loops = eng, sem, 0, []

    def __call__(self, ins):
        ins.then_inc(self.sem, 1)
        self.n += 1
        self.wait()

    def wait(self):
        v = self.n
        for var, per, _ in self.loops:
            v = var * per + v
        self.eng.wait_ge(self.sem, v)

    def enter(self, var, per):
        self.loops.append((var, per, self.n))

    def leave(self, turns):
        _, per, at = self.loops.pop()
        assert self.n - at == per, f"{self.eng}: {self.n - at} steps in a turn, not {per}"
        self.n = at + per * turns


def build_program(nc, ws, c1_d, c2_d, lc_d, bc_d, x_d, mem_d, pos_d, gfin_d, out_d):
    plan = make_plan()
    with ExitStack() as ctx:
        def sb(name, shape, dt=F32):
            return ctx.enter_context(nc.sbuf_tensor(name, shape, dt))

        sems = {}

        def S(name):
            if name not in sems:
                sems[name] = ctx.enter_context(nc.semaphore(name))
            return sems[name]

        raw = sb("raw", [P, RING, UW])
        whi = sb("whi", [P, RING, UW], FR)
        wlo = sb("wlo", [P, RING, UW], FR)
        h_hi = sb("h_hi", [P, KD, TOK], FR)
        h_lo = sb("h_lo", [P, KD, TOK], FR)
        b_hi = sb("b_hi", [P, KD, TOK], FR)
        b_lo = sb("b_lo", [P, KD, TOK], FR)
        x = sb("x_rows", [P, T, D])
        c1 = sb("c1", [P, NC1])
        lc = sb("lc", [P, NLC])
        sm = sb("sm", [P, 1700])
        pos = sb("pos", [P, T], I32)
        s5c = sb("s5c", [P, 2048])
        s5x = sb("s5x", [P, 1024])
        ar = sb("ar", [P, 18432])

        pb = {n: ctx.enter_context(nc.psum_tensor(n, [P, 512], F32)) for n in ("p0", "p1", "p2", "p3")}
        big = ctx.enter_context(nc.psum_tensor("big", [P, 4, 512], F32))
        bigf = big[:, :, :].rearrange("p a b -> p (a b)")

        def norm_bank(first, c):
            return big[:, c, :] if first else pb[f"p{c}"][:, :]

        def area(at, n):
            return ar[:, at:at + n]

        XS, MG, GT, R, W = 0, 2048, 4096, 8192, 12288
        xs = area(XS, 2048).rearrange("p (t d) -> p t d", t=T)
        merged = area(MG, 2048).rearrange("p (m t) -> p m t", m=KD)
        junk_act, junk_act2, junk_dve = area(MG, 1024), area(MG + 1024, 512), area(MG + 1536, 512)
        gates = area(GT, 4096).rearrange("p (g t) -> p g t", g=16)
        f_s = area(GT, 512).rearrange("p (a t) -> p a t", a=2)
        f_g = area(GT + 512, 512).rearrange("p (a t) -> p a t", a=2)
        f_c = area(GT + 1024, 1024).rearrange("p (a t) -> p a t", a=2)

        def col(name, k=0, n=1):
            a, _ = C1[name]
            return c1[:, a + k:a + k + n]

        ident, ones, causal = (c1[:, C1[n][0]:C1[n][0] + C1[n][1]] for n in ("ident", "ones", "causal"))
        c2 = area(W, NC2)

        def col2(name):
            a, w = C2[name]
            return c2[:, a:a + w]

        def lcol(name, k=0, n=1):
            a, _ = LC[name]
            return lc[:, a + k:a + k + n]

        smt = [0]

        def small(n):
            a = smt[0]
            smt[0] += n
            assert smt[0] <= 1700
            return sm[:, a:a + n]

        ss, msq, rstd = small(3), small(2), small(2)
        neg_half = small(16)

        ang, tri_k, tri_r, tri_w, tri_m = small(48), small(48), small(48), small(48), small(48)
        cos48, sin48 = small(48), small(48)
        theta, rope_c, rope_s = ang[:, 0:ST], cos48[:, ST:], sin48[:, ST:]
        dt_, mag = small(ST), small(ST)
        tA, tB, tC, tD = small(ST), small(ST), small(ST), small(ST)
        f_re, f_im = small(ST), small(ST)
        pA, pB, pC = small(ST), small(ST), small(ST)
        pw = [(small(ST), small(ST)), (small(ST), small(ST))]
        e128n = small(ST)
        ini = small(2)
        posf = small(T)
        gxx, gqk = small(1), small(1)
        hb = small(3 * KD + 4)
        ssk, rsk, msx, rsq = small(8), small(8), small(8), small(8)
        xmax, xneg, xsum, xrec, xscl = small(8), small(8), small(8), small(8), small(8)
        msc, rc = small(4), small(4)
        mq, mk, rq_, rk_, mkr, qsc = small(16), small(16), small(16), small(16), small(2), small(16)
        qmx, qng, qsm, qrc = small(8), small(8), small(8), small(8)
        kr, krg, kro = small(64), small(64), small(64)
        rms8, rr8 = small(8), small(8)

        E_c = area(W, ST * P).rearrange("p (j t) -> p j t", j=ST)
        E_s = area(W + ST * P, ST * P).rearrange("p (j t) -> p j t", j=ST)
        s5_m1, s5_m2 = area(W + 4096, 512), area(W + 4608, 512)
        s5_z = [area(W + 5120, 512), area(W + 5632, 512)]
        s5_p, s5_q = s5x[:, 0:512], s5x[:, 512:1024]
        Bl = [s5c[:, 512 * a:512 * (a + 1)].rearrange("p (b n) -> p b n", b=4) for a in range(2)]
        Cl = [s5c[:, 1024 + 512 * a:1536 + 512 * a].rearrange("p (j c) -> p j c", j=ST) for a in range(2)]
        bcr = area(W + 4096, 4 * ST * GCH).rearrange("p (a j c) -> p a j c", a=4, j=ST)
        bbd = area(W + 5120, 1024).rearrange("p (a j c) -> p a j c", a=2, j=ST)
        btmp = area(XS, 512).rearrange("p (a j c) -> p a j c", a=2, j=ST)
        e_tmp = [area(GT + 1024 * i, 1024).rearrange("p (j t) -> p j t", j=ST) for i in range(4)]
        kt_x = area(R, 1024).rearrange("p (h t) -> p h t", h=XH)
        v_x = area(R + 1024, 1024).rearrange("p (t n) -> p t n", t=T)
        q_x = area(R + 2048, 1024).rearrange("p (h t) -> p h t", h=XH)
        u_fm = area(R + 3072, 1024).rearrange("p (b t) -> p b t", b=4)
        k_x = area(MG, 1024).rearrange("p (t n) -> p t n", t=T)
        sq_x = area(MG + 1024, 1024).rearrange("p (h t) -> p h t", h=XH)
        p_x = area(GT, 2048).rearrange("p (a t) -> p a t", a=8)
        pT_x = area(GT + 2048, 2048)
        x_y = area(GT + 2048, 1024)
        c_sq = area(MG, 5 * TOK).rearrange("p (c t) -> p c t", c=5)
        K_m = area(R, 16 * DQK).rearrange("p (a d) -> p a d", a=16)
        Q_m = area(R + 1536, 16 * DQK)
        Qh = Q_m.rearrange("p (a d) -> p a d", a=16)
        V_m = area(XS + 1024, 1024).rearrange("p (t n) -> p t n", t=T)
        m_sq = area(MG, 1536)
        m_t = [area(GT + 3072 + 256 * i, 256) for i in range(4)]
        QT, KT = area(W, 1024), area(W + 1024, 1024)
        P_m = [area(W + 2048 + 1536 * g, 1536).rearrange("p (h c) -> p h c", h=4) for g in range(2)]
        PT = area(W, 1536).rearrange("p (h c) -> p h c", h=4)
        y_s = area(XS, 1024).rearrange("p (b t) -> p b t", b=4)
        sg_s = area(W + 5120, 1024).rearrange("p (b t) -> p b t", b=4)
        strict4 = col2("strict").unsqueeze(1).to_broadcast([P, 4, 3 * P])
        A_z, C_z, B_z, D_z = (area(a, 1536).rearrange("p (h c) -> p h c", h=4)
                              for a in (GT, GT + 1536, W + 4608, MG))
        sbq, sbk, sbv = area(R, 512), area(R + 512, 512), area(R + 1024, 512)
        rq, rk, rt = area(R + 1536, 512), area(R + 2048, 512), area(R + 2560, 512)
        rv = area(R + 3072, 1024).rearrange("p (t n) -> p t n", t=T)
        rg, up = area(XS, 1024), area(XS + 1024, 512)
        y_sq, y_n = area(W + 4608, 1024), area(R, 1024)

        def slot(u):
            return u % RING

        def wait(eng, name, v):
            if isinstance(v, int) and v <= 0:
                return
            eng.wait_ge(S(name), v)

        def job_done(eng, name, l=None):
            eng.wait_ge(S("pe_done"), plan.done(name, l))

        def place_read(eng, name, l=None):
            wait(eng, plan.place(name, l) + "_read", plan.use(name, l) + 1)

        def place_free(eng, name, l=None):
            wait(eng, plan.place(name, l) + "_read", plan.use(name, l))

        def read_sem(name, l=None):
            return S(plan.place(name, l) + "_read")

        def bank(name, l=None):
            return pb[plan.place(name, l)]

        def unit(k, l=None):
            return k if l is None else l * U_LAYER + (U_BLOCK1 + k)

        def ustat(k, l=None):
            return k if l is None else U_BLOCK1 + k

        def last_splits(eng, l):
            eng.wait_ge(S("pe_done"), l * plan.count[True] + plan.count[False])
            return [(s % RING, l * (U_LAYER // RING) + (s // RING + 1), l * U_LAYER + (s + 1))
                    for s in (U_BLOCK1 - 2 + RING, U_BLOCK1 - 1 + RING)]

        block = ctx.enter_context(nc.Block())

        @block.sync
        def _(sp):
            sp.dma_start(c1[:, :], c1_d).then_inc(S("c1_in"), 16)
            sp.dma_start(pos[:, :], pos_d).then_inc(S("pos_in"), 16)
            for r in range(RING):
                sp.dma_start(raw[:, r, :], ws[r]).then_inc(S(f"raw_in{r}"), 16)
                if r == 0:
                    sp.dma_start(x[:, :, :], x_d.rearrange("t p d -> p t d")).then_inc(S("x_in"), 16)
            sp.dma_start(bcr, bc_d).then_inc(S("bc_in"), 16)
            turns = (U_ALL - RING) // RING
            with sp.Fori(0, turns) as i:
                for r in range(RING):
                    sp.wait_ge(S("lo_done"), i * RING + (r + 1))
                    sp.dma_start(raw[:, r, :], ws[i * RING + (RING + r)]).then_inc(S(f"raw_in{r}"), 16)
            for u in range(RING + turns * RING, U_ALL):
                sp.wait_ge(S("lo_done"), u - RING + 1)
                sp.dma_start(raw[:, u % RING, :], ws[u]).then_inc(S(f"raw_in{u % RING}"), 16)
            for n, t in enumerate((1, 0)):
                sp.wait_ge(S("out_ready"), n + 1)
                sp.dma_start(out_d[t], xs[:, t, :]).then_inc(S("out_sent"), 16)
            sp.wait_ge(S("out_sent"), 16 * T)
            for r in range(RING):
                sp.wait_ge(S(f"raw_in{r}"), 16 * len(range(r, U_ALL, RING)))

        def split_act(act, s, l=None, m=None):
            us = ustat(s, l) + RING
            r, q = us % RING, us // RING + 1
            done = plan.unit_done(s, l)
            if l is not None:
                q = l * (U_LAYER // RING) + q
            if m is not None:
                q, done = m * 2 + q, m * 6 + done
            act.wait_ge(S(f"raw_in{r}"), q * 16)
            act.wait_ge(S("pe_done"), done)
            act.activation(whi[:, r, :], raw[:, r, :], ACT.Copy).then_inc(S("hi_done"), 1)

        def split_dve(dve, s, l=None, m=None):
            r = (ustat(s, l) + RING) % RING
            n = unit(s, l) + (RING + 1)
            if m is not None:
                n = m * 6 + n
            dve.wait_ge(S("hi_done"), n)
            dve.tensor_tensor(wlo[:, r, :], raw[:, r, :], whi[:, r, :].bitcast(F32), ALU.subtract)\
               .then_inc(S("lo_done"), 1)

        @block.gpsimd
        def _(pool):
            step = Steps(pool, S("pool_step"))
            step(nc.gpsimd.memset(neg_half, -0.5))
            step(nc.gpsimd.memset(area(W + 5120, 1024), 0.0))
            nc.gpsimd.memset(s5c[:, 1024:2048], 0.0).then_inc(S("bd_zero"), 1)

            def rsqrt(dst, src, n, ready, v, done):
                pool.wait_ge(S(ready), v)
                nc.gpsimd.tensor_tensor(dst, src, neg_half[:, 0:n], ALU.pow).then_inc(S(done), 1)

            def norm(n):
                rsqrt(rstd[:, 1:2], msq[:, 1:2], 1, "msq1", n + 1, "rstd1")
                rsqrt(rstd[:, 0:1], msq[:, 0:1], 1, "msq0", n + 1, "rstd0")

            norm(0)
            norm(1)
            pool.wait_ge(S("trig"), 2)
            step(nc.gpsimd.memset(E_c[:, :, 0:1], 1.0))
            step(nc.gpsimd.memset(E_s[:, :, 0:1], 0.0))
            e, s = (cos48[:, 0:ST], sin48[:, 0:ST]), 1
            while s < P:
                if s == 16:
                    rsqrt(rsk, ssk, 8, "kx_msq", 1, "kx_rstd")
                pc, ps = (a.unsqueeze(2).to_broadcast([P, ST, s]) for a in e)
                a = [t[:, :, 0:s] for t in e_tmp]
                nc.gpsimd.tensor_tensor(a[0], E_c[:, :, 0:s], pc, ALU.mult)
                nc.gpsimd.tensor_tensor(a[1], E_s[:, :, 0:s], ps, ALU.mult)
                nc.gpsimd.tensor_tensor(a[2], E_c[:, :, 0:s], ps, ALU.mult)
                step(nc.gpsimd.tensor_tensor(a[3], E_s[:, :, 0:s], pc, ALU.mult))
                nc.gpsimd.tensor_tensor(E_c[:, :, s:2 * s], a[0], a[1], ALU.subtract)
                step(nc.gpsimd.tensor_tensor(E_s[:, :, s:2 * s], a[2], a[3], ALU.add))
                to = pw[1] if e[0] is pw[0][0] else pw[0]
                nc.gpsimd.tensor_tensor(pA, e[0], e[0], ALU.mult)
                nc.gpsimd.tensor_tensor(pB, e[1], e[1], ALU.mult)
                step(nc.gpsimd.tensor_tensor(pC, e[0], e[1], ALU.mult))
                nc.gpsimd.tensor_tensor(to[0], pA, pB, ALU.subtract)
                step(nc.gpsimd.tensor_tensor(to[1], pC, pC, ALU.add))
                e, s = to, 2 * s
            assert e is pw[0]
            nc.gpsimd.tensor_scalar(e128n, e[1], -1.0, None, ALU.mult).then_inc(S("E_ready"), 1)
            rsqrt(rsq, msx, 8, "p3_read", plan.use("ssq") + 1, "xq_rstd")

            def rotate_out(j):
                z4 = s5_z[j % 2].rearrange("p (a t) -> p a t", a=4)
                pool.wait_ge(S("z_ready"), j + 1)
                if j:
                    job_done(pool, f"cy{j - 1}")
                ec, es = (a[:, j, :].unsqueeze(1).to_broadcast([P, 4, P]) for a in (E_c, E_s))
                nc.gpsimd.tensor_tensor(s5_p.rearrange("p (a t) -> p a t", a=4), z4, ec, ALU.mult)
                step(nc.gpsimd.tensor_tensor(s5_q.rearrange("p (a t) -> p a t", a=4), z4, es, ALU.mult))
                nc.gpsimd.tensor_tensor(s5_p[:, 0:TOK], s5_p[:, 0:TOK], s5_q[:, TOK:], ALU.subtract)
                nc.gpsimd.tensor_tensor(s5_p[:, TOK:], s5_p[:, TOK:], s5_q[:, 0:TOK], ALU.add).then_inc(S("s_ready"), 1)
                pool.wait_ge(S("s_ready"), j + 1)

            for j in range(ST):
                rotate_out(j)
                if j == 3:
                    rsqrt(rc, msc, 4, "big_read", plan.use("cs") + 1, "c_rstd")
                if j == 11:
                    rsqrt(rq_, mq, 16, "mq_msq", 1, "mq_rstd")
                    rsqrt(rk_, mk, 16, "mk_msq", 1, "mk_rstd")
            norm(2)
            pool.wait_ge(S("p3_read"), plan.use("pv1") + 1)
            nc.gpsimd.dma_start(c2, c2_d).then_inc(S("c2_in"), 16)
            pool.wait_ge(S("c2_in"), 16)
            with pool.Fori(0, LAYERS) as l:
                pool.wait_ge(S("h_lo"), l * (3 * KD) + 3 * KD)
                nc.gpsimd.dma_start(lc[:, :], lc_d[l]).then_inc(S("lc_in"), 16)
                norm(l * 3 + 3)
                norm(l * 3 + 4)
                place_read(pool, "z", l)
                nc.gpsimd.tensor_tensor(C_z, C_z, strict4, ALU.mult).then_inc(S("lf_ready"), 1)
                pool.wait_ge(S("w_exp"), l + 1)
                nc.gpsimd.tensor_tensor(B_z, B_z, strict4, ALU.mult).then_inc(S("w_ready"), 1)
                rsqrt(rr8, rms8, 8, "y_msq", l + 1, "y_rstd")
                place_read(pool, "ry", l)
                place_read(pool, "rg0", l)
                place_read(pool, "rg1", l)
                nc.gpsimd.tensor_tensor(y_n, y_n, rg, ALU.mult).then_inc(S("yn_ready"), 1)
                norm(l * 3 + 5)
            nc.gpsimd.dma_start(area(R, D), gfin_d).then_inc(S("gfin_in"), 16)
            norm(3 + 3 * LAYERS)

        @block.tensor
        def _(pe):
            def mm3(out, s, m, start, stop):
                pe.matmul(out, s[0], m[0], start=start, stop=False)
                pe.matmul(out, s[0], m[1], start=False, stop=False)
                return pe.matmul(out, s[1], m[0], start=False, stop=stop)

            def w(k, l, a, n):
                r = slot(ustat(k, l))
                return whi[:, r, a:a + n], wlo[:, r, a:a + n]

            def hk(k, lo=0, n=TOK):
                return h_hi[:, k, lo:lo + n], h_lo[:, k, lo:lo + n]

            def bk(k, lo=0, n=TOK):
                return b_hi[:, k, lo:lo + n], b_lo[:, k, lo:lo + n]

            def bk_from(k0):
                return lambda k, lo=0, n=TOK: bk(k0 + k, lo, n)

            def unit_in(k, l=None, extra=0):
                pe.wait_ge(S("lo_done"), extra + unit(k, l) + 1)

            def fin(ins):
                ins.then_inc(S("pe_done"), 1)

            def norm_T(n, first=False):

                def turn(t, ks):
                    for k in ks:
                        at = (k % 2) * TOK + t * P
                        last = pe.transpose(norm_bank(first, k // 2)[:, at:at + P], xs[:, t, k * P:(k + 1) * P], ident)
                        if t == 0 and k % 2:
                            fin(last)

                pe.wait_ge(S("xs_t1a"), n + 1)
                turn(1, range(KD // 2))
                pe.wait_ge(S("xs_t1b"), n + 1)
                turn(1, range(KD // 2, KD))
                pe.wait_ge(S("xs_t0a"), n + 1)
                turn(0, range(KD // 2))
                pe.wait_ge(S("xs_t0b"), n + 1)
                turn(0, range(KD // 2, KD))

            def fm(k, l, out, moving, K, m, n=None):
                for kk in range(K):
                    if n is not None:
                        pe.wait_ge(S("h_lo"), n * KD + max(kk + 1, 2))
                    last = mm3(out, w(k, l, (m * K + kk) * P, P), moving(kk), kk == 0, kk == K - 1)
                return last

            def fm_unit(k, l, name, n=None):
                unit_in(k, l)
                place_free(pe, name, l)
                b = bank(name, l)
                fm(k, l, b[:, 0:TOK], hk, KD, 0, n)
                fin(fm(k, l, b[:, TOK:], hk, KD, 1))

            def tm_half(k, l, name, half, moving=hk, n=None):
                unit_in(k, l)
                for t in range(T):
                    job = name + str(t)
                    if half == 0:
                        place_free(pe, job, l)
                    for q in range(4):
                        kk = half * 4 + q
                        if n is not None and t == 0:
                            pe.wait_ge(S("h_lo"), n * KD + (kk + 1))
                        last = mm3(bank(job, l)[:, :], moving(kk, t * P, P), w(k, l, q * 512, 512),
                                   kk == 0, kk == KD - 1)
                    fin(last)

            def tm_unit(k, l, name):
                unit_in(k, l)
                place_free(pe, name, l)
                for t in range(T):
                    for kk in range(KD):
                        last = mm3(bank(name, l)[:, t * TOK:(t + 1) * TOK], hk(kk, t * P, P), w(k, l, kk * TOK, TOK),
                                   kk == 0, kk == KD - 1)
                fin(last)

            def branch(k, l, names, moving, K):
                unit_in(k, l)
                for j, name in enumerate(names):
                    place_free(pe, name, l)
                    b = bank(name, l)
                    fm(k, l, b[:, 0:TOK], moving, K, 2 * j)
                    fin(fm(k, l, b[:, TOK:], moving, K, 2 * j + 1))

            def w_out(k, l):
                place_free(pe, "wo", l)
                m_base = 0 if l is None else l * 4 + 4
                for q in range(4):
                    kh, nh = q // 2, q % 2
                    pe.wait_ge(S("m_lo"), m_base + (2 + 2 * kh))
                    unit_in(k + q, l)
                    for t in (1, 0):
                        for a in range(4):
                            kk = kh * 4 + a
                            last = mm3(big[:, 2 * t + nh, :], hk(kk, t * P, P), w(k + q, l, a * 512, 512),
                                       kk == 0, kk == KD - 1)
                        if q == 3 or t == 0:
                            fin(last)

            def ffn(k0, l, tag, n):
                ua, ub = plan.use(tag + "A0", l), plan.use(tag + "B0", l)

                def up(k, place, used, extra=0, n=None):
                    unit_in(k, l, extra)
                    wait(pe, place + "_read", used)
                    b = pb[place]
                    fm(k, l, b[:, 0:TOK], hk, KD, 0, n)
                    fin(fm(k, l, b[:, TOK:], hk, KD, 1))

                def down(k, start, stop, i, par, extra=0):
                    unit_in(k, l, extra)
                    pe.wait_ge(S("p0_read"), i + (ua + 1))
                    pe.wait_ge(S("p1_read"), i + (ub + 1))
                    for t in (1, 0):
                        for nh in range(2):
                            for a in range(2):
                                last = mm3(big[:, 2 * t + nh, :], bk(2 * par + a, t * P, P),
                                           w(k, l, a * D + nh * 512, 512), start and a == 0, stop and a == 1)
                        if stop or t == 0:
                            fin(last)

                up(k0, "p0", ua, n=n)
                up(k0 + 1, "p1", ub)
                up(k0 + 2, "p0", ua + 1)
                up(k0 + 3, "p1", ub + 1)
                down(k0 + 4, True, False, 0, 0)
                up(k0 + 5, "p0", ua + 2)
                up(k0 + 6, "p1", ub + 2)
                down(k0 + 7, False, False, 1, 1)
                with pe.Fori(0, (NI - 3) // 2) as m:
                    for h in range(2):
                        up(k0 + 8 + 3 * h, "p0", m * 2 + (ua + 3 + h), extra=m * 6)
                        up(k0 + 9 + 3 * h, "p1", m * 2 + (ub + 3 + h), extra=m * 6)
                        down(k0 + 10 + 3 * h, False, False, m * 2 + (2 + h), h, extra=m * 6)
                down(k0 + 32, False, True, NI - 1, (NI - 1) % 2)

            pe.wait_ge(S("c1_in"), 16)
            norm_T(0, True)

            def s5_b():
                pe.wait_ge(S("bbd"), 1)
                place_free(pe, "bT")
                for a in range(2):
                    for b in range(4):
                        last = pe.transpose(big[:, a, b * P:(b + 1) * P],
                                            bbd[:, a, 4 * b:4 * b + 4, :].rearrange("p j c -> p (j c)"), ident)
                fin(last)

            def s5_in(j):
                if j % 8 == 0:
                    place_read(pe, "ux0" if j == 0 else "ux1")
                    place_read(pe, "bT")
                place_free(pe, f"bu{j}")
                b, q = j // 4, 32 * (j % 4)
                for a in range(2):
                    last = pe.matmul(pb["p3"][:, a * TOK:(a + 1) * TOK], Bl[a][q:q + 32, b, :],
                                     u_fm[q:q + 32, b, :], start=True, stop=True, tile_position=(q, 0))
                fin(last)

            def s5_out(j):
                b, q = j // 4, 32 * (j % 4)
                if j % 4 == 0:
                    place_free(pe, f"cy{j + 3}")
                pe.wait_ge(S("s_ready"), j + 1)
                out = pb["p2"][q:q + 32, (b % 2) * TOK:(b % 2 + 1) * TOK]
                pe.matmul(out, Cl[0][:, j, :], s5_p[:, 0:TOK], start=True, stop=False)
                fin(pe.matmul(out, Cl[1][:, j, :], s5_p[:, TOK:], start=False, stop=True))

            def x_kT():
                pe.wait_ge(S("h_lo"), 2 * KD)
                pe.wait_ge(S("kx_ready"), 1)
                for h in range(XH):
                    for t in range(T):
                        last = pe.transpose(big[:, h // 2, (h % 2) * TOK + t * P:(h % 2) * TOK + (t + 1) * P],
                                            k_x[:, t, h * XD:(h + 1) * XD], ident)
                fin(last)

            def x_scores():
                place_read(pe, "xq0")
                place_read(pe, "xq1")
                for t in range(T):
                    for h in range(XH):
                        last = pe.matmul(pb["p3"][:, t * XH + h:t * XH + h + 1], sq_x[:, h, t * P:(t + 1) * P],
                                         ones[:, 0:1], start=True, stop=True)
                fin(last)
                place_read(pe, "kT")
                place_free(pe, "xs")
                for t in range(T):
                    for h in range(XH):
                        last = pe.matmul(big[:, 2 * t + h // 2, (h % 2) * TOK:(h % 2 + 1) * TOK],
                                         q_x[:, h, t * P:(t + 1) * P], kt_x[:, h, :], start=True, stop=True)
                fin(last)

            def x_probs():
                pe.wait_ge(S("xp_ready"), 1)
                place_free(pe, "xp")
                for h in range(XH):
                    for kt in range(T):
                        for t in range(T):
                            last = pe.transpose(
                                big[:, 2 * kt + h // 2, (h % 2) * TOK + t * P:(h % 2) * TOK + (t + 1) * P],
                                p_x[:, t * XH + h, kt * P:(kt + 1) * P], ident)
                fin(last)

            def x_out():
                place_read(pe, "mv0")
                place_read(pe, "mv1")
                place_read(pe, "xp")
                for h in range(XH):
                    for kt in range(T):
                        last = pe.matmul(big[:, h // 2, (h % 2) * TOK:(h % 2 + 1) * TOK],
                                         v_x[:, kt, h * XD:(h + 1) * XD],
                                         pT_x[:, kt * 1024 + h * TOK:kt * 1024 + (h + 1) * TOK],
                                         start=kt == 0, stop=kt == 1)
                fin(last)

            def c_sums():
                for name in ("c0", "c1", "c2"):
                    place_read(pe, name)
                place_free(pe, "cs")
                for c, ks in enumerate((range(0, 3), range(3, 5))):
                    for t in range(T):
                        for kk in ks:
                            last = pe.matmul(bigf[:, 2 * c + t:2 * c + t + 1], c_sq[:, kk, t * P:(t + 1) * P],
                                             ones[:, 0:1], start=kk == ks[0], stop=kk == ks[-1])
                fin(last)

            def m_turn(g):
                if g == 0:
                    pe.wait_ge(S("qk_ready"), 1)
                place_free(pe, f"tq{g}")
                for which, src in enumerate((Qh, K_m)):
                    for h in range(4):
                        for t in range(T):
                            at = (h % 2) * TOK + t * P
                            last = pe.transpose(big[0:DQK, 2 * which + h // 2, at:at + P],
                                                src[:, t * H_MLA + 4 * g + h, :], ident)
                fin(last)

            def m_scores(g):
                place_read(pe, f"tq{g}")
                for h in range(4):
                    q, k = QT[0:DQK, h * TOK:(h + 1) * TOK], KT[0:DQK, h * TOK:(h + 1) * TOK]
                    pe.matmul(big[:, h, 0:P], q[:, 0:P], k[:, 0:P], start=True, stop=True)
                    last = pe.matmul(big[:, h, P:3 * P], q[:, P:TOK], k[:, :], start=True, stop=True)
                fin(last)

            def m_probs(g):
                pe.wait_ge(S("mp_ready"), g + 1)
                place_free(pe, f"pt{g}")
                for h in range(4):
                    for c in range(3):
                        last = pe.transpose(big[:, h, c * P:(c + 1) * P], P_m[g][:, h, c * P:(c + 1) * P], ident)
                fin(last)

            def pv_product(out, v0, v1, probs):
                pe.matmul(out, v0, probs[:, 0:TOK], start=True, stop=False)
                return pe.matmul(out[:, P:TOK], v1, probs[:, TOK:3 * P], start=False, stop=True)

            def m_out(g):
                place_read(pe, f"pt{g}")
                place_read(pe, "kv")
                place_free(pe, f"pv{g}")
                for h in range(4):
                    a = (4 * g + h) * DV
                    last = pv_product(pb["p3"][64 * (h % 2):64 * (h % 2) + 64, (h // 2) * TOK:(h // 2 + 1) * TOK],
                                      V_m[:, 0, a:a + DV], V_m[:, 1, a:a + DV], PT[:, h, :])
                fin(last)

            for u in range(U_MIX1):
                names = UNITS1[u]
                if u < 4:
                    tm_half(u, None, ("mk", "mv")[u // 2], u % 2, bk, 0 if u < 2 else None)
                elif u == 10:
                    unit_in(u)
                    place_free(pe, "c2")
                    fm(u, None, bank("c2")[:, 0:TOK], hk, KD, 0)
                    for t in range(T):
                        for kk in range(KD):
                            last = mm3(bank("c2")[:, TOK + t * DROPE:TOK + (t + 1) * DROPE], hk(kk, t * P, P),
                                       w(u, None, D + kk * DROPE, DROPE), kk == 0, kk == KD - 1)
                    fin(last)
                elif u == 12:
                    unit_in(u)
                    place_free(pe, "kv")
                    for part in range(2):
                        for t in range(T):
                            for kk in range(2):
                                last = mm3(big[:, 2 * part + t, :], bk(3 + kk, t * P, P),
                                           w(u, None, kk * D + part * 512, 512), kk == 0, kk == 1)
                    fin(last)
                elif u == 14:
                    unit_in(u)
                    place_free(pe, "qa")
                    for t in range(T):
                        for kk in range(3):
                            last = mm3(big[:, t, :], bk(kk, t * P, P), w(u, None, kk * 512, 512), kk == 0, kk == 2)
                    fin(last)
                elif u == 13:
                    unit_in(u)
                    place_free(pe, "qb")
                    for t in range(T):
                        for kk in range(3):
                            last = mm3(bank("qb")[:, t * TOK:(t + 1) * TOK], bk(kk, t * P, P),
                                       w(u, None, kk * TOK, TOK), kk == 0, kk == 2)
                    fin(last)
                elif names[0][0] == "b":
                    if u == 29:
                        pe.wait_ge(S("s_lo"), 1)
                    if u == 18:
                        pe.wait_ge(S("xo_lo"), 1)
                    if u == 31:
                        place_read(pe, "pv1")
                    branch(u, None, names, bk_from({"c": 4, "s": 4, "m": 0}[names[0][1]]), 4)
                elif u == 26:
                    pe.wait_ge(S("y_lo"), 4)
                    branch(u, None, names, bk, 4)
                elif u == 33:
                    w_out(u, None)
                elif u < 33:
                    fm_unit(u, None, names[0])
                if u == 0:
                    pe.wait_ge(S("h_lo"), KD)
                    norm_T(1, True)
                if u == 3:
                    x_kT()
                if u == 5:
                    s5_b()
                if u == 6:
                    x_scores()
                if u == 9:
                    x_probs()
                if u == 10:
                    x_out()
                if u == 11:
                    c_sums()
                if u in (24, 26):
                    m_turn((u - 24) // 2)
                if u in (25, 27):
                    m_scores((u - 25) // 2)
                if u == 28:
                    m_probs(0)
                if u == 29:
                    m_out(0)
                    m_probs(1)
                if u == 30:
                    m_out(1)
                if 7 <= u < 7 + ST:
                    s5_in(u - 7)
                if 9 <= u < 9 + ST:
                    s5_out(u - 9)
            norm_T(2)
            ffn(U_MIX1, None, "f0", 2)

            pe.wait_ge(S("c2_in"), 16)
            decay = col2("decay").rearrange("p (h c) -> p h c", h=RH)
            pool_m = col2("pool").rearrange("p (g c) -> p g c", g=4)
            with pe.Fori(0, LAYERS) as l:
                norm_T(l * 3 + 3)
                ffn(0, l, "f1", l * 3 + 3)
                norm_T(l * 3 + 4)

                def head(h):
                    return slice(64 * (h % 2), 64 * (h % 2) + 64), (h // 2) * TOK

                def two_tiles(out, s, m):
                    pe.matmul(out[:, 0:TOK], s[:, 0:P], m[:, 0:TOK], start=True, stop=True)
                    return pe.matmul(out[:, TOK:3 * P], s[:, P:TOK], m[:, P:TOK], start=True, stop=True)

                def sb_scores():
                    place_read(pe, "sbq", l)
                    place_read(pe, "sbk", l)
                    place_free(pe, "z", l)
                    for h in range(SBH):
                        p, c = head(h)
                        last = two_tiles(big[:, h, :], sbk[p, c:c + TOK], sbq[p, c:c + TOK])
                    fin(last)

                def rotate(name, src, needs):
                    place_read(pe, needs, l)
                    place_free(pe, name, l)
                    fin(pe.matmul(pb["p3"][:, :], col2("rot"), src, start=True, stop=True))

                def sb_after():
                    pe.wait_ge(S("lf_ready"), l + 1)
                    place_free(pe, "sa", l)
                    for h in range(SBH):
                        pe.matmul(big[:, h, 0:TOK], col2("after"), C_z[:, h, 0:TOK], start=True, stop=False)
                        pe.matmul(big[:, h, P:TOK], ones, C_z[:, h, TOK:3 * P], start=False, stop=True)
                        last = pe.matmul(big[:, h, TOK:3 * P], col2("after"), C_z[:, h, TOK:3 * P], start=True,
                                         stop=True)
                    fin(last)

                def sb_out():
                    pe.wait_ge(S("w_ready"), l + 1)
                    place_read(pe, "sbv", l)
                    place_free(pe, "pv", l)
                    for h in range(SBH):
                        p, c = head(h)
                        last = pv_product(pb["p3"][p, c:c + TOK], sbv[:, h * 64:h * 64 + 64],
                                          sbv[:, TOK + h * 64:TOK + h * 64 + 64], B_z[:, h, :])
                    fin(last)

                def ret_scores():
                    pe.wait_ge(S("rq_rot"), l + 1)
                    pe.wait_ge(S("rk_rot"), l + 1)
                    place_free(pe, "rs", l)
                    for h in range(RH):
                        p, c = head(h)
                        last = two_tiles(big[:, h, :], rk[p, c:c + TOK], rq[p, c:c + TOK])
                    fin(last)

                def pool_means():
                    place_read(pe, "up", l)
                    place_free(pe, "pl1", l)
                    for g in range(4):
                        p, c = head(g)
                        last = pv_product(pb["p3"][p, c:c + TOK], up[:, g * 64:g * 64 + 64],
                                          up[:, TOK + g * 64:TOK + g * 64 + 64], pool_m[:, g, :])
                    fin(last)

                def pool_mix():
                    place_read(pe, "pl1", l)
                    for c in range(2):
                        last = pe.matmul(pb["p3"][:, c * TOK:(c + 1) * TOK], lcol("w_pool", c * P, P),
                                         rt[:, c * TOK:(c + 1) * TOK], start=True, stop=True)
                    fin(last)

                def ret_out():
                    place_read(pe, "rs", l)
                    place_read(pe, "rv0", l)
                    place_read(pe, "rv1", l)
                    for h in range(RH):
                        o = slice(h * P, (h + 1) * P)
                        pe.matmul(big[:, 0, o], D_z[:, h, 0:P], rv[:, 0, o], start=True, stop=True)
                        pe.matmul(big[:, 1, o], D_z[:, h, P:TOK], rv[:, 0, o], start=True, stop=False)
                        last = pe.matmul(big[:, 1, o], D_z[:, h, TOK:3 * P], rv[:, 1, o], start=False, stop=True)
                    fin(last)

                def ret_turn():
                    pe.wait_ge(S("yn_ready"), l + 1)
                    place_free(pe, "rt", l)
                    for h in range(RH):
                        for t in range(T):
                            last = pe.transpose(big[:, h // 2, (h % 2) * TOK + t * P:(h % 2) * TOK + (t + 1) * P],
                                                y_n[:, t * 512 + h * P:t * 512 + (h + 1) * P], ident)
                    fin(last)

                for u in range(U_MIX2):
                    k, names = U_FFN + u, UNITS2[u]
                    if u in (5, 6):
                        tm_half(k, l, "rv", u - 5)
                    elif u in (8, 9):
                        tm_half(k, l, "rg", u - 8)
                    elif u in (2, 7):
                        tm_unit(k, l, names[0])
                    elif names[0][0] == "b":
                        if u in (14, 19, 24):
                            place_read(pe, {14: "pv", 19: "pl2", 24: "rt"}[u], l)
                        branch(k, l, names, bk_from({"a": 0, "p": 2, "r": 4}[names[0][1]]), 4 if u >= 24 else 2)
                    elif u == 26:
                        w_out(k, l)
                    elif u < 26:
                        fm_unit(k, l, names[0], n=l * 3 + 4 if u == 0 else None)
                    if u == 3:
                        sb_scores()
                    if u == 5:
                        rotate("pq", rq, "rq")
                    if u == 6:
                        rotate("pk", rk, "rk")
                    if u == 8:
                        pool_means()
                    if u == 9:
                        pool_mix()
                        sb_after()
                    if u == 11:
                        ret_scores()
                    if u == 12:
                        sb_out()
                    if u == 13:
                        ret_out()
                    if u == 19:
                        ret_turn()
                norm_T(l * 3 + 5)
                ffn(U_FFN + U_MIX2, l, "f2", l * 3 + 5)

        @block.scalar
        def _(act):
            step = Steps(act, S("act_step"))
            act.dma_start(xs, mem_d.rearrange("t p d -> p t d")).then_inc(S("mem_in"), 16)

            def copy(dst, src, scale=1.0):
                return act.activation(dst, src, ACT.Copy, scale=scale)

            def norm_rows(n, src, t1, t0, scaled=True):
                act.wait_ge(S(t1[0]), t1[1])
                act.activation(junk_act, src[:, 1, :], ACT.Square, scale=D ** -0.5, accum_out=ss[:, 0:1])\
                   .then_inc(S("sq_t1"), 1)
                if scaled:
                    act.wait_ge(S("rstd1"), n + 1)
                    copy(xs[:, 1, 0:512], src[:, 1, 0:512], rstd[:, 1:2]).then_inc(S("xs_t1a"), 1)
                act.wait_ge(S(t0[0]), t0[1])
                act.activation(junk_act2, src[:, 0, 0:512], ACT.Square, scale=D ** -0.5, accum_out=ss[:, 1:2])\
                   .then_inc(S("sq_t0"), 1)

            def norm_split(n, tag, dst, gain, l=None, first=False):
                for k in range(KD):
                    if k % 2 == 0:
                        job_done(act, f"{tag}T{k // 2}", l)
                    copy(dst[:, k, :], norm_bank(first, k // 2)[:, (k % 2) * TOK:(k % 2 + 1) * TOK], gain(k))\
                        .then_inc(S("h_hi"), 1)

            def evac(name, dst, l=None, scale=1.0, src=None):
                job_done(act, name, l)
                copy(dst, bank(name, l)[:, :] if src is None else src, scale).then_inc(read_sem(name, l), 1)

            def gate(name, first, l=None, bias=None):
                job_done(act, name, l)
                b = bank(name, l)
                if bias is None:
                    act.activation(gates[:, first:first + 2, :], b[:, :].rearrange("p (a t) -> p a t", a=2), ACT.Tanh,
                                   scale=0.5).then_inc(read_sem(name, l), 1)
                    return
                act.activation(gates[:, first, :], b[:, 0:TOK], ACT.Tanh, scale=0.5, bias=hb[:, bias:bias + 1])
                act.activation(gates[:, first + 1, :], b[:, TOK:], ACT.Tanh, scale=0.5, bias=hb[:, bias + 1:bias + 2])\
                   .then_inc(read_sem(name, l), 1)

            def merged_high(j, l=None):
                act.wait_ge(S("merged"), (j + 1) if l is None else l * 4 + (4 + j + 1))
                copy(h_hi[:, 2 * j:2 * j + 2, :], merged[:, 2 * j:2 * j + 2, :]).then_inc(S("m_hi"), 1)

            def ffn_evac(par, done, used):
                act.wait_ge(S("pe_done"), done)
                b = pb[("p0", "p1")[par]]
                wait(act, ("p0", "p1")[par] + "_read", used)
                act.activation(f_s[:, par, :], b[:, 0:TOK], ACT.Silu).then_inc(S("silu"), 1)

            def conv_evac(par, f, done, used):
                act.wait_ge(S("pe_done"), done)
                wait(act, ("p0", "p1")[par] + "_read", used)
                for half in range(2):
                    a = C1["conv_w"][0] + 3 * (half * NF) + 2
                    bb = C1["conv_b"][0] + half * NF
                    ins = act.activation(f_c4[:, par, half, :], pb[("p0", "p1")[par]][:, half * TOK:(half + 1) * TOK],
                                         ACT.Identity, scale=c1[:, bass.ds(f * 3 + a, 1)],
                                         bias=c1[:, bass.ds(f + bb, 1)])
                ins.then_inc(S("conv0"), 1)

            def conv_silu(par, n):
                act.wait_ge(S("conv"), n)
                act.activation(f_s[:, par, :], f_c4[:, par, 0, :], ACT.Silu).then_inc(S("silu"), 1)

            f_c4 = area(GT + 1024, 1024).rearrange("p (a b t) -> p a b t", a=2, b=2)

            def ffn(k0, l, tag, conv=False):
                ua, ub = plan.use(tag + "A0", l), plan.use(tag + "B0", l)

                def up(k, i, par, m=None, i_more=0):
                    done = plan.unit_done(k, l)
                    used = (ua if par == 0 else ub) + i
                    f = 2 * i + par
                    if m is not None:
                        done, used, f = m * 6 + done, m * 2 + used, m * 4 + f
                    if conv:
                        conv_evac(par, f, done, used)
                        split_act(act, k, l, m)
                        conv_silu(par, f + 1)
                    else:
                        ffn_evac(par, done, used)
                        split_act(act, k, l, m)

                def down(k, m=None):
                    split_act(act, k, l, m)

                up(k0, 0, 0)
                up(k0 + 1, 0, 1)
                up(k0 + 2, 1, 0)
                up(k0 + 3, 1, 1)
                down(k0 + 4)
                up(k0 + 5, 2, 0)
                up(k0 + 6, 2, 1)
                down(k0 + 7)
                with act.Fori(0, (NI - 5) // 2) as m:
                    for h in range(2):
                        up(k0 + 8 + 3 * h, 3 + h, 0, m)
                        up(k0 + 9 + 3 * h, 3 + h, 1, m)
                        down(k0 + 10 + 3 * h, m)
                k1 = k0 + U_FFN - 7
                for h in range(2):
                    up(k1 + 3 * h, NI - 2 + h, 0)
                    up(k1 + 1 + 3 * h, NI - 2 + h, 1)
                    if h == 0:
                        down(k1 + 2)

            act.wait_ge(S("c1_in"), 16)
            act.activation(dt_, col("log_dt", 0, ST), ACT.Exp).then_inc(S("dt"), 1)
            act.wait_ge(S("s5_a"), 1)
            act.activation(mag, tA, ACT.Exp).then_inc(S("mag"), 1)
            def first_split(r):
                act.wait_ge(S(f"raw_in{r}"), 16)
                copy(whi[:, r, :], raw[:, r, :]).then_inc(S("hi_done"), 1)

            norm_rows(0, xs, ("mem_in", 16), ("mem_in", 16))
            first_split(0)
            norm_split(0, "mem", b_hi, lambda k: col("g_mem", k), first=True)
            first_split(1)
            job_done(act, "memT3")
            norm_rows(1, x, ("x_in", 16), ("x_in", 16))
            act.wait_ge(S("reduced"), 1)
            act.activation(sin48, tri_r, ACT.Sin).then_inc(S("trig"), 1)
            act.activation(cos48, tri_w, ACT.Sin).then_inc(S("trig"), 1)
            first_split(2)
            norm_split(1, "x", h_hi, lambda k: col("g_mix", k), first=True)

            def mla_out_high(g):
                job_done(act, f"pv{g}")
                copy(b_hi[:, 2 * g:2 * g + 2, :].rearrange("p a t -> p (a t)"), pb["p3"][:, :]).then_inc(S("pv_hi"), 1)

            for u in range(U_MIX1):
                name = UNITS1[u][0]
                if u in (8, 9, 10):
                    job_done(act, name)
                    for c in range(2 if u < 10 else 1):
                        kk = 2 * (u - 8) + c
                        src = bank(name)[:, c * TOK:(c + 1) * TOK]
                        step(act.activation(c_sq[:, kk, :], src, ACT.Square))
                        g = col("g_qa", kk) if kk < 3 else col("g_kva", kk - 3)
                        copy(b_hi[:, kk, :], src, g).then_inc(S("c_hi"), 1)
                    if u == 10:
                        copy(kr, bank(name)[:, TOK:TOK + 2 * DROPE]).then_inc(S("kr"), 1)
                if u == 8:
                    act.wait_ge(S("x_rec"), 1)
                    for a in range(8):
                        ins = copy(p_x[:, a, :], p_x[:, a, :], xrec[:, a:a + 1])
                    ins.then_inc(S("xp_ready"), 1)
                if name[:2] == "gc":
                    gate(name, 2 * int(name[2]), bias=2 * KD + 2 * int(name[2]))
                if name[:2] == "gs":
                    if u == 22:
                        act.wait_ge(S("roped"), 1)
                    gate(name, 8 + 2 * (u - 20), bias=KD + 2 * (u - 20))
                if name[:2] == "gm":
                    if u == 24:
                        place_read(act, "bc3")
                    gate(name, 2 * int(name[2]), bias=2 * int(name[2]))
                if u == 26:
                    for j in range(2):
                        job_done(act, f"gl{j}")
                        for c in range(2):
                            m = 2 * j + c
                            ins = act.activation(sg_s[:, m, :], bank(f"gl{j}")[:, c * TOK:(c + 1) * TOK], ACT.Tanh,
                                                 scale=0.5, bias=hb[:, 3 * KD + m:3 * KD + m + 1])
                        ins.then_inc(read_sem(f"gl{j}"), 1)
                if u == 30:
                    mla_out_high(u - 29)
                if u < U_MIX1 - 2:
                    split_act(act, u)
                if u == 1:
                    for t in range(T):
                        evac(f"mk{t}", k_x[:, t, :])
                    for t in range(T):
                        place_read(act, f"mk{t}")
                        ins = act.activation(sq_x[:, 2 * t:2 * t + 2, :].rearrange("p a t -> p (a t)"),
                                             k_x[:, t, :], ACT.Square)
                    ins.then_inc(S("kx_sq"), 1)
                if u == 3:
                    evac("mv0", v_x[:, 0, :])
                    evac("mv1", v_x[:, 1, :])
                if u == 4:
                    job_done(act, "kT")
                    act.wait_ge(S("gxx"), 1)
                    kt2 = kt_x.rearrange("p (a h) t -> p a (h t)", a=2)
                    copy(kt2[:, 0, :], big[:, 0, :], gxx[:, 0:1])
                    copy(kt2[:, 1, :], big[:, 1, :], gxx[:, 0:1]).then_inc(read_sem("kT"), 1)
                if u in (4, 5):
                    h = 2 * (u - 4)
                    job_done(act, name)
                    b2 = bank(name)[:, :].rearrange("p (a t) -> p a t", a=2)
                    copy(q_x[:, h:h + 2, :], b2)
                    act.activation(sq_x[:, h:h + 2, :], b2, ACT.Square).then_inc(read_sem(name), 1)
                if u in (6, 7):
                    evac(name, u_fm[:, 2 * (u - 6):2 * (u - 6) + 2, :].rearrange("p a t -> p (a t)"))
                if u == 7:
                    job_done(act, "xs")
                    act.wait_ge(S("x_neg"), 1)
                    act.wait_ge(S("E_ready"), 1)
                    for a in range(8):
                        ins = act.activation(p_x[:, a, :], bigf[:, a * TOK:(a + 1) * TOK], ACT.Exp,
                                             scale=xscl[:, a:a + 1], bias=xneg[:, a:a + 1],
                                             accum_out=xsum[:, a:a + 1])
                    ins.then_inc(read_sem("xs"), 1)
                if u == 10:
                    job_done(act, "xo")
                    copy(x_y, bigf[:, 0:1024]).then_inc(read_sem("xo"), 1)
                if u == 9:
                    job_done(act, "xp")
                    copy(pT_x, bigf).then_inc(read_sem("xp"), 1)
                if u == 12:
                    act.wait_ge(S("c_rstd"), 1)
                    job_done(act, "kv")
                    for t in range(T):
                        step(copy(K_m[:, t * H_MLA:(t + 1) * H_MLA, 0:DNOPE],
                                  big[:, t, :].rearrange("p (h d) -> p h d", h=H_MLA), rc[:, 2 + t:3 + t]))
                    step(copy(V_m[:, 0, :], big[:, 2, :], rc[:, 2:3]))
                    copy(V_m[:, 1, :], big[:, 3, :], rc[:, 3:4]).then_inc(read_sem("kv"), 1)
                if u == 13:
                    job_done(act, "qb")
                    step(copy(Q_m[:, 512:768], bank("qb")[:, 0:TOK], rc[:, 0:1]))
                    copy(Q_m[:, 768 + 512:1536], bank("qb")[:, TOK:], rc[:, 1:2]).then_inc(read_sem("qb"), 1)
                if u == 14:
                    job_done(act, "qa")
                    step(copy(Q_m[:, 0:512], big[:, 0, :], rc[:, 0:1]))
                    copy(Q_m[:, 768:1280], big[:, 1, :], rc[:, 1:2]).then_inc(read_sem("qa"), 1)
                    place_read(act, "qa")
                    place_read(act, "qb")
                    act.activation(m_sq, Q_m, ACT.Square).then_inc(S("q_sq"), 1)
                if u == 15:
                    act.wait_ge(S("mq_msq"), 1)
                    act.activation(m_sq[:, 0:1024].rearrange("p (a d) -> p a d", a=16), K_m[:, :, 0:DNOPE],
                                   ACT.Square).then_inc(S("k_sq"), 1)
                if u == 15:
                    copy(b_hi[:, 4:8, :].rearrange("p a t -> p (a t)"), x_y).then_inc(S("xo_hi"), 1)
                if u in Y_SLOTS:
                    b = Y_SLOTS.index(u)
                    place_read(act, f"cy{4 * b + 3}")
                    act.activation(y_s[:, b, :], y_s[:, b, :], ACT.Gelu_apprx_tanh).then_inc(S("y_gelu"), 1)
                    act.wait_ge(S("y_gelu"), b + 1)
                    copy(b_hi[:, b, :], y_s[:, b, :]).then_inc(S("y_hi"), 1)
                if u in (24, 26):
                    job_done(act, f"tq{(u - 24) // 2}")
                    job_done(act, "cy15")
                    copy(QT[0:DQK, :], bigf[0:DQK, 0:1024]).then_inc(S("mq_T"), 1)
                if u == 26:
                    act.wait_ge(S("glu"), 1)
                    copy(b_hi[:, 4:8, :], sg_s, 0.5).then_inc(S("s_hi"), 1)
                if u in (26, 28):
                    g = (u - 26) // 2
                    act.wait_ge(S("m_neg"), g + 1)
                    for t in range(T):
                        for h in range(4):
                            seg = P_m[g][:, h, 0:P] if t == 0 else P_m[g][:, h, P:3 * P]
                            a = t * 4 + h
                            s = t * H_MLA + 4 * g + h
                            ins = act.activation(seg, seg, ACT.Exp, scale=qsc[:, s:s + 1], bias=qng[:, a:a + 1],
                                                 accum_out=qsm[:, a:a + 1])
                    ins.then_inc(S("m_exp"), 1)
                if u in (28, 29):
                    job_done(act, f"pt{u - 28}")
                    copy(PT[:, 0:2, :], big[:, 0:2, 0:3 * P]).then_inc(S("mp_T"), 1)
                if u == 29:
                    mla_out_high(u - 29)
                if u in (31, 32):
                    merged_high(2 * (u - 31))
                    merged_high(2 * (u - 31) + 1)

            def norm(n, tag, gain, l=None):
                norm_rows(n, x, ("x_t1", n - 1), ("x_t0", n - 1))
                norm_split(n, tag, h_hi, gain, l)

            norm(2, "f0", lambda k: col("g_ffn", k))
            split_act(act, U_MIX1 - 2)
            split_act(act, U_MIX1 - 1)
            ffn(U_MIX1, None, "f0", conv=True)
            with act.Fori(0, LAYERS) as l:
                step.enter(l, 2)

                def layer_gain(name):
                    return lambda k: lcol(name, k)

                act.wait_ge(S("lc_in"), l * 16 + 16)
                norm(l * 3 + 3, "f1", layer_gain("g_ffn1"), l)
                for r, loads, _ in last_splits(act, l):
                    act.wait_ge(S(f"raw_in{r}"), loads * 16)
                    copy(whi[:, r, :], raw[:, r, :]).then_inc(S("hi_done"), 1)
                ffn(0, l, "f1")
                norm(l * 3 + 4, "m", layer_gain("g_mix"), l)
                split_act(act, U_FFN - 2, l)
                split_act(act, U_FFN - 1, l)
                for u in range(U_MIX2):
                    k, name = U_FFN + u, UNITS2[u][0]
                    if name[0] == "g":
                        if u == 20:
                            place_read(act, "ba3", l)
                        gate(name, {"a": 0, "p": 8, "r": 0}[name[1]] + 2 * int(name[2]), l)
                    if u < U_MIX2 - 2:
                        split_act(act, k, l)
                    if u == 0:
                        evac(name, sbq, l, scale=64.0 ** -0.5)
                    if u in (1, 2, 3, 4):
                        evac(name, {1: sbk, 2: sbv, 3: rq, 4: rk}[u], l)
                    if u == 4:
                        job_done(act, "z", l)
                        step(act.activation(A_z, big[:, :, 0:3 * P], ACT.Abs))
                    if u == 5:
                        step(act.activation(A_z, A_z, ACT.Exp, scale=-1.0))
                    if u == 6:
                        evac("rv0", rv[:, 0, :], l)
                        evac("rv1", rv[:, 1, :], l)
                        act.activation(A_z, A_z, ACT.Ln, bias=1.0).then_inc(S("ln"), 1)
                    if u == 7:
                        evac("up", up, l)
                    if u == 8:
                        act.wait_ge(S("rk_rot"), l + 1)
                        evac("pl1", rt, l, src=pb["p3"][:, :])
                    if u == 9:
                        job_done(act, "pl2", l)
                        for c in range(2):
                            ins = copy(b_hi[:, 2 + c, :], pb["p3"][:, c * TOK:(c + 1) * TOK], lcol("pool_scale", c))
                        ins.then_inc(S("pl_hi"), 1)
                        for t in range(T):
                            job_done(act, f"rg{t}", l)
                            act.activation(rg[:, t * 512:(t + 1) * 512], bank(f"rg{t}", l)[:, :], ACT.Silu)\
                               .then_inc(read_sem(f"rg{t}", l), 1)
                    if u == 10:
                        place_read(act, "sa", l)
                        act.activation(B_z, B_z, ACT.Exp).then_inc(S("w_exp"), 1)
                    if u == 12:
                        job_done(act, "pv", l)
                        copy(b_hi[:, 0:2, :].rearrange("p a t -> p (a t)"), pb["p3"][:, :]).then_inc(S("pv_hi"), 1)
                    if u == 14:
                        job_done(act, "ry", l)
                        act.activation(y_sq, bigf[:, 0:1024], ACT.Square).then_inc(S("y_sq"), 1)
                    if u == 20:
                        job_done(act, "rt", l)
                        copy(b_hi[:, 4:8, :].rearrange("p a t -> p (a t)"), bigf[:, 0:1024]).then_inc(S("rt_hi"), 1)
                    if u in (24, 25):
                        merged_high(2 * (u - 24), l)
                        merged_high(2 * (u - 24) + 1, l)
                norm(l * 3 + 5, "f2", layer_gain("g_ffn2"), l)
                split_act(act, U_FFN + U_MIX2 - 2, l)
                split_act(act, U_FFN + U_MIX2 - 1, l)
                ffn(U_FFN + U_MIX2, l, "f2")
                step.leave(LAYERS)
            norm_rows(3 + 3 * LAYERS, x, ("x_t1", 2 + 3 * LAYERS), ("x_t0", 2 + 3 * LAYERS), False)

        @block.vector
        def _(dve):
            step = Steps(dve, S("dve_step"))
            f_c4 = area(GT + 1024, 1024).rearrange("p (a b t) -> p a b t", a=2, b=2)

            def tt(out, a, b, op):
                return dve.tensor_tensor(out, a, b, op)

            def ts(out, a, s1, op0, s2=None, op1=None):
                if op1 is None:
                    return dve.tensor_scalar(out, a, s1, None, op0)
                return dve.tensor_scalar(out, a, s1, s2, op0, op1)

            def stt(out, a, s, b, op0, op1):
                return dve.scalar_tensor_tensor(out=out, in0=a, scalar=s, in1=b, op0=op0, op1=op1)

            def low(dst, src, high):
                return tt(dst, src, high.bitcast(F32), ALU.subtract)

            def mean_t1(n):
                dve.wait_ge(S("sq_t1"), n + 1)
                ts(msq[:, 1:2], ss[:, 0:1], EPS, ALU.add).then_inc(S("msq1"), 1)

            def mean_t0(n, src):
                step(dve.tensor_tensor_reduce(out=junk_dve, in0=src[:, 0, 512:], in1=src[:, 0, 512:], scale=1.0 / D,
                                              scalar=0.0, op0=ALU.mult, op1=ALU.add, accum_out=ss[:, 2:3]))
                dve.wait_ge(S("sq_t0"), n + 1)
                stt(msq[:, 0:1], ss[:, 1:2], EPS, ss[:, 2:3], ALU.add, ALU.add).then_inc(S("msq0"), 1)

            def norm_scale(n, src):
                dve.wait_ge(S("rstd1"), n + 1)
                ts(xs[:, 1, 512:], src[:, 1, 512:], rstd[:, 1:2], ALU.mult).then_inc(S("xs_t1b"), 1)
                dve.wait_ge(S("rstd0"), n + 1)
                ts(xs[:, 0, 0:512], src[:, 0, 0:512], rstd[:, 0:1], ALU.mult).then_inc(S("xs_t0a"), 1)
                ts(xs[:, 0, 512:], src[:, 0, 512:], rstd[:, 0:1], ALU.mult).then_inc(S("xs_t0b"), 1)

            def norm_split(n, dst, high, gain, first=False):
                for k in range(KD):
                    dve.wait_ge(S("h_hi"), n * KD + (k // 2 * 2 + 2))
                    stt(dst[:, k, :], norm_bank(first, k // 2)[:, (k % 2) * TOK:(k % 2 + 1) * TOK], gain(k),
                        high[:, k, :].bitcast(F32), ALU.mult, ALU.subtract).then_inc(S("h_lo"), 1)

            def norm(n, gain):
                norm_scale(n, x)
                norm_split(n, h_lo, h_hi, gain)

            def add_x(n, name, scale, l=None):
                def add(t, nh):
                    xx = x[:, t, nh * 512:(nh + 1) * 512]
                    return stt(xx, big[:, 2 * t + nh, :], scale, xx, ALU.mult, ALU.add)

                job_done(dve, name + "t1", l)
                add(1, 0)
                add(1, 1).then_inc(S("x_t1"), 1)
                mean_t1(n)
                job_done(dve, name, l)
                add(0, 0).then_inc(S("x_t0"), 1)
                add(0, 1).then_inc(read_sem(name, l), 1)
                place_read(dve, name, l)
                mean_t0(n, x)

            def gated(name, first, j, tmp, start, last, l=None):
                job_done(dve, name, l)
                g = gates[:, first + 2 * j:first + 2 * j + 2, :].rearrange("p a t -> p (a t)")
                acc = merged[:, 2 * j:2 * j + 2, :].rearrange("p a t -> p (a t)")
                dst = acc if start else tmp
                stt(dst, g, 1.0, bank(name, l)[:, :], ALU.add, ALU.mult).then_inc(read_sem(name, l), 1)
                place_read(dve, name, l)
                if start:
                    return
                ins = tt(acc, acc, tmp, ALU.add)
                if last:
                    ins.then_inc(S("merged"), 1)
                    dve.wait_ge(S("merged"), (j + 1) if l is None else l * 4 + (4 + j + 1))
                else:
                    step(ins)

            def merged_low(j, l=None):
                dve.wait_ge(S("m_hi"), (j + 1) if l is None else l * 4 + (4 + j + 1))
                low(h_lo[:, 2 * j:2 * j + 2, :], merged[:, 2 * j:2 * j + 2, :], h_hi[:, 2 * j:2 * j + 2, :])\
                    .then_inc(S("m_lo"), 1)

            def ffn(k0, l, tag, scale, conv=False):
                ua, ub = plan.use(tag + "A0", l), plan.use(tag + "B0", l)
                s0 = 0 if l is None else (l * (4 * NI) + (2 * NI if tag == "f1" else 4 * NI))

                def up(k, i, par, m=None):
                    n = 2 * i + par + 1
                    f = 2 * i + par
                    if m is not None:
                        n, f = m * 4 + n, m * 4 + f
                    b = pb[("p0", "p1")[par]]
                    g, tile = f_g[:, par, :], 2 * (i % 2) + par
                    if conv:
                        dve.wait_ge(S("conv0"), n)
                        for tap in (1, 0):
                            for half in (1, 0):
                                back = 2 - tap
                                a = C1["conv_w"][0] + 3 * half * NF + tap
                                y = f_c4[:, par, half, back:]
                                ins = stt(y, b[:, half * TOK:(half + 1) * TOK - back], c1[:, bass.ds(f * 3 + a, 1)], y,
                                          ALU.mult, ALU.add)
                                if half == 0 and tap == 1:
                                    step(ins)
                        ins.then_inc(S("conv"), 1)
                        split_dve(dve, k, l, m)
                        dve.wait_ge(S("conv"), n)
                        dve.wait_ge(S("silu"), s0 + n)
                        step(tt(g, f_s[:, par, :], f_c4[:, par, 1, :], ALU.mult))
                    else:
                        dve.wait_ge(S("silu"), s0 + n)
                        step(stt(g, f_s[:, par, :], scale, b[:, TOK:], ALU.mult, ALU.mult))
                    step(dve.tensor_copy(b_hi[:, tile, :], g))
                    low(b_lo[:, tile, :], g, b_hi[:, tile, :]).then_inc(S(("p0", "p1")[par] + "_read"), 1)
                    if not conv:
                        split_dve(dve, k, l, m)

                def down(k, m=None):
                    split_dve(dve, k, l, m)

                up(k0, 0, 0)
                up(k0 + 1, 0, 1)
                up(k0 + 2, 1, 0)
                up(k0 + 3, 1, 1)
                down(k0 + 4)
                up(k0 + 5, 2, 0)
                up(k0 + 6, 2, 1)
                down(k0 + 7)
                with dve.Fori(0, (NI - 5) // 2) as m:
                    step.enter(m, 4 * 3 if conv else 4 * 2)
                    for h in range(2):
                        up(k0 + 8 + 3 * h, 3 + h, 0, m)
                        up(k0 + 9 + 3 * h, 3 + h, 1, m)
                        down(k0 + 10 + 3 * h, m)
                    step.leave((NI - 5) // 2)
                k1 = k0 + U_FFN - 7
                for h in range(2):
                    up(k1 + 3 * h, NI - 2 + h, 0)
                    up(k1 + 1 + 3 * h, NI - 2 + h, 1)
                    if h == 0:
                        down(k1 + 2)

            dve.wait_ge(S("c1_in"), 16)
            step(ts(hb[:, 0:3 * KD], col("b_gate", 0, 3 * KD), 0.5, ALU.mult))
            step(ts(hb[:, 3 * KD:], col("b_glu", 0, 4), 0.5, ALU.mult))
            step(tt(gqk, col("gq_nope"), col("gk_nope"), ALU.mult))
            tt(gxx, col("g_xq"), col("g_xk"), ALU.mult).then_inc(S("gxx"), 1)
            dve.wait_ge(S("dt"), 1)
            step(tt(theta, col("lam_im", 0, ST), dt_, ALU.mult))
            tt(tA, col("lam_re", 0, ST), dt_, ALU.mult).then_inc(S("s5_a"), 1)
            def s5_factors():
                dve.wait_ge(S("trig"), 2)
                dve.wait_ge(S("mag"), 1)
                lr, li = col("lam_re", 0, ST), col("lam_im", 0, ST)
                step(tt(tA, mag, cos48[:, 0:ST], ALU.mult))
                step(ts(tA, tA, 1.0, ALU.subtract))
                step(tt(tB, mag, sin48[:, 0:ST], ALU.mult))
                step(tt(tC, lr, lr, ALU.mult))
                step(tt(tD, li, li, ALU.mult))
                step(tt(tC, tC, tD, ALU.add))
                step(dve.reciprocal(tC, tC))
                for dst, (a, b), op in ((f_re, (tA, tB), ALU.add), (f_im, (tB, tA), ALU.subtract)):
                    step(tt(dst, a, lr, ALU.mult))
                    step(tt(tD, b, li, ALU.mult))
                    step(tt(dst, dst, tD, op))
                    step(tt(dst, dst, tC, ALU.mult))

            def s5_b_tiles():
                dve.wait_ge(S("bc_in"), 16)
                dve.wait_ge(S("bd_zero"), 1)
                br, bi = bcr[:, 0], bcr[:, 1]
                fr3, fi3 = (f.unsqueeze(2).to_broadcast([P, ST, GCH]) for f in (f_re, f_im))
                for out, (a, b), op in ((0, (fr3, fi3), ALU.subtract), (1, (fi3, fr3), ALU.add)):
                    tt(btmp[:, 0], br, a, ALU.mult)
                    step(tt(btmp[:, 1], bi, b, ALU.mult))
                    for g in range(2):
                        s = slice(64 * g, 64 * g + 64)
                        ins = tt(bbd[s, out, :, GCH * g:GCH * (g + 1)], btmp[s, 0], btmp[s, 1], op)
                        if out == 1 and g == 1:
                            ins.then_inc(S("bbd"), 1)
                            dve.wait_ge(S("bbd"), 1)
                        else:
                            step(ins)

            def s5_c_tiles():
                for g in range(2):
                    s = slice(64 * g, 64 * g + 64)
                    step(dve.tensor_copy(Cl[0][s, :, GCH * g:GCH * (g + 1)], bcr[s, 2]))
                    step(ts(Cl[1][s, :, GCH * g:GCH * (g + 1)], bcr[s, 3], -1.0, ALU.mult))

            def s5_b_in():
                job_done(dve, "bT")
                step(dve.tensor_copy(s5c[:, 0:512], big[:, 0, :]))
                dve.tensor_copy(s5c[:, 512:1024], big[:, 1, :]).then_inc(read_sem("bT"), 1)
                place_read(dve, "bT")

            def first_split(r):
                dve.wait_ge(S("hi_done"), r + 1)
                low(wlo[:, r, :], raw[:, r, :], whi[:, r, :]).then_inc(S("lo_done"), 1)

            dve.wait_ge(S("mem_in"), 16)
            mean_t1(0)
            mean_t0(0, xs)
            norm_scale(0, xs)
            first_split(0)
            norm_split(0, b_lo, b_hi, lambda k: col("g_mem", k), first=True)
            first_split(1)
            dve.wait_ge(S("x_in"), 16)
            mean_t1(1)
            mean_t0(1, x)
            job_done(dve, "memT3")
            norm_scale(1, x)
            dve.wait_ge(S("pos_in"), 16)
            step(dve.tensor_copy(posf, pos[:, :]))
            step(tt(ang[:, ST:].rearrange("p (t f) -> p t f", t=T),
                    col("inv_freq", 0, DROPE // 2).unsqueeze(1).to_broadcast([P, T, DROPE // 2]),
                    posf.unsqueeze(2).to_broadcast([P, T, DROPE // 2]), ALU.mult))
            step(ts(tri_k, ang, 1.0 / TWO_PI, ALU.mult))
            step(ts(tri_k, tri_k, MAGIC, ALU.add))
            step(ts(tri_k, tri_k, MAGIC, ALU.subtract))
            step(stt(tri_r, tri_k, -CW[0], ang, ALU.mult, ALU.add))
            step(stt(tri_r, tri_k, -CW[1], tri_r, ALU.mult, ALU.add))
            step(stt(tri_r, tri_k, -CW[2], tri_r, ALU.mult, ALU.add))
            step(ts(tri_w, tri_r, float(np.float32(np.pi / 2)), ALU.add))
            step(ts(tri_m, tri_w, float(np.float32(np.pi)), ALU.is_gt, -float(np.float32(TWO_PI)), ALU.mult))
            step(tt(tri_w, tri_w, tri_m, ALU.add))
            step(ts(tri_w, tri_w, PI_LOW, ALU.min, -PI_LOW, ALU.max))
            ts(tri_r, tri_r, PI_LOW, ALU.min, -PI_LOW, ALU.max).then_inc(S("reduced"), 1)
            first_split(2)
            norm_split(1, h_lo, h_hi, lambda k: col("g_mix", k), first=True)

            def s5_scan(j):
                job_done(dve, f"bu{j}")
                if j == 0:
                    dve.wait_ge(S("E_ready"), 1)
                src = pb["p3"][:, :].rearrange("p (a t) -> p a t", a=4)
                ec, es = (a[:, j, :].unsqueeze(1).to_broadcast([P, 4, P]) for a in (E_c, E_s))
                tt(s5_m1.rearrange("p (a t) -> p a t", a=4), src, ec, ALU.mult)
                tt(s5_m2.rearrange("p (a t) -> p a t", a=4), src, es, ALU.mult).then_inc(S("p3_read"), 1)
                place_read(dve, f"bu{j}")
                tt(s5_m1[:, 0:TOK], s5_m1[:, 0:TOK], s5_m2[:, TOK:], ALU.add)
                step(tt(s5_m1[:, TOK:], s5_m1[:, TOK:], s5_m2[:, 0:TOK], ALU.subtract))
                if j >= 2:
                    dve.wait_ge(S("s_ready"), j - 1)
                z, d = s5_z[j % 2], mag[:, j:j + 1].to_broadcast([P, P])
                for a in range(2):
                    ins = dve.tensor_tensor_scan(z[:, a * TOK:a * TOK + P], d, s5_m1[:, a * TOK:a * TOK + P], 0.0,
                                                 ALU.mult, ALU.add)
                step(ins)
                zr, zi = z[:, P - 1:P], z[:, TOK + P - 1:TOK + P]
                er, ei, en = pw[0][0][:, j:j + 1], pw[0][1][:, j:j + 1], e128n[:, j:j + 1]
                ts(ini[:, 0:1], zr, er, ALU.mult)
                step(ts(ini[:, 1:2], zi, er, ALU.mult))
                stt(ini[:, 0:1], zi, en, ini[:, 0:1], ALU.mult, ALU.add)
                step(stt(ini[:, 1:2], zr, ei, ini[:, 1:2], ALU.mult, ALU.add))
                dve.tensor_tensor_scan(z[:, P:TOK], d, s5_m1[:, P:TOK], ini[:, 0:1], ALU.mult, ALU.add)
                dve.tensor_tensor_scan(z[:, TOK + P:], d, s5_m1[:, TOK + P:], ini[:, 1:2], ALU.mult, ALU.add)\
                   .then_inc(S("z_ready"), 1)
                dve.wait_ge(S("z_ready"), j + 1)

            heads = "p (t h) d -> p t h d"

            def mla_prepare_q():
                dve.wait_ge(S("q_sq"), 1)
                step(dve.tensor_reduce(mq, m_sq.rearrange("p (a d) -> p a d", a=16), AX.X, ALU.add))
                ts(mq, mq, 1.0 / DQK, ALU.mult, EPS, ALU.add).then_inc(S("mq_msq"), 1)

            def rope(out, src, n, done=None):
                c, s = (a.rearrange("p (t f) -> p t f", t=T).unsqueeze(2).to_broadcast([P, T, n, 16])
                        for a in (rope_c, rope_s))
                x1, x2 = src[:, :, :, 0:16], src[:, :, :, 16:32]
                tmp = [(a[:, 0:T * n * 16]).rearrange("p (t h f) -> p t h f", t=T, h=n) for a in m_t]
                tt(tmp[0], x1, c, ALU.mult)
                tt(tmp[1], x2, s, ALU.mult)
                tt(tmp[2], x1, s, ALU.mult)
                step(tt(tmp[3], x2, c, ALU.mult))
                tt(out[:, :, :, 0:16], tmp[0], tmp[1], ALU.subtract)
                ins = tt(out[:, :, :, 16:32], tmp[2], tmp[3], ALU.add)
                if done:
                    ins.then_inc(S(done), 1)
                    dve.wait_ge(S(done), 1)
                else:
                    step(ins)

            def mla_prepare_k():
                dve.wait_ge(S("k_sq"), 1)
                dve.wait_ge(S("kr"), 1)
                step(dve.tensor_reduce(mk, m_sq[:, 0:1024].rearrange("p (a d) -> p a d", a=16), AX.X, ALU.add))
                step(tt(krg, kr, kr, ALU.mult))
                step(dve.tensor_reduce(mkr, krg.rearrange("p (t d) -> p t d", t=T), AX.X, ALU.add))
                mk2 = mk.rearrange("p (t h) -> p t h", t=T)
                step(tt(mk2, mk2, mkr.unsqueeze(2).to_broadcast([P, T, H_MLA]), ALU.add))
                ts(mk, mk, 1.0 / DQK, ALU.mult, EPS, ALU.add).then_inc(S("mk_msq"), 1)

            def mla_rope():
                gq3 = col("gq_rope", 0, DROPE).unsqueeze(1).to_broadcast([P, 16, DROPE])
                step(tt(Qh[:, :, DNOPE:], Qh[:, :, DNOPE:], gq3, ALU.mult))
                q4 = Qh[:, :, DNOPE:].rearrange(heads, t=T)
                rope(q4, q4, H_MLA)
                gk3 = col("gk_rope", 0, DROPE).unsqueeze(1).to_broadcast([P, T, DROPE])
                step(tt(krg.rearrange("p (t d) -> p t d", t=T), kr.rearrange("p (t d) -> p t d", t=T), gk3, ALU.mult))
                rope(kro.rearrange("p (t h d) -> p t h d", t=T, h=1), krg.rearrange("p (t h d) -> p t h d", t=T, h=1), 1,
                     "roped")

            def mla_scale_k():
                dve.wait_ge(S("mk_rstd"), 1)
                dve.wait_ge(S("mq_rstd"), 1)
                rk3 = rk_.rearrange("p (t h) -> p t h", t=T).unsqueeze(3)
                tt(K_m[:, :, DNOPE:].rearrange(heads, t=T),
                   kro.rearrange("p (t d) -> p t d", t=T).unsqueeze(2).to_broadcast([P, T, H_MLA, DROPE]),
                   rk3.to_broadcast([P, T, H_MLA, DROPE]), ALU.mult)
                tt(K_m[:, :, 0:DNOPE], K_m[:, :, 0:DNOPE], rk_.unsqueeze(2).to_broadcast([P, 16, DNOPE]), ALU.mult)
                ts(qsc, rq_, float(DQK) ** -0.5, ALU.mult).then_inc(S("qk_ready"), 1)
                dve.wait_ge(S("qk_ready"), 1)

            causal4 = causal.unsqueeze(1).to_broadcast([P, 4, 3 * P])

            def mla_mask(g):
                job_done(dve, f"sc{g}")
                tt(P_m[g], big[:, :, 0:3 * P], causal4, ALU.add).then_inc(read_sem(f"sc{g}"), 1)
                place_read(dve, f"sc{g}")
                dve.tensor_reduce(qmx[:, 0:4], P_m[g][:, :, 0:P], AX.X, ALU.max)
                step(dve.tensor_reduce(qmx[:, 4:8], P_m[g][:, :, P:], AX.X, ALU.max))
                v = "p (t h) -> p t h"
                stt(qng.rearrange(v, t=T), qmx.rearrange(v, t=T), -1.0,
                    qsc.rearrange(v, t=T)[:, :, 4 * g:4 * g + 4], ALU.mult, ALU.mult).then_inc(S("m_neg"), 1)

            def mla_weights(g):
                dve.wait_ge(S("m_exp"), g + 1)
                step(dve.reciprocal(qrc, qsm))
                tt(P_m[g][:, :, 0:P], P_m[g][:, :, 0:P], qrc[:, 0:4].unsqueeze(2).to_broadcast([P, 4, P]), ALU.mult)
                tt(P_m[g][:, :, P:], P_m[g][:, :, P:], qrc[:, 4:8].unsqueeze(2).to_broadcast([P, 4, TOK]), ALU.mult)\
                    .then_inc(S("mp_ready"), 1)
                dve.wait_ge(S("mp_ready"), g + 1)

            def mla_out_low(g):
                dve.wait_ge(S("pv_hi"), g + 1)
                low(b_lo[:, 2 * g:2 * g + 2, :].rearrange("p a t -> p (a t)"), pb["p3"][:, :],
                    b_hi[:, 2 * g:2 * g + 2, :].rearrange("p a t -> p (a t)")).then_inc(read_sem(f"pv{g}"), 1)

            def branch_evac(u, i):
                name = UNITS1[u][i]
                kind = name[1]
                gated(name, 8 if kind == "s" else 0, int(name[2]), area(XS, 512), kind == "c", kind == "m")

            for u in range(U_MIX1):
                name = UNITS1[u][0]
                if u == 11:
                    job_done(dve, "cs")
                    ts(msc[:, 0:2], bigf[:, 0:2], 1.0 / Q_LORA, ALU.mult, EPS, ALU.add)
                    ts(msc[:, 2:4], bigf[:, 2:4], 1.0 / KV_LORA, ALU.mult, EPS, ALU.add)\
                        .then_inc(read_sem("cs"), 1)
                if name[0] == "b":
                    branch_evac(u, 1)
                if u == 8:
                    place_read(dve, "xs")
                    dve.reciprocal(xrec, xsum).then_inc(S("x_rec"), 1)
                if u in (12, 16, 20, 24):
                    b = (u - 12) // 4
                    job_done(dve, f"cy{4 * b + 3}")
                    stt(y_s[:, b, :], u_fm[:, b, :], col("ssm_d", b), pb["p2"][:, (b % 2) * TOK:(b % 2 + 1) * TOK],
                        ALU.mult, ALU.add).then_inc(read_sem(f"cy{4 * b + 3}"), 1)
                if 8 <= u < 7 + ST:
                    s5_scan(u - 7)
                if u == 7:
                    dve.wait_ge(S("xq_rstd"), 1)
                    step(ts(xscl, rsq, float(XD) ** -0.5, ALU.mult))
                    stt(xneg, xmax, -1.0, xscl, ALU.mult, ALU.mult).then_inc(S("x_neg"), 1)
                if u in (8, 9, 10):
                    for c in range(2 if u < 10 else 1):
                        kk = 2 * (u - 8) + c
                        dve.wait_ge(S("c_hi"), min(2 * (u - 8) + 2, 5))
                        g = col("g_qa", kk) if kk < 3 else col("g_kva", kk - 3)
                        if u == 10:
                            dve.wait_ge(S("kr"), 1)
                        ins = stt(b_lo[:, kk, :], bank(name)[:, c * TOK:(c + 1) * TOK], g, b_hi[:, kk, :].bitcast(F32),
                                  ALU.mult, ALU.subtract)
                    ins.then_inc(read_sem(name), 1)
                if u == 30:
                    mla_out_low(u - 29)
                if u < U_MIX1 - 2:
                    split_dve(dve, u)
                if u == 7:
                    s5_scan(u - 7)
                if u == 0:
                    s5_factors()
                if u == 2:
                    s5_b_tiles()
                if u == 3:
                    s5_c_tiles()
                if u == 5:
                    s5_b_in()
                if u == 1:
                    dve.wait_ge(S("kx_sq"), 1)
                    step(dve.tensor_reduce(ssk, sq_x.rearrange("p a t -> p (a t)").rearrange("p (a d) -> p a d", a=8),
                                           AX.X, ALU.add))
                    ts(ssk, ssk, 1.0 / XD, ALU.mult, EPS, ALU.add).then_inc(S("kx_msq"), 1)
                    dve.wait_ge(S("kx_rstd"), 1)
                    tt(k_x.rearrange("p t (h d) -> p (t h) d", h=XH), k_x.rearrange("p t (h d) -> p (t h) d", h=XH),
                       rsk.unsqueeze(2).to_broadcast([P, T * XH, XD]), ALU.mult).then_inc(S("kx_ready"), 1)
                if u == 6:
                    job_done(dve, "ssq")
                    ts(msx, pb["p3"][:, 0:8], 1.0 / XD, ALU.mult, EPS, ALU.add).then_inc(read_sem("ssq"), 1)
                    job_done(dve, "xs")
                    step(dve.tensor_reduce(xmax, bigf.rearrange("p (a t) -> p a t", a=8), AX.X, ALU.max))
                if u == 15:
                    dve.wait_ge(S("xo_hi"), 1)
                    low(b_lo[:, 4:8, :].rearrange("p a t -> p (a t)"), x_y,
                        b_hi[:, 4:8, :].rearrange("p a t -> p (a t)")).then_inc(S("xo_lo"), 1)
                if u == 14:
                    mla_prepare_q()
                if u == 17:
                    mla_prepare_k()
                if u == 19:
                    mla_rope()
                if u == 22:
                    mla_scale_k()
                if u in Y_SLOTS:
                    b = Y_SLOTS.index(u)
                    dve.wait_ge(S("y_hi"), b + 1)
                    low(b_lo[:, b, :], y_s[:, b, :], b_hi[:, b, :]).then_inc(S("y_lo"), 1)
                if u == 26:
                    for j in range(2):
                        place_read(dve, f"gl{j}")
                        a = sg_s[:, 2 * j:2 * j + 2, :]
                        ins = stt(a, a, 1.0, y_s[:, 2 * j:2 * j + 2, :], ALU.add, ALU.mult)
                    ins.then_inc(S("glu"), 1)
                    dve.wait_ge(S("s_hi"), 1)
                    stt(b_lo[:, 4:8, :], sg_s, 0.5, b_hi[:, 4:8, :].bitcast(F32), ALU.mult, ALU.subtract)\
                        .then_inc(S("s_lo"), 1)
                if u in (24, 26):
                    g = (u - 24) // 2
                    dve.wait_ge(S("mq_T"), g + 1)
                    ts(KT[0:DQK, :], bigf[0:DQK, 1024:], gqk[0:DQK, :], ALU.mult).then_inc(read_sem(f"tq{g}"), 1)
                if u == 27:
                    mla_weights(0)
                if u in (25, 27):
                    mla_mask((u - 25) // 2)
                if u in (28, 29):
                    dve.wait_ge(S("mp_T"), u - 27)
                    dve.tensor_copy(PT[:, 2:4, :], big[:, 2:4, 0:3 * P]).then_inc(read_sem(f"pt{u - 28}"), 1)
                if u == 28:
                    mla_weights(1)
                if u == 29:
                    mla_out_low(u - 29)
                if u in (31, 32):
                    merged_low(2 * (u - 31))
                    merged_low(2 * (u - 31) + 1)
                if u < U_MIX1 - 1 and UNITS1[u + 1][0][0] == "b":
                    branch_evac(u + 1, 0)
            add_x(2, "wo", 0.5)
            norm(2, lambda k: col("g_ffn", k))
            split_dve(dve, U_MIX1 - 2)
            split_dve(dve, U_MIX1 - 1)
            ffn(U_MIX1, None, "f0", 1.0, conv=True)
            add_x(3, f"f0D{NI - 1}", 1.0)

            decay = col2("decay").rearrange("p (h c) -> p h c", h=RH)
            with dve.Fori(0, LAYERS) as l:
                step.enter(l, DVE_LAYER_STEPS)
                norm(l * 3 + 3, lambda k: lcol("g_ffn1", k))
                for r, _, units in last_splits(dve, l):
                    dve.wait_ge(S("hi_done"), units)
                    low(wlo[:, r, :], raw[:, r, :], whi[:, r, :]).then_inc(S("lo_done"), 1)
                ffn(0, l, "f1", 0.5)
                add_x(l * 3 + 4, f"f1D{NI - 1}", 1.0, l)
                norm(l * 3 + 4, lambda k: lcol("g_mix", k))
                split_dve(dve, U_FFN - 2, l)
                split_dve(dve, U_FFN - 1, l)

                def rotated(name, src, ready):
                    job_done(dve, name, l)
                    c, s = (col2(n).unsqueeze(1).to_broadcast([P, 2, TOK]) for n in ("cos", "sin"))
                    v = "p (a t) -> p a t"
                    tt(rt.rearrange(v, a=2), pb["p3"][:, :].rearrange(v, a=2), s, ALU.mult)\
                        .then_inc(read_sem(name, l), 1)
                    place_read(dve, name, l)
                    step(tt(src.rearrange(v, a=2), src.rearrange(v, a=2), c, ALU.mult))
                    tt(src, src, rt, ALU.add).then_inc(S(ready), 1)
                    dve.wait_ge(S(ready), l + 1)

                def branch_evac(names):
                    for name in names:
                        kind = name[1]
                        gated(name, 8 if kind == "p" else 0, int(name[2]), area(XS + 1536, 512), kind == "a",
                              kind == "r", l)

                for u in range(U_MIX2):
                    k, name = U_FFN + u, UNITS2[u][0]
                    if name[0] == "b":
                        branch_evac(UNITS2[u][-1:])
                    if u < U_MIX2 - 2:
                        split_dve(dve, k, l)
                    if u == 5:
                        rotated("pq", rq, "rq_rot")
                    if u == 6:
                        rotated("pk", rk, "rk_rot")
                    if u == 7:
                        dve.wait_ge(S("ln"), l + 1)
                        z = big[:, :, 0:3 * P]
                        step(stt(B_z, z, 0.0, A_z, ALU.min, ALU.subtract))
                        tt(C_z, B_z, z, ALU.subtract).then_inc(read_sem("z", l), 1)
                    if u == 9:
                        dve.wait_ge(S("pl_hi"), l + 1)
                        for c in range(2):
                            ins = stt(b_lo[:, 2 + c, :], pb["p3"][:, c * TOK:(c + 1) * TOK], lcol("pool_scale", c),
                                      b_hi[:, 2 + c, :].bitcast(F32), ALU.mult, ALU.subtract)
                        ins.then_inc(read_sem("pl2", l), 1)
                        job_done(dve, "sa", l)
                        tt(B_z, B_z, big[:, :, 0:3 * P], ALU.add).then_inc(read_sem("sa", l), 1)
                    if u == 11:
                        job_done(dve, "rs", l)
                        tt(D_z, big[:, :, 0:3 * P], decay, ALU.mult).then_inc(read_sem("rs", l), 1)
                    if u == 12:
                        dve.wait_ge(S("pv_hi"), l + 3)
                        low(b_lo[:, 0:2, :].rearrange("p a t -> p (a t)"), pb["p3"][:, :],
                            b_hi[:, 0:2, :].rearrange("p a t -> p (a t)")).then_inc(read_sem("pv", l), 1)
                    if u == 15:
                        dve.wait_ge(S("y_sq"), l + 1)
                        step(dve.tensor_reduce(rms8, y_sq.rearrange("p (a e) -> p a e", a=8), AX.X, ALU.add))
                        ts(rms8, rms8, 1.0 / P, ALU.mult, EPS, ALU.add).then_inc(S("y_msq"), 1)
                    if u == 17:
                        dve.wait_ge(S("y_rstd"), l + 1)
                        v = "p (a e) -> p a e"
                        tt(y_n.rearrange(v, a=8), bigf[:, 0:1024].rearrange(v, a=8),
                           rr8.unsqueeze(2).to_broadcast([P, 8, P]), ALU.mult).then_inc(read_sem("ry", l), 1)
                    if u == 20:
                        dve.wait_ge(S("rt_hi"), l + 1)
                        low(b_lo[:, 4:8, :].rearrange("p a t -> p (a t)"), bigf[:, 0:1024],
                            b_hi[:, 4:8, :].rearrange("p a t -> p (a t)")).then_inc(read_sem("rt", l), 1)
                    if u in (24, 25):
                        merged_low(2 * (u - 24), l)
                        merged_low(2 * (u - 24) + 1, l)
                    if u < U_MIX2 - 1 and UNITS2[u + 1][0][0] == "b":
                        branch_evac(UNITS2[u + 1][0:-1])
                add_x(l * 3 + 5, "wo", 0.5, l)
                norm(l * 3 + 5, lambda k: lcol("g_ffn2", k))
                split_dve(dve, U_FFN + U_MIX2 - 2, l)
                split_dve(dve, U_FFN + U_MIX2 - 1, l)
                ffn(U_FFN + U_MIX2, l, "f2", 0.5)
                add_x(l * 3 + 6, f"f2D{NI - 1}", 1.0, l)
                step.leave(LAYERS)
            dve.wait_ge(S("gfin_in"), 16)
            for t in (1, 0):
                dve.wait_ge(S(f"rstd{t}"), 4 + 3 * LAYERS)
                stt(xs[:, t, :], x[:, t, :], rstd[:, t:t + 1], area(R, D), ALU.mult, ALU.mult).then_inc(S("out_ready"), 1)


def _units(v):
    def fm(wt, ks, ms):
        return [wt[k * P:(k + 1) * P, m * P:(m + 1) * P] for m in ms for k in ks]

    def tm(wt, ks, n0, n):
        return [wt[k * P:(k + 1) * P, n0:n0 + n] for k in ks]

    out = []

    def unit(parts):
        w = sum(p.shape[1] for p in parts)
        if w < UW:
            parts = parts + [np.zeros((P, UW - w), np.float32)]
        out.append(np.concatenate(parts, axis=1))

    K8 = range(KD)

    def fm_units(wt, c0, n):
        ww = wt[:, c0:c0 + n]
        for m in range(0, n // P, 2):
            unit(fm(ww, K8, (m, m + 1)))

    def tm512(wt, c0):
        for half in range(2):
            unit(tm(wt, range(4 * half, 4 * half + 4), c0, 512))

    def wout(wt):
        for kh in range(2):
            for nh in range(2):
                unit(tm(wt, range(4 * kh, 4 * kh + 4), nh * 512, 512))

    def ffn(w1, w3, w2):
        def up(f):
            unit(fm(w1, K8, (f,)) + fm(w3, K8, (f,)))

        def down(i):
            unit([w2[f * P:(f + 1) * P] for f in (2 * i, 2 * i + 1)])

        up(0)
        up(1)
        for i in range(1, NI):
            up(2 * i)
            up(2 * i + 1)
            down(i - 1)
        down(NI - 1)

    kvw = v["w_mem_kv"][0]
    tm512(kvw, 0)
    tm512(kvw, 512)
    wi = v["w_in"][0]
    o_kv, o_kr, o_u = Q_LORA, Q_LORA + KV_LORA, Q_LORA + KV_LORA + DROPE
    o_x, o_g = o_u + SSM_W, o_u + SSM_W + XH * XD
    fm_units(wi, o_x, XH * XD)
    fm_units(wi, o_u, SSM_W)
    unit(fm(wi, K8, (0, 1)))
    unit(fm(wi, K8, (2, 3)))
    unit(fm(wi, K8, (4,)) + tm(wi, K8, o_kr, DROPE))
    kv = v["w_kv_b"][0].reshape(KV_LORA, H_MLA, DNOPE + DV)
    kv = np.concatenate([kv[:, :, :DNOPE].reshape(KV_LORA, -1), kv[:, :, DNOPE:].reshape(KV_LORA, -1)], axis=1)
    qb = v["w_q_b"][0]
    fm_units(wi, o_g + 2 * D, TOK)
    unit([kv[0:P], kv[P:2 * P]])
    unit(tm(qb, range(3), 512, TOK))
    unit(tm(qb, range(3), 0, 512))
    fm_units(wi, o_g + 2 * D + TOK, D - TOK)

    def gates(wt, c0, g):
        fm_units(wt, c0 + g * D, D)

    def branch(wt, K):
        per = UW // (K * P)
        for m in range(0, KD, per):
            unit(fm(wt, range(K), range(m, m + per)))

    branch(v["w_o_cross"][0], 4)
    gates(wi, o_g, 1)
    fm_units(wi, o_g, D // 2)
    unit(fm(v["w_glu"][0], range(4), range(4)))
    fm_units(wi, o_g + D // 2, D // 2)
    branch(v["w_o_ssm"][0], 4)
    branch(v["w_o_mla"][0], 4)
    wout(v["w_out"][0])
    assert len(out) == U_MIX1
    wu = v["w_up"][0]
    ffn(wu[:, :DFF], wu[:, DFF:], v["w_down"][0])
    for l in range(LAYERS):
        ffn(v["w1_ffn1_2"][l], v["w3_ffn1_2"][l], v["w2_ffn1_2"][l])
        w2 = v["w_in_2"][l]
        o = np.cumsum([0, 256, 256, 256, 256, 256, 512, 512, 256])
        fm_units(w2, o[0], 256)
        fm_units(w2, o[1], 256)
        unit(tm(w2, K8, o[2], 256))
        fm_units(w2, o[3], 256)
        fm_units(w2, o[4], 256)
        tm512(w2, o[5])
        unit(tm(w2, K8, o[7], 256))
        tm512(w2, o[6])
        gates(w2, o[8], 0)
        branch(v["w_branch_sb_2"][l], 2)
        gates(w2, o[8], 2)
        branch(v["w_branch_pool_2"][l], 2)
        gates(w2, o[8], 1)
        branch(v["w_branch_ret_2"][l], 4)
        wout(v["w_out_2"][l])
        ffn(v["w1_ffn2_2"][l], v["w3_ffn2_2"][l], v["w2_ffn2_2"][l])
    assert len(out) == U_USED, len(out)
    while len(out) < U_ALL:
        out.append(np.zeros((P, UW), np.float32))
    return np.stack(out)


def _cols(a):
    return np.ascontiguousarray(a.reshape(-1, P).T)


def _rows(a):
    return np.broadcast_to(a.reshape(1, -1), (P, a.size))


def _state_cols(a):
    return a.reshape(ST, 2 * NST).T


def _tri(fill_true, fill_false, keep):
    q, k = np.arange(P)[:, None], np.arange(P)[None, :]
    return np.where(keep(q, k), fill_true, fill_false).astype(np.float32)


def _consts1(v):
    a = np.zeros((P, NC1), np.float32)

    def put(name, val):
        c, w = C1[name]
        a[:, c:c + w] = val

    put("ident", np.eye(P, dtype=np.float32))
    put("ones", 1.0)
    diag = _tri(0.0, -1e37, lambda q, k: k <= q)
    put("causal", np.concatenate([diag, np.zeros((P, P), np.float32), diag], axis=1))
    for name, src in (("g_mem", "mem_norm_g"), ("g_mix", "norm_mix_g"), ("g_qa", "q_a_norm_g"),
                      ("g_kva", "kv_a_norm_g"), ("g_xq", "xq_norm_g"), ("g_xk", "xk_norm_g"), ("b_glu", "b_glu"),
                      ("g_ffn", "norm_ffn_g"), ("b_gate", "b_gate"), ("conv_b", "conv_b")):
        put(name, _cols(v[src][0]))
    put("ssm_d", _cols(v["ssm_d"][0].reshape(-1)))
    for name, src in (("gq_nope", "q_norm_g"), ("gk_nope", "k_norm_g")):
        c = np.ones((P, 1), np.float32)
        c[:DNOPE, 0] = v[src][0][:DNOPE]
        put(name, c)
    put("gq_rope", _rows(v["q_norm_g"][0][DNOPE:]))
    put("gk_rope", _rows(v["k_norm_g"][0][DNOPE:]))
    freq = np.float32(10000.0) ** (-np.arange(0, DROPE, 2, dtype=np.float32) / np.float32(DROPE))
    put("inv_freq", _rows(freq))
    put("lam_re", _state_cols(v["ssm_lambda_re"][0]))
    put("lam_im", _state_cols(v["ssm_lambda_im"][0]))
    put("log_dt", _state_cols(np.repeat(v["ssm_log_dt"][0][:, None], NST, axis=1)))
    cw = v["conv_w"][0].reshape(3, 2 * NF, P)
    put("conv_w", cw.transpose(2, 1, 0).reshape(P, 6 * NF))
    return a


def _consts2():
    a = np.zeros((P, NC2), np.float32)

    def put(name, val):
        c, w = C2[name]
        a[:, c:c + w] = val

    j = np.arange(TOK)[:, None]
    i = np.arange(TOK)[None, :]

    def two(m):
        return np.concatenate([m[:P], m[P:, P:]], axis=1)

    dec = []
    for h in range(RH):
        lg = np.log(1.0 - 2.0 ** (-5.0 - h))
        dec.append(two(np.where(i >= j, np.exp(np.maximum(i - j, 0) * lg), 0.0) * 64.0 ** -0.5))
    put("decay", np.concatenate(dec, axis=1))
    pl = []
    for win in POOLS:
        cnt = np.minimum(i + 1, win)
        pl.append(two(np.where((j <= i) & (j > i - win), 1.0 / cnt, 0.0) - (i == j)))
    put("pool", np.concatenate(pl, axis=1))
    d = np.arange(P) % 64 % 32
    freq = 10000.0 ** (-d.astype(np.float64) / 32)
    angle = (freq.astype(np.float32)[:, None] * np.arange(TOK, dtype=np.float32)[None, :]).astype(np.float64)
    put("cos", np.cos(angle))
    put("sin", np.sin(angle))
    rot = np.zeros((P, P), np.float32)
    for m in range(P):
        if m % 64 < 32:
            rot[m + 32, m] = -1.0
        else:
            rot[m - 32, m] = 1.0
    put("rot", rot)
    put("after", _tri(1.0, 0.0, lambda q, k: q > k))
    put("strict", two((j < i).astype(np.float64)))
    return a


def _layer_consts(v, l):
    a = np.zeros((P, NLC), np.float32)
    for name, val in (("g_ffn1", _cols(v["g_ffn1_2"][l])), ("g_mix", _cols(v["g_mix_2"][l])),
                      ("g_ffn2", _cols(v["g_ffn2_2"][l])), ("pool_scale", _cols(v["pool_scale_2"][l]))):
        c, w = LC[name]
        a[:, c:c + w] = val
    c, w = LC["w_pool"]
    for g in range(4):
        q, m = 64 * (g % 2), c + P * (g // 2) + 64 * (g % 2)
        a[q:q + 64, m:m + 64] = v["w_pool_2"][l][g]
    return a


def kernel(**inputs):
    import concourse.bacc as bacc
    from concourse.bass_utils import run_bass_kernel_spmd

    v = {k: np.asarray(a) for k, a in inputs.items()}
    b_re, b_im = (v[n][0].reshape(ST, P, GCH).transpose(1, 0, 2) for n in ("ssm_b_re", "ssm_b_im"))
    c_re, c_im = (v[n][0].transpose(0, 2, 1).reshape(ST, P, GCH).transpose(1, 0, 2)
                  for n in ("ssm_c_re", "ssm_c_im"))
    arrays = {
        "weights": _units(v),
        "consts1": _consts1(v),
        "consts2": _consts2(),
        "layer_consts": np.stack([_layer_consts(v, l) for l in range(LAYERS)]),
        "ssm_bc": np.ascontiguousarray(np.stack([b_re, b_im, c_re, c_im], axis=1)),
        "x": np.ascontiguousarray(v["x"].reshape(T, P, D)),
        "mem": np.ascontiguousarray(v["mem"].reshape(T, P, D)),
        "positions": np.ascontiguousarray(v["positions"].reshape(T, P).T),
        "g_final": np.ascontiguousarray(_rows(v["g_final_2"])),
    }
    nc = bacc.Bacc("TRN2", target_bir_lowering=False, num_devices=1)
    args = [nc.dram_tensor(n, a.shape, mybir.dt.from_np(a.dtype), kind="ExternalInput").ap()
            for n, a in arrays.items()]
    out = nc.dram_tensor("out", (T, P, D), F32, kind="ExternalOutput").ap()
    build_program(nc, *args, out)
    r = run_bass_kernel_spmd(nc, [arrays], core_ids=[0])
    return r.results[0]["out"].reshape(1, TOK, D)
```
